# Optimizing a Trainium2 kernel written in Bass

```python
import math
import jax
import jax.numpy as jnp
from jax import lax
import numpy as np
import jax, jax.numpy as jnp

D_MODEL = 1024
BATCH = 1
SEQ = 256
DEPTH = 1

MOBA_HEADS = 8
MOBA_HEAD_DIM = 64
MOBA_BLOCK = 256
MOBA_TOPK = 3
MOBA_Q_CHUNK = 32
GLA_HEADS = 4
GLA_DK = D_MODEL // 2 // GLA_HEADS
GLA_DV = D_MODEL // GLA_HEADS
GLA_GATE_RANK = 16
GLA_GATE_TAU = 16.0
GLA_CHUNK = 64
T5_BUCKETS = 32
T5_MAX_DIST = 128
D_FF = 4 * D_MODEL
EPS = 1e-6

MOBA_WIDTH = MOBA_HEADS * MOBA_HEAD_DIM
GLA_K_WIDTH = GLA_HEADS * GLA_DK
GLA_V_WIDTH = GLA_HEADS * GLA_DV
IN_SPLIT_SIZES = (MOBA_WIDTH, MOBA_WIDTH, MOBA_WIDTH,
                  GLA_K_WIDTH, GLA_K_WIDTH, GLA_V_WIDTH, GLA_GATE_RANK, GLA_V_WIDTH,
                  D_MODEL, D_MODEL)
IN_SPLIT_POINTS = tuple(sum(IN_SPLIT_SIZES[:i + 1]) for i in range(len(IN_SPLIT_SIZES) - 1))
D_IN = sum(IN_SPLIT_SIZES)


def rms_norm(x, gain):
    xf = x.astype(jnp.float32)
    y = xf * lax.rsqrt(jnp.mean(xf * xf, axis=-1, keepdims=True) + EPS) * gain.astype(jnp.float32)
    return y.astype(x.dtype)

def t5_bucket(dist):
    max_exact = T5_BUCKETS // 2
    d = jnp.maximum(dist, 0)
    large = max_exact + (jnp.log(jnp.maximum(d, 1).astype(jnp.float32) / max_exact)
                         / math.log(T5_MAX_DIST / max_exact)
                         * (T5_BUCKETS - max_exact)).astype(jnp.int32)
    large = jnp.minimum(large, T5_BUCKETS - 1)
    return jnp.where(d < max_exact, d, large)

def moba_attention(q, k, v, t5_bias):
    B, S, H, Dh = q.shape
    q = q.transpose(0, 2, 1, 3)
    k = k.transpose(0, 2, 1, 3)
    v = v.transpose(0, 2, 1, 3)
    nb = -(-S // MOBA_BLOCK)
    s_pad = nb * MOBA_BLOCK
    pad = ((0, 0), (0, 0), (0, s_pad - S), (0, 0))
    kb = jnp.pad(k, pad).reshape(B, H, nb, MOBA_BLOCK, Dh)
    vb = jnp.pad(v, pad).reshape(B, H, nb, MOBA_BLOCK, Dh)
    scale = Dh ** -0.5
    q_block = jnp.arange(S) // MOBA_BLOCK
    n_sel = min(MOBA_TOPK, nb - 1)
    if n_sel > 0:
        k_mean = kb.astype(jnp.float32).mean(axis=3)
        gate = jnp.einsum("bhsd,bhnd->bhsn", q.astype(jnp.float32), k_mean)
        fully_past = jnp.arange(nb)[None, :] < q_block[:, None]
        gate = jnp.where(fully_past, gate, -jnp.inf)
        _, sel_idx = lax.top_k(gate, n_sel)
    else:
        sel_idx = jnp.zeros((B, H, S, 0), jnp.int32)
    n_chunks = S // MOBA_Q_CHUNK
    q_c = q.reshape(B, H, n_chunks, MOBA_Q_CHUNK, Dh).transpose(2, 0, 1, 3, 4)
    idx_c = sel_idx.reshape(B, H, n_chunks, MOBA_Q_CHUNK, n_sel).transpose(2, 0, 1, 3, 4)
    bias_hb = t5_bias.T
    b_ix = jnp.arange(B)[:, None, None, None]
    h_ix = jnp.arange(H)[None, :, None, None]
    h_ix5 = jnp.arange(H)[None, :, None, None, None]
    blk = jnp.arange(MOBA_BLOCK)

    def chunk_fn(args):
        ci, qc, ic = args
        c0 = ci * MOBA_Q_CHUNK
        t = c0 + jnp.arange(MOBA_Q_CHUNK)
        ob = c0 // MOBA_BLOCK
        k_own = lax.dynamic_index_in_dim(kb, ob, axis=2, keepdims=False)
        v_own = lax.dynamic_index_in_dim(vb, ob, axis=2, keepdims=False)
        d_own = t[:, None] - (ob * MOBA_BLOCK + blk)[None, :]
        l_own = jnp.einsum("bhqd,bhkd->bhqk", qc, k_own).astype(jnp.float32) * scale
        l_own = l_own + bias_hb[:, t5_bucket(d_own)].astype(jnp.float32)
        l_own = jnp.where(d_own >= 0, l_own, -jnp.inf)
        k_sel = kb[b_ix, h_ix, ic]
        v_sel = vb[b_ix, h_ix, ic]
        l_sel = jnp.einsum("bhqd,bhqjkd->bhqjk", qc, k_sel).astype(jnp.float32) * scale
        d_sel = t[None, None, :, None, None] - (ic[..., None] * MOBA_BLOCK + blk)
        l_sel = l_sel + bias_hb[h_ix5, t5_bucket(d_sel)].astype(jnp.float32)
        l_sel = jnp.where((ic < ob)[..., None], l_sel, -jnp.inf)
        l_sel = l_sel.reshape(B, H, MOBA_Q_CHUNK, n_sel * MOBA_BLOCK)
        p = jax.nn.softmax(jnp.concatenate([l_sel, l_own], axis=-1), axis=-1)
        p_sel = p[..., :n_sel * MOBA_BLOCK].astype(v.dtype)
        p_own = p[..., n_sel * MOBA_BLOCK:].astype(v.dtype)
        o = (jnp.einsum("bhqj,bhqjd->bhqd", p_sel,
                        v_sel.reshape(B, H, MOBA_Q_CHUNK, n_sel * MOBA_BLOCK, Dh))
             + jnp.einsum("bhqk,bhkd->bhqd", p_own, v_own))
        return o.astype(q.dtype)

    out = lax.map(chunk_fn, (jnp.arange(n_chunks, dtype=jnp.int32), q_c, idx_c))
    return out.transpose(1, 0, 3, 2, 4).reshape(B, S, H * Dh)

def gla_attention(q, k, v, log_a):
    B, S, H, dk = q.shape
    C = GLA_CHUNK
    nc = S // C

    def chunks(t):
        return t.astype(jnp.float32).reshape(B, nc, C, H, -1).transpose(1, 0, 3, 2, 4)

    qc = chunks(q) * dk ** -0.5
    kc = chunks(k)
    vc = chunks(v)
    b = jnp.cumsum(chunks(log_a), axis=3)
    b_last = b[..., -1:, :]
    q_dec = qc * jnp.exp(b)
    k_inv = kc * jnp.exp(-b)
    k_dec = kc * jnp.exp(b_last - b)
    causal = jnp.tril(jnp.ones((C, C), dtype=bool))
    attn = jnp.where(causal, jnp.einsum("nbhcd,nbhed->nbhce", q_dec, k_inv), 0.0)
    o_intra = jnp.einsum("nbhce,nbhev->nbhcv", attn, vc)

    def step(state, xs):
        qd, kd, vv, bl = xs
        o_inter = jnp.einsum("bhcd,bhdv->bhcv", qd, state)
        state = jnp.exp(bl)[:, :, 0, :, None] * state + jnp.einsum("bhcd,bhcv->bhdv", kd, vv)
        return state, o_inter

    state0 = jnp.zeros((B, H, dk, v.shape[-1]), jnp.float32)
    _, o_inter = lax.scan(step, state0, (q_dec, k_dec, vc, b_last))
    o = o_intra + o_inter
    return o.transpose(1, 0, 3, 2, 4).reshape(B, S, H, v.shape[-1])

def first_inputs(seed: int = 0) -> dict:
    key = jax.random.key(seed)
    ks = jax.random.split(key, 16)

    def nrm(k, shape, scale):
        return jax.random.normal(k, shape, jnp.float32) * scale

    return {
        "x": nrm(ks[0], (BATCH, SEQ, D_MODEL), 1.0),
        "norm1_g": 1.0 + nrm(ks[1], (DEPTH, D_MODEL), 0.05),
        "w_in": nrm(ks[2], (DEPTH, D_MODEL, D_IN), D_MODEL ** -0.5),
        "moba_q_norm_g": 1.0 + nrm(ks[3], (DEPTH, MOBA_HEAD_DIM), 0.05),
        "moba_k_norm_g": 1.0 + nrm(ks[4], (DEPTH, MOBA_HEAD_DIM), 0.05),
        "t5_bias": nrm(ks[5], (T5_BUCKETS, MOBA_HEADS), 0.5),
        "gla_gate_up": nrm(ks[6], (DEPTH, GLA_GATE_RANK, GLA_K_WIDTH), GLA_GATE_RANK ** -0.5),
        "gla_gate_bias": nrm(ks[7], (DEPTH, GLA_K_WIDTH), 0.1),
        "gla_out_norm_g": 1.0 + nrm(ks[8], (DEPTH, GLA_DV), 0.05),
        "w_branch_moba": nrm(ks[9], (DEPTH, MOBA_WIDTH, D_MODEL), MOBA_WIDTH ** -0.5),
        "w_branch_gla": nrm(ks[10], (DEPTH, GLA_V_WIDTH, D_MODEL), GLA_V_WIDTH ** -0.5),
        "w_out": nrm(ks[11], (DEPTH, D_MODEL, D_MODEL), D_MODEL ** -0.5),
        "norm2_g": 1.0 + nrm(ks[12], (DEPTH, D_MODEL), 0.05),
        "w_up": nrm(ks[13], (DEPTH, D_MODEL, D_FF), D_MODEL ** -0.5),
        "w_down": nrm(ks[14], (DEPTH, D_FF, D_MODEL), D_FF ** -0.5),
    }

def first_block(x, norm1_g, w_in, moba_q_norm_g, moba_k_norm_g, t5_bias, gla_gate_up,
              gla_gate_bias, gla_out_norm_g, w_branch_moba, w_branch_gla, w_out,
              norm2_g, w_up, w_down):
    B, S, _ = x.shape
    h = x
    for layer in range(DEPTH):
        n = rms_norm(h, norm1_g[layer])
        proj = n @ w_in[layer]
        (mq, mk, mv, gq, gk, gv, g_low, g_out, gate_moba, gate_gla) = jnp.split(
            proj, IN_SPLIT_POINTS, axis=-1)
        mq = rms_norm(mq.reshape(B, S, MOBA_HEADS, MOBA_HEAD_DIM), moba_q_norm_g[layer])
        mk = rms_norm(mk.reshape(B, S, MOBA_HEADS, MOBA_HEAD_DIM), moba_k_norm_g[layer])
        mv = mv.reshape(B, S, MOBA_HEADS, MOBA_HEAD_DIM)
        y_moba = moba_attention(mq, mk, mv, t5_bias)
        log_a = jax.nn.log_sigmoid(
            (g_low @ gla_gate_up[layer] + gla_gate_bias[layer]).astype(jnp.float32)) / GLA_GATE_TAU
        y_gla = gla_attention(gq.reshape(B, S, GLA_HEADS, GLA_DK),
                              gk.reshape(B, S, GLA_HEADS, GLA_DK),
                              gv.reshape(B, S, GLA_HEADS, GLA_DV),
                              log_a.reshape(B, S, GLA_HEADS, GLA_DK))
        y_gla = rms_norm(y_gla, gla_out_norm_g[layer]).astype(x.dtype)
        y_gla = (y_gla * jax.nn.silu(g_out.reshape(B, S, GLA_HEADS, GLA_DV))).reshape(B, S, GLA_V_WIDTH)
        mixed = (jax.nn.sigmoid(gate_moba) * (y_moba @ w_branch_moba[layer])
                 + jax.nn.sigmoid(gate_gla) * (y_gla @ w_branch_gla[layer]))
        h = h + mixed @ w_out[layer]
        n2 = rms_norm(h, norm2_g[layer])
        h = h + jnp.square(jax.nn.relu(n2 @ w_up[layer])) @ w_down[layer]
    return h


DEPTH_2 = 2

N_EVEN = (DEPTH_2 + 1) // 2
N_ODD = DEPTH_2 // 2
RMS_EPS = 1e-6
LN_EPS = 1e-5

W_A = D_MODEL
CONV_K = 31
A_GROUPS = 8
H_B = 4
DQK_B = D_MODEL // (2 * H_B)
DV_B = D_MODEL // H_B
W_B = H_B * DV_B
CHUNK = 64
H_C = 8
QK_NOPE = 128
QK_ROPE = 64
V_HEAD = 128
Q_LORA = 3 * D_MODEL // 8
KV_LORA = D_MODEL // 4
W_C = H_C * V_HEAD
Q_BLOCK = 128
ROPE_THETA = 10000.0
D_GROUPS = 4
D_GROUP_CH = D_MODEL // 8
W_D = D_GROUPS * D_GROUP_CH

EVEN_SIZES = (W_A, W_A, W_A, H_B * DQK_B, H_B * DQK_B, W_B, W_B, W_B, 4 * H_B)
ODD_SIZES = (Q_LORA, KV_LORA, QK_ROPE, W_D, W_C, W_D)
P_EVEN = sum(EVEN_SIZES)
P_ODD = sum(ODD_SIZES)


def split_cols(p, sizes):
    idx = [int(i) for i in np.cumsum(sizes)[:-1]]
    return jnp.split(p, idx, axis=-1)

def rms_norm_2(x, g):
    xf = x.astype(jnp.float32)
    y = xf * lax.rsqrt(jnp.mean(xf * xf, axis=-1, keepdims=True) + RMS_EPS)
    return (y * g.astype(jnp.float32)).astype(x.dtype)

def group_layer_norm(x, g, b, groups):
    B, S, C = x.shape
    xf = x.astype(jnp.float32).reshape(B, S, groups, C // groups)
    mu = jnp.mean(xf, axis=-1, keepdims=True)
    xc = xf - mu
    var = jnp.mean(xc * xc, axis=-1, keepdims=True)
    y = (xc * lax.rsqrt(var + LN_EPS)).reshape(B, S, C)
    return (y * g.astype(jnp.float32) + b.astype(jnp.float32)).astype(x.dtype)

def depthwise_conv_centred(x, w, b):
    K = w.shape[0]
    y = lax.conv_general_dilated(
        x, w[:, None, :].astype(x.dtype), window_strides=(1,),
        padding=[(K // 2, K // 2)], dimension_numbers=("NWC", "WIO", "NWC"),
        feature_group_count=x.shape[-1])
    return y + b.astype(x.dtype)

def rope_tables(positions):
    inv = ROPE_THETA ** (-jnp.arange(0, QK_ROPE, 2, dtype=jnp.float32) / QK_ROPE)
    ang = positions.astype(jnp.float32)[..., None] * inv
    return jnp.cos(ang), jnp.sin(ang)

def apply_rope(x, cos, sin):
    half = x.shape[-1] // 2
    xf = x.astype(jnp.float32)
    x1, x2 = xf[..., :half], xf[..., half:]
    return jnp.concatenate([x1 * cos - x2 * sin, x1 * sin + x2 * cos], axis=-1).astype(x.dtype)

def mlstm_chunkwise(q, k, v, i_pre, f_pre):
    B, H, S, dk = q.shape
    dv = v.shape[-1]
    nc = S // CHUNK
    f32 = jnp.float32

    def chunks(a):
        return jnp.moveaxis(a.reshape(B, H, nc, CHUNK, *a.shape[3:]), 2, 0)

    qc = chunks(q.astype(f32))
    kc = chunks(k.astype(f32) * (dk ** -0.5))
    vc = chunks(v.astype(f32))
    ic = chunks(i_pre.astype(f32))
    bc = jnp.cumsum(chunks(jax.nn.log_sigmoid(f_pre.astype(f32))), axis=-1)
    tril = jnp.tril(jnp.ones((CHUNK, CHUNK), dtype=bool))

    def step(carry, inp):
        C, n, m = carry
        qb, kb, vb, ib, bb = inp
        D = jnp.where(tril, bb[..., :, None] - bb[..., None, :] + ib[..., None, :], -jnp.inf)
        a = bb + m[..., None]
        m_t = jnp.maximum(a, jnp.max(D, axis=-1))
        Dw = jnp.exp(D - m_t[..., None])
        aw = jnp.exp(a - m_t)
        s = jnp.einsum('bhtd,bhsd->bhts', qb, kb) * Dw
        num = jnp.einsum('bhts,bhsv->bhtv', s, vb) + aw[..., None] * jnp.einsum('bhtd,bhdv->bhtv', qb, C)
        den = jnp.sum(s, axis=-1) + aw * jnp.einsum('bhtd,bhd->bht', qb, n)
        h = num / jnp.maximum(jnp.abs(den), jnp.exp(-m_t))[..., None]
        bL = bb[..., -1]
        g = bL[..., None] - bb + ib
        m_new = jnp.maximum(bL + m, jnp.max(g, axis=-1))
        wk = jnp.exp(g - m_new[..., None])
        decay = jnp.exp(bL + m - m_new)
        C_new = decay[..., None, None] * C + jnp.einsum('bhs,bhsd,bhsv->bhdv', wk, kb, vb)
        n_new = decay[..., None] * n + jnp.einsum('bhs,bhsd->bhd', wk, kb)
        return (C_new, n_new, m_new), h

    init = (jnp.zeros((B, H, dk, dv), f32), jnp.zeros((B, H, dk), f32), jnp.zeros((B, H), f32))
    _, hs = lax.scan(step, init, (qc, kc, vc, ic, bc))
    return jnp.moveaxis(hs, 0, 2).reshape(B, H, S, dv)

def even_layer(x, g_pre, g_post, w_in, b_gate, conv_w, conv_b, gn_g, gn_b, hn_g, w_out):
    B, S, _ = x.shape
    h = rms_norm_2(x, g_pre)
    p = h @ w_in
    a_val, a_gate, z_a, q, k, v, o, z_b, gates = split_cols(p, EVEN_SIZES)
    u = a_val * jax.nn.sigmoid(a_gate)
    u = depthwise_conv_centred(u, conv_w, conv_b)
    u = jax.nn.silu(group_layer_norm(u, gn_g, gn_b, A_GROUPS))
    y_a = u * jax.nn.silu(z_a)
    to_heads = lambda t, d: t.reshape(B, S, H_B, d).transpose(0, 2, 1, 3)
    qh, kh, vh = to_heads(q, DQK_B), to_heads(k, DQK_B), to_heads(v, DV_B)
    gt = (gates.astype(jnp.float32) + b_gate.astype(jnp.float32)).reshape(B, S, 4, H_B).transpose(2, 0, 3, 1)
    i_f, f_f, i_b, f_b = gt[0], gt[1], gt[2], gt[3]
    h_fwd = mlstm_chunkwise(qh, kh, vh, i_f, f_f)
    fl = lambda t: jnp.flip(t, axis=2)
    h_bwd = fl(mlstm_chunkwise(fl(qh), fl(kh), fl(vh), fl(i_b), fl(f_b)))
    hm = (h_fwd + h_bwd).transpose(0, 2, 1, 3)
    hm = rms_norm_2(hm, hn_g.reshape(H_B, DV_B)).astype(x.dtype)
    hm = jax.nn.sigmoid(o.reshape(B, S, H_B, DV_B)) * hm
    y_b = hm.reshape(B, S, W_B) * jax.nn.silu(z_b)
    y = jnp.concatenate([y_a, y_b], axis=-1) @ w_out
    return x + rms_norm_2(y, g_post)

def odd_layer(x, cos, sin, g_pre, g_post, w_in, g_q, w_uq, g_kv, w_ukv, w_fd, w_out):
    B, S, _ = x.shape
    h = rms_norm_2(x, g_pre)
    p = h @ w_in
    c_q, c_kv, k_r, f_in, z_c, z_d = split_cols(p, ODD_SIZES)
    qh = (rms_norm_2(c_q, g_q) @ w_uq).reshape(B, S, H_C, QK_NOPE + QK_ROPE)
    q_nope = qh[..., :QK_NOPE]
    q_rope = apply_rope(qh[..., QK_NOPE:], cos[:, :, None, :], sin[:, :, None, :])
    kv = (rms_norm_2(c_kv, g_kv) @ w_ukv).reshape(B, S, H_C, QK_NOPE + V_HEAD)
    k_nope, v = kv[..., :QK_NOPE], kv[..., QK_NOPE:]
    k_rope = apply_rope(k_r, cos, sin)
    scale = (QK_NOPE + QK_ROPE) ** -0.5
    nb = S // Q_BLOCK
    blk = lambda t: jnp.moveaxis(t.reshape(B, nb, Q_BLOCK, *t.shape[2:]), 1, 0)

    def attend(qs):
        qn, qr = qs
        s = jnp.einsum('bqhd,bkhd->bhqk', qn, k_nope) + jnp.einsum('bqhr,bkr->bhqk', qr, k_rope)
        pr = jax.nn.softmax(s.astype(jnp.float32) * scale, axis=-1).astype(v.dtype)
        return jnp.einsum('bhqk,bkhd->bqhd', pr, v)

    att = lax.map(attend, (blk(q_nope), blk(q_rope)))
    att = jnp.moveaxis(att, 0, 1).reshape(B, S, W_C)
    y_c = att * jax.nn.silu(z_c)
    fg = f_in.astype(jnp.float32).reshape(B, S, D_GROUPS, D_GROUP_CH)
    fr = jnp.real(jnp.fft.fft2(fg, axes=(1, 3), norm="ortho")).astype(x.dtype).reshape(B, S, W_D)
    y_d = (fr @ w_fd) * jax.nn.silu(z_d)
    y = jnp.concatenate([y_c, y_d], axis=-1) @ w_out
    return x + rms_norm_2(y, g_post)

def second_inputs(seed: int = 0) -> dict:
    key = jax.random.key(seed)
    ks = jax.random.split(key, 24)
    f32 = jnp.float32
    nrm = lambda k, shape, fan_in: jax.random.normal(k, shape, f32) * (fan_in ** -0.5)
    gain = lambda k, shape: 1.0 + 0.05 * jax.random.normal(k, shape, f32)
    small = lambda k, shape: 0.02 * jax.random.normal(k, shape, f32)
    x = jax.random.normal(ks[0], (BATCH, SEQ, D_MODEL), f32)
    positions = (jnp.arange(SEQ, dtype=jnp.int32)[None, :]
                 + jax.random.randint(ks[1], (BATCH, 1), 0, 1024, dtype=jnp.int32))
    fbias = jnp.linspace(3.0, 6.0, H_B, dtype=f32)
    gate_base = jnp.concatenate([jnp.zeros((H_B,), f32), fbias, jnp.zeros((H_B,), f32), fbias])
    even_b_gate = gate_base[None, :] + 0.1 * jax.random.normal(ks[2], (N_EVEN, 4 * H_B), f32)
    return {
        "x": x,
        "positions": positions,
        "even_g_pre": gain(ks[3], (N_EVEN, D_MODEL)),
        "even_g_post": gain(ks[4], (N_EVEN, D_MODEL)),
        "even_w_in": nrm(ks[5], (N_EVEN, D_MODEL, P_EVEN), D_MODEL),
        "even_b_gate": even_b_gate,
        "even_conv_w": nrm(ks[6], (N_EVEN, CONV_K, W_A), CONV_K),
        "even_conv_b": small(ks[7], (N_EVEN, W_A)),
        "even_gn_g": gain(ks[8], (N_EVEN, W_A)),
        "even_gn_b": small(ks[9], (N_EVEN, W_A)),
        "even_hn_g": gain(ks[10], (N_EVEN, W_B)),
        "even_w_out": nrm(ks[11], (N_EVEN, W_A + W_B, D_MODEL), W_A + W_B),
        "odd_g_pre": gain(ks[12], (N_ODD, D_MODEL)),
        "odd_g_post": gain(ks[13], (N_ODD, D_MODEL)),
        "odd_w_in": nrm(ks[14], (N_ODD, D_MODEL, P_ODD), D_MODEL),
        "odd_g_q": gain(ks[15], (N_ODD, Q_LORA)),
        "odd_w_uq": nrm(ks[16], (N_ODD, Q_LORA, H_C * (QK_NOPE + QK_ROPE)), Q_LORA),
        "odd_g_kv": gain(ks[17], (N_ODD, KV_LORA)),
        "odd_w_ukv": nrm(ks[18], (N_ODD, KV_LORA, H_C * (QK_NOPE + V_HEAD)), KV_LORA),
        "odd_w_fd": nrm(ks[19], (N_ODD, W_D, W_D), W_D),
        "odd_w_out": nrm(ks[20], (N_ODD, W_C + W_D, D_MODEL), W_C + W_D),
    }

def second_block(x, positions, even_g_pre, even_g_post, even_w_in, even_b_gate, even_conv_w,
              even_conv_b, even_gn_g, even_gn_b, even_hn_g, even_w_out, odd_g_pre, odd_g_post,
              odd_w_in, odd_g_q, odd_w_uq, odd_g_kv, odd_w_ukv, odd_w_fd, odd_w_out):
    cos, sin = rope_tables(positions)
    h = x
    for layer in range(DEPTH_2):
        j = layer // 2
        if layer % 2 == 0:
            h = even_layer(h, even_g_pre[j], even_g_post[j], even_w_in[j], even_b_gate[j],
                           even_conv_w[j], even_conv_b[j], even_gn_g[j], even_gn_b[j],
                           even_hn_g[j], even_w_out[j])
        else:
            h = odd_layer(h, cos, sin, odd_g_pre[j], odd_g_post[j], odd_w_in[j], odd_g_q[j],
                          odd_w_uq[j], odd_g_kv[j], odd_w_ukv[j], odd_w_fd[j], odd_w_out[j])
    return h


def setup_inputs(seed=0):
    out = dict(first_inputs(seed))
    for name, value in second_inputs(seed + 1).items():
        if name != "x":
            out[name + "_2"] = value
    return out


def reference(
    x, norm1_g, w_in, moba_q_norm_g, moba_k_norm_g, t5_bias, gla_gate_up, gla_gate_bias,
    gla_out_norm_g, w_branch_moba, w_branch_gla, w_out, norm2_g, w_up, w_down, positions_2,
    even_g_pre_2, even_g_post_2, even_w_in_2, even_b_gate_2, even_conv_w_2, even_conv_b_2,
    even_gn_g_2, even_gn_b_2, even_hn_g_2, even_w_out_2, odd_g_pre_2, odd_g_post_2, odd_w_in_2,
    odd_g_q_2, odd_w_uq_2, odd_g_kv_2, odd_w_ukv_2, odd_w_fd_2, odd_w_out_2,
):
    x = first_block(
        x, norm1_g, w_in, moba_q_norm_g, moba_k_norm_g, t5_bias, gla_gate_up, gla_gate_bias,
        gla_out_norm_g, w_branch_moba, w_branch_gla, w_out, norm2_g, w_up, w_down,
    )
    return second_block(
        x, positions_2, even_g_pre_2, even_g_post_2, even_w_in_2, even_b_gate_2, even_conv_w_2,
        even_conv_b_2, even_gn_g_2, even_gn_b_2, even_hn_g_2, even_w_out_2, odd_g_pre_2,
        odd_g_post_2, odd_w_in_2, odd_g_q_2, odd_w_uq_2, odd_g_kv_2, odd_w_ukv_2, odd_w_fd_2,
        odd_w_out_2,
    )


_drawn_inputs = setup_inputs


def setup_inputs(seed=0):
    import zlib

    import numpy as np

    out = dict(_drawn_inputs(seed))
    spreads = {}
    factors = {'moba_q_norm_g': 5.94,
     'moba_k_norm_g': 7.471,
     'even_conv_b_2': 3.439,
     'even_gn_b_2': 6.295,
     'even_hn_g_2': 2.911,
     'odd_g_q_2': 8.0,
     'odd_g_kv_2': 4.124}
    for name, (base, spread) in spreads.items():
        noise = np.random.default_rng([zlib.crc32(name.encode()), seed]).standard_normal(out[name].shape)
        drawn = base * np.exp(spread * noise) if base else spread * noise
        out[name] = jnp.asarray(drawn.astype(out[name].dtype))
    for name, factor in factors.items():
        out[name] = (out[name] * factor).astype(out[name].dtype)
    return out
```

```python
import math
from contextlib import ExitStack

import concourse.bass as bass
from concourse import mybir

F32 = mybir.dt.float32
F32R = mybir.dt.float32r
I32 = mybir.dt.int32
ALU = mybir.AluOpType
ACT = mybir.ActivationFunctionType
AX = mybir.AxisListType
P = 128
TOK = 256
NT = TOK // P
D = 1024
FF = 4096
NEG = -1e30
UNIT = 1024
RAW, SPLIT = 4, 5
STAGES = 3

TWO_PI = (6.28125, 0.0019350051879882812, 2.0 * math.pi - 6.28125 - 0.0019350051879882812)

VEC_ROWS = {}


def vec_plan(named):
    at = 0
    for name, n in named:
        VEC_ROWS[name] = (at, n)
        at += n
    return at


VECS = vec_plan([("norm1", 8), ("gbias", 4), ("gout", 2), ("norm2", 8), ("mq", 1), ("mk", 1),
                 ("epre", 8), ("convb", 8), ("hn", 8), ("opre", 8), ("gq", 3), ("gkv", 2)])


def program(nc, A, out):
    ctx = ExitStack()
    with ctx:
        def sb(name, shape, dt=F32, c=ctx):
            return c.enter_context(nc.sbuf_tensor(name, shape, dt))

        sems = {}

        def sem(name):
            if name not in sems:
                sems[name] = ctx.enter_context(nc.semaphore(name))
            return sems[name]

        w_in, e_in, o_in = A["w_in"][0], A["even_w_in_2"][0], A["odd_w_in_2"][0]
        CH, UN, CI = [], [], {}

        def chunk(name, w, n0, nn, kts, acts):
            CI[name] = len(CH)
            per = max(1, UNIT // nn)
            first = len(UN)
            for k in range(0, kts, per):
                UN.append((w, k, min(per, kts - k), n0, nn))
            CH.append(dict(name=name, nn=nn, kts=kts, acts=acts, units=range(first, len(UN))))

        for name, n0 in [("mq", 0), ("mk", 512), ("mv", 1024)]:
            chunk(name, w_in, n0, 512, 8, "n1")
        chunk("glow", w_in, 3584, 16, 8, "n1")
        for name, n0 in [("gq", 1536), ("gk", 2048), ("gv0", 2560), ("gv1", 3072),
                         ("go0", 3600), ("go1", 4112), ("gm0", 4624), ("gm1", 5136),
                         ("gg0", 5648), ("gg1", 6160)]:
            chunk(name, w_in, n0, 512, 8, "n1")
        for n in range(2):
            chunk(f"bm{n}", A["w_branch_moba"][0], 512 * n, 512, 4, "ym")
            chunk(f"bg{n}", A["w_branch_gla"][0], 512 * n, 512, 8, "yg")
        for n in range(2):
            chunk(f"wo{n}", A["w_out"][0], 512 * n, 512, 8, "mix")
        for n in range(8):
            chunk(f"up{n}", A["w_up"][0], 512 * n, 512, 8, "n2")
        for n in range(2):
            chunk(f"dn{n}", A["w_down"][0], 512 * n, 512, 32, "u")
        if STAGES >= 2:
            chunk("eg", e_in, 7168, 16, 8, "en")
            for name, n0 in [("ea0", 0), ("eb0", 1024), ("ea1", 512), ("eb1", 1536), ("eq", 3072), ("ek", 3584),
                             ("ev0", 4096), ("ev1", 4608), ("eo0", 5120), ("ew0", 6144), ("eo1", 5632),
                             ("ew1", 6656), ("ez0", 2048), ("ez1", 2560)]:
                chunk(name, e_in, n0, 512, 8, "en")
            for n in range(2):
                chunk(f"ey{n}", A["even_w_out_2"][0], 512 * n, 512, 16, "ey")
        if STAGES >= 3:
            ukv, uq = A["odd_w_ukv_2"][0], A["odd_w_uq_2"][0]
            chunk("oq", o_in, 0, 384, 8, "on")
            chunk("okv", o_in, 384, 320, 8, "on")
            chunk("of", o_in, 704, 512, 8, "on")
            chunk("oz0", o_in, 1216, 512, 8, "on")
            for n in range(4):
                chunk(f"oc{n}", ukv, 512 * n, 512, 2, "ckv")
            chunk("oz1", o_in, 1728, 512, 8, "on")
            for n in range(3):
                chunk(f"ou{n}", uq, 512 * n, 512, 3, "cq")
            chunk("ozd", o_in, 2240, 512, 8, "on")
            chunk("ofd", A["odd_w_fd_2"][0], 0, 512, 4, "fr")
            for n in range(2):
                chunk(f"oy{n}", A["odd_w_out_2"][0], 512 * n, 512, 12, "oy")

        def split_keys(name, kts):
            return [("tr", name, j) for j in range((kts + 1) // 2)]

        AUX = [("vec",)] + [("bias", h) for h in range(8)] + split_keys("n1", 8)
        AUX += [("qkT", w, j) for w in range(2) for j in range(2)]
        AUX += [("glT",), ("qk0", 0), ("qk0", 1)] + [("qk1", p, i) for i in range(2) for p in range(2)]
        AUX += [("gz", 0), ("gz", 1)]
        AUX += [("pt", i) for i in range(6)]
        AUX += [("gqT", 0), ("gqT", 1), ("gkT", 0), ("gkT", 1)]
        AUX += [("pv", 0), ("pv", 1), ("kdt", 0), ("kdt", 1), ("ga", 0), ("ga", 1)]
        AUX += [("kv", j, i) for j in range(3) for i in range(2)]
        AUX += [("o", t, i) for t in range(2) for i in range(2)]
        AUX += split_keys("ym", 4) + split_keys("yg", 8) + split_keys("mix", 8) + split_keys("n2", 8)
        AUX += split_keys("u", 32)
        if STAGES >= 2:
            AUX += split_keys("en", 8) + [("gat", 0), ("gat", 1), ("wcv",), ("uT", 0), ("uT", 1), ("mcol",)]
            AUX += [("mb", h) for h in range(4)] + [("uT", 2), ("uT", 3)]
            AUX += [("eqT", w, j) for w in range(2) for j in range(2)] + [("kq", h) for h in range(4)]
            AUX += [("num", h, d, t) for h in range(4) for d in range(2) for t in range(2)]
            AUX += split_keys("eh", 8) + [("cvT", t, i) for t in range(2) for i in range(2)] + split_keys("ea", 8)
        if STAGES >= 3:
            AUX += split_keys("on", 8) + split_keys("cq", 3) + split_keys("ckv", 2) + [("krT",)]
            AUX += [("dft", g) for g in range(4)] + split_keys("fr", 4) + [("knT", j) for j in range(4)]
            AUX += [("qnT", j) for j in range(4)] + [("qrT", j) for j in range(2)]
            for h in range(8):
                AUX += [("os", h)] + [("opt", h - 1)] * (h >= 1) + [("opv", (h - 3) // 2)] * (h >= 3 and h % 2)
            AUX += [("opt", 7), ("opv", 3)] + split_keys("yd", 4) + split_keys("yc", 8)
        PLACE = {key: i for i, key in enumerate(AUX)}
        SPLITS = {key: i for i, key in enumerate(k for k in AUX if k[0] == "tr")}

        raw = [sb(f"raw{i}", [P, UNIT]) for i in range(RAW)]
        whi = [sb(f"whi{i}", [P, UNIT], F32R) for i in range(SPLIT)]
        wlo = [sb(f"wlo{i}", [P, UNIT], F32R) for i in range(SPLIT)]
        H = sb("H", [P, NT, D])
        XN = sb("XN", [P, NT, D])
        a_hi, a_lo = sb("a_hi", [P, 8, TOK], F32R), sb("a_lo", [P, 8, TOK], F32R)
        b_hi, b_lo = sb("b_hi", [P, 12, TOK], F32R), sb("b_lo", [P, 12, TOK], F32R)
        ident = sb("ident", [P, P])
        vec_in, vec = sb("vec_in", [P, P]), sb("vec", [P, P])
        stat = sb("stat", [P, 8])
        epsc = sb("epsc", [P, 4])
        ystat = sb("ystat", [P, 2, NT])
        junk = sb("junk", [P, D])
        acc = [ctx.enter_context(nc.psum_tensor(f"acc{i}", [P, 512], F32)) for i in range(4)]
        aux = [ctx.enter_context(nc.psum_tensor(f"aux{i}", [P, 512], F32)) for i in range(4)]

        def gain(name, k):
            r = VEC_ROWS[name][0] + k
            return vec[:, r:r + 1]

        c1 = ExitStack()
        t5x = sb("t5x", [33, 8], c=c1)
        B0, B1 = sb("B0", [P, 8, P], c=c1), sb("B1", [P, 8, TOK], c=c1)
        QKN = sb("QKN", [P, 2, NT, 512], c=c1)
        QKT = sb("QKT", [P, 2, 4, TOK], c=c1)
        PR = sb("PR", [P, 8 * 384], c=c1)
        PT = sb("PT", [P, 24, P], c=c1)
        MV = sb("MV", [P, NT, 512], c=c1)
        GQK = sb("GQK", [P, 2, NT, 512], c=c1)
        T = sb("T", [P, 4, 4, TOK], c=c1)
        rmask = sb("rmask", [P, 4 * TOK], c=c1)
        gl = sb("gl", [P, NT, 16], c=c1)
        glT = sb("glT", [16, TOK], c=c1)
        gup = sb("gup", [16, 512], c=c1)
        edl = sb("edl", [P, 4, 4], c=c1)
        qst = sb("qst", [P, 2, NT, 8], c=c1)
        pst = sb("pst", [P, 3, NT, 8], c=c1)
        gst = sb("gst", [P, NT, 4], c=c1)
        c1.close()

        def flat(ap):
            while len(ap.shape) > 2:
                ap = ap.rearrange("p a b -> p (a b)") if len(ap.shape) == 3 else \
                    ap.rearrange("p a b c -> p (a b c)") if len(ap.shape) == 4 else \
                    ap.rearrange("p a b c d -> p (a b c d)")
            return ap

        P0 = PR[:, 0:1024].rearrange("p (h s) -> p h s", h=8)
        P1 = PR[:, 1024:3072].rearrange("p (h s) -> p h s", h=8)
        T1, T2, T3, T4 = T[:, 0], T[:, 1], T[:, 2], T[:, 3]
        bias_w = [junk[:, 0:512], junk[:, 512:1024]]
        onehot = flat(GQK[0:33, 0, 0:1])
        ST = [flat(B0[:, :, :]).rearrange("p (h v) -> p h v", h=4),
              flat(B1[:, 0:4]).rearrange("p (h v) -> p h v", h=4),
              flat(B1[:, 4:8]).rearrange("p (h v) -> p h v", h=4)]
        QD = flat(QKN[:, 0]).rearrange("p (h c) -> p h c", h=4)
        KI = flat(QKN[:, 1]).rearrange("p (h c) -> p h c", h=4)
        KD = QKT[:, 0]
        KDT = flat(QKT[:, 1]).rearrange("p (t h d) -> p t h d", t=2, h=4)
        OG = PR[:, 0:2048].rearrange("p (t n) -> p t n", t=2)
        GA = PR[:, 2048:3072].rearrange("p (t h c) -> p t h c", t=2, h=4)
        SGO = flat(PT[:, 0:16]).rearrange("p (t n) -> p t n", t=2)
        YM = GQK[:, 0]
        SG = flat(T[:, :, :, :]).rearrange("p (w t n) -> p w t n", w=2, t=2)
        MX, MTMP = OG, QKN[:, 1, 0]
        GV = XN

        c2 = ExitStack()
        u_hi, u_lo = sb("u_hi", [P, 20, TOK], F32R, c=c2), sb("u_lo", [P, 20, TOK], F32R, c=c2)
        RL = sb("RL", [P, 2, NT, 512], c=c2)
        c2.close()

        c3 = ExitStack()
        if STAGES >= 2:
            AV = sb("AV", [P, NT, D], c=c3)
            EU = sb("EU", [P, 8, TOK + 30], c=c3)
            CV = sb("CV", [P, 8, TOK], c=c3)
            wcv = sb("wcv", [P, 8, 32], c=c3)
            gates = sb("gates", [P, NT, 2, 2, 4], c=c3)
            gbias = sb("gbias", [P, 16], c=c3)
            rone = sb("rone", [4, 2, TOK], c=c3)
            mcol = sb("mcol", [P, 2, 2, NT, 4], c=c3)
            den = sb("den", [P, 4, 2, NT], c=c3)
            EQK = sb("EQK", [P, 2, NT, 512], c=c3)
            EQT = sb("EQT", [P, 2, 4, TOK], c=c3)
            EV = sb("EV", [P, NT, 4, 258], c=c3)
            DW = sb("DW", [P, 4, 2, 384], c=c3)
            SOB = sb("SOB", [P, NT, D], c=c3)
            ETMP = sb("ETMP", [P, NT, 512], c=c3)
            gng, gnb = sb("gng", [P, D], c=c3), sb("gnb", [P, D], c=c3)
            est = sb("est", [P, NT, 4], c=c3)
            bst, bag = sb("bst", [P, 16, 6], c=c3), sb("bag", [P, 16, 2], c=c3)
            HM = flat(EQK[:, :, :, :]).rearrange("p (t n) -> p t n", t=NT)
            SZA = flat(EQT[:, :, :, :]).rearrange("p (t n) -> p t n", t=NT)
            post_g = flat(EV[:, 0])[:, 0:D]
            wcv_in = flat(CV[0:31, 0:4])
            RF, RX = XN[0:4, 0, 0:512].rearrange("p (d t) -> p d t", d=2), XN[0:4, 0, 512:1024].rearrange("p (d t) -> p d t", d=2)
            RG, RM = XN[0:4, 1, 0:512].rearrange("p (d t) -> p d t", d=2), XN[0:4, 1, 512:1024].rearrange("p (d t) -> p d t", d=2)
        c3.close()

        c4 = ExitStack()
        if STAGES >= 3:
            QF = sb("QF", [P, NT, 1536], c=c4)
            KN = sb("KN", [P, NT, 8, P], c=c4)
            OV = sb("OV", [P, NT, 8, P], c=c4)
            KR0, KR = sb("KR0", [P, NT, 64], c=c4), sb("KR", [P, NT, 2, 64], c=c4)
            KRT = sb("KRT", [P, TOK], c=c4)
            QNT, KNT = sb("QNT", [P, 8, TOK], c=c4), sb("KNT", [P, 8, TOK], c=c4)
            QRT = sb("QRT", [P, 4, TOK], c=c4)
            SZC = sb("SZC", [P, NT, D], c=c4)
            YD = sb("YD", [P, NT, 512], c=c4)
            FX = sb("FX", [P, NT, 512], c=c4)
            dft_s = sb("dft_s", [P, NT, 512], c=c4)
            dft_c = sb("dft_c", [P, 2, P], c=c4)
            ZT = sb("ZT", [P, 5 * 512], c=c4)
            post2 = sb("post2", [P, D], c=c4)
            pos_i = sb("pos_i", [P, NT], I32, c=c4)
            pos = sb("pos", [P, NT], c=c4)
            invf = sb("invf", [P, 32], c=c4)
            ang = sb("ang", [P, NT, 32], c=c4)
            turns = sb("turns", [P, 2, NT, 32], c=c4)
            trig = sb("trig", [P, 2, NT, 32], c=c4)

            cst = sb("cst", [P, 2, NT], c=c4)
            omx, osum, orec = [sb(n, [P, 8, NT], c=c4) for n in ("omx", "osum", "orec")]
            OP = [ZT[:, 512 * i:512 * i + 512].rearrange("p (t s) -> p t s", t=NT) for i in range(2)]
            OPT = [ZT[:, 1024 + 512 * i:1536 + 512 * i].rearrange("p (s t) -> p s t", s=NT) for i in range(3)]
            YC = QF[:, :, 0:D]
            rt = ZT[:, 0:1024].rearrange("p (a b) -> p a b", a=4)
            QR = XN[:, :, 0:512]
            YO = KN[:, :].rearrange("p t h d -> p t (h d)")
        c4.close()

        def bank(key):
            return aux[PLACE[key] % 4]

        def aux_wait(e, key):
            i = PLACE[key]
            e.wait_ge(sem(f"aux_ready{i % 4}"), i // 4 + 1)

        def aux_free(ins, key):
            ins.then_inc(sem(f"aux_free{PLACE[key] % 4}"), 1)

        def aux_done(e, key):
            i = PLACE[key]
            e.wait_ge(sem(f"aux_free{i % 4}"), i // 4 + 1)

        def acc_wait(e, c, t):
            if t == 0:
                e.wait_ge(sem("tile0_done"), CI[c] + 1)
            else:
                e.wait_ge(sem("units_used"), CH[CI[c]]["units"][-1] + 1)

        def acc_of(c, t):
            return acc[2 * (CI[c] % 2) + t][:, 0:CH[CI[c]]["nn"]]

        def acc_free(ins, c):
            ins.then_inc(sem(f"acc_free{CI[c] % 2}"), 1)

        def acc_done(e, c, t):
            e.wait_ge(sem(f"acc_free{CI[c] % 2}"), 2 * (CI[c] // 2) + t + 1)

        class Chain:
            def __init__(self, e, name):
                self.e, self.s, self.n = e, sem(name), 0

            def __call__(self, ins):
                self.n += 1
                ins.then_inc(self.s, 1)
                self.e.wait_ge(self.s, self.n)

        def w_view(buf, u):
            _, _, nk, _, nn = UN[u]
            return buf[:, 0:nk * nn]

        WHERE = {"n1": (a_hi, a_lo, 0), "mix": (a_hi, a_lo, 0), "n2": (a_hi, a_lo, 0), "en": (a_hi, a_lo, 0),
                 "on": (a_hi, a_lo, 0), "eh": (a_hi, a_lo, 0), "ym": (b_hi, b_lo, 0), "yg": (b_hi, b_lo, 4),
                 "ea": (b_hi, b_lo, 0), "cq": (b_hi, b_lo, 0), "ckv": (b_hi, b_lo, 3), "fr": (b_hi, b_lo, 5),
                 "yd": (b_hi, b_lo, 8), "yc": (b_hi, b_lo, 0)}

        def act_tile(name, k):
            if name == "ey":
                name, k = ("ea", k) if k < 8 else ("eh", k - 8)
            if name == "oy":
                name, k = ("yc", k) if k < 8 else ("yd", k - 8)
            key = ("tr", name, k // 2)
            if name == "u":
                return (b_hi[:, k], b_lo[:, k], key) if k < 12 else (u_hi[:, k - 12], u_lo[:, k - 12], key)
            hi, lo, o = WHERE[name]
            return hi[:, o + k], lo[:, o + k], key

        def halves(key):
            return bank(key)[:, :].rearrange("p (k t) -> p k t", k=2)

        block = ctx.enter_context(nc.Block())

        @block.sync
        def _(sp):
            sp.dma_start(H[:, :, :], A["x"][0].rearrange("(t p) d -> p t d", p=P)).then_inc(sem("x_in"), 16)
            for u, (w, k, nk, n0, nn) in enumerate(UN):
                if u >= RAW:
                    sp.wait_ge(sem("lo_done"), u - RAW + 1)
                dst = raw[u % RAW][:, 0:nk * nn].rearrange("p (k n) -> p k n", k=nk)
                src = w[k * P:(k + nk) * P, n0:n0 + nn].rearrange("(k p) n -> p k n", p=P)
                sp.dma_start(dst, src).then_inc(sem(f"raw_in{u % RAW}"), 16)
            for t in range(NT):
                sp.wait_ge(sem("h_out"), NT * (STAGES - 2) + t + 1)
                sp.dma_start(out[0, t * P:(t + 1) * P, :], H[:, t]).then_inc(sem("stored"), 16)
            sp.wait_ge(sem("stored"), 16 * NT)

        @block.gpsimd
        def _(pool):
            chain = Chain(pool, "pool_chain")
            pool.memset(vec_in[:, :], 0.0).then_inc(sem("vec_zero"), 1)
            chain(pool.memset(ident[:, :], 0.0))
            pool.affine_select(out=ident[:, :], in_=ident[:, :], compare_op=ALU.not_equal, fill=1.0, base=0,
                               pattern=[[-1, P]], channel_multiplier=1).then_inc(sem("ident"), 1)
            chain(pool.memset(t5x[:, :], NEG))
            pool.dma_start(t5x[0:32, :], A["t5_bias"]).then_inc(sem("t5_in"), 16)
            pool.dma_start(onehot, A["onehot"]).then_inc(sem("t5_in"), 16)
            pool.dma_start(gup[:, :], A["gla_gate_up"][0]).then_inc(sem("gup_in"), 16)
            for i in range(8):
                h = 2 * (i % 4) + i // 4
                aux_done(pool, ("bias", i))
                pool.dma_start(A["skew"][i], bias_w[i % 2]).then_inc(sem("skew_out"), 16)
                pool.wait_ge(sem("skew_out"), 16 * (i + 1))
                line = A["skew"][i].rearrange("a b -> (a b)")
                for t, B in enumerate((B0, B1)):
                    lo = 255 - P * t
                    src = line[lo:lo + 511 * (P - 1) + TOK]
                    src = bass.AP(tensor=src.tensor, offset=src.offset, ap=[[511, P], [1, P * (t + 1)]])
                    pool.dma_start(B[:, i], src).then_inc(sem("bias_in"), 16)
            for t in range(NT):
                aux_done(pool, ("ga", t))
                chain(pool.affine_select(out=GA[:, t], in_=GA[:, t], compare_op=ALU.is_ge, fill=0.0, base=0,
                                         pattern=[[0, 4], [1, P]], channel_multiplier=-1))
                pool.memset(GA[0:64, t, :, 64:128], 0.0).then_inc(sem("ga_masked"), 1)
            if STAGES >= 2:
                pool.wait_ge(sem("units_used"), CH[CI["dn1"]]["units"][-1] + 1)
                pool.dma_start(gbias[:, :], A["even_b_gate_2"][0].partition_broadcast(P)).then_inc(sem("gbias_in"), 16)
                pool.dma_start(wcv_in, A["even_conv_w_2"][0]).then_inc(sem("wcv_in"), 16)
                pool.dma_start(gng[:, :], A["even_gn_g_2"][0].partition_broadcast(P)).then_inc(sem("gn_in"), 16)
                pool.dma_start(gnb[:, :], A["even_gn_b_2"][0].partition_broadcast(P)).then_inc(sem("gn_in"), 16)
                for h in range(4):
                    pool.wait_ge(sem("dw_exp"), h + 1)
                    for d in range(2):
                        v = DW[:, h, d].rearrange("p (b c) -> p b c", b=3)[:, 0:3:2]
                        pool.affine_select(out=v, in_=v, compare_op=ALU.is_ge, fill=0.0, base=0,
                                           pattern=[[0, 2], [1 - 2 * d, P]], channel_multiplier=2 * d - 1
                                           ).then_inc(sem("dw_masked"), 1)
                aux_wait(pool, ("num", 3, 1, 1))
                pool.dma_start(post_g, A["even_g_post_2"][0].partition_broadcast(P)).then_inc(sem("post_in"), 16)
            if STAGES >= 3:
                pool.wait_ge(sem("h_out"), NT)
                pool.dma_start(pos_i[:, :], A["positions_2"][0].rearrange("(t p) -> p t", p=P),
                               allow_slow_non_contiguous=True).then_inc(sem("pos_in"), 16)
                pool.dma_start(invf[:, :], A["inv_freq"].partition_broadcast(P)).then_inc(sem("pos_in"), 16)
                pool.dma_start(dft_s[:, :], A["dft_s"].rearrange("(t p) n -> p t n", p=P)).then_inc(sem("dft_in"), 16)
                pool.dma_start(dft_c[:, :], A["dft_c"].rearrange("a p n -> p a n")).then_inc(sem("dft_in"), 16)
                pool.dma_start(post2[:, :], A["odd_g_post_2"][0].partition_broadcast(P)).then_inc(sem("post_in"), 16)

        @block.scalar
        def _(act):
            chain = Chain(act, "act_chain")
            at = [0]

            def pump(c, ahead=SPLIT - 1):
                last = min(CH[CI[c]]["units"][-1] + ahead, len(UN) - 1)
                while at[0] <= last:
                    u = at[0]
                    act.wait_ge(sem(f"raw_in{u % RAW}"), 16 * (u // RAW + 1))
                    if u >= SPLIT:
                        act.wait_ge(sem("units_used"), u - SPLIT + 1)
                    act.activation(w_view(whi[u % SPLIT], u), w_view(raw[u % RAW], u), ACT.Copy
                                   ).then_inc(sem("hi_done"), 1)
                    at[0] += 1

            def split_hi(name, ks, g=None):
                for j in range(ks[0] // 2, (ks[-1] + 2) // 2):
                    key = ("tr", name, j)
                    aux_wait(act, key)
                    for i in range(min(2, ks[-1] + 1 - 2 * j)):
                        hi = act_tile(name, 2 * j + i)[0]
                        if g is None:
                            ins = act.activation(hi, halves(key)[:, i], ACT.Copy)
                        else:
                            ins = act.activation(hi, halves(key)[:, i], ACT.Copy, scale=g(2 * j + i))
                    ins.then_inc(sem("hi_split"), 1)

            def rstd(ap, n, eps=0):
                chain(act.activation(ap, ap, ACT.Ln, scale=1.0 / n, bias=epsc[0:ap.shape[0], eps:eps + 1]))
                return act.activation(ap, ap, ACT.Exp, scale=-0.5)

            def norm_stats(i, before):
                for t in range(NT):
                    before(t)
                    chain(act.activation(junk[:, :], H[:, t], ACT.Square, accum_out=stat[:, 2 * i + t:2 * i + t + 1]))
                rstd(stat[:, 2 * i:2 * i + 2], D).then_inc(sem("rstd"), 1)

            def copy_out(c, dst, t, func=ACT.Copy):
                acc_wait(act, c, t)
                acc_free(act.activation(dst, acc_of(c, t), func), c)

            act.wait_ge(sem("vec_zero"), 1)
            for name, key in (("norm1", "norm1_g"), ("gbias", "gla_gate_bias"), ("gout", "gla_out_norm_g"),
                              ("norm2", "norm2_g"), ("epre", "even_g_pre_2"), ("convb", "even_conv_b_2"),
                              ("hn", "even_hn_g_2"), ("opre", "odd_g_pre_2"), ("gq", "odd_g_q_2"),
                              ("gkv", "odd_g_kv_2")):
                r, n = VEC_ROWS[name]
                act.dma_start(vec_in[r:r + n, :], A[key][0].rearrange("(r c) -> r c", c=P)).then_inc(sem("vec_in"), 16)
            for name, key in (("mq", "moba_q_norm_g"), ("mk", "moba_k_norm_g")):
                r = VEC_ROWS[name][0]
                for i in range(2):
                    act.dma_start(vec_in[r:r + 1, 64 * i:64 * i + 64], A[key]).then_inc(sem("vec_in"), 16)

            act.wait_ge(sem("consts"), 1)
            norm_stats(0, lambda t: act.wait_ge(sem("x_in"), 16))
            pump("mq", -1)
            aux_done(act, ("vec",))
            split_hi("n1", range(8), lambda k: gain("norm1", k))
            for w, c in enumerate(("mq", "mk")):
                pump(c)
                for t in range(NT):
                    acc_wait(act, c, t)
                    act.activation(QKN[:, w, t], acc_of(c, t), ACT.Square).then_inc(sem("q_square"), 1)
                act.wait_ge(sem("q_sum"), 2 * w + 2)
                rstd(flat(qst[:, w]), 64).then_inc(sem("q_rstd"), 1)
            pump("mv")
            for t in range(NT):
                copy_out("mv", MV[:, t], t)
            pump("glow")
            for t in range(NT):
                copy_out("glow", gl[:, t], t)
            pump("gq")
            for t in range(NT):
                copy_out("gq", GQK[:, 0, t], t)
            aux_wait(act, ("glT",))
            aux_free(act.activation(glT[:, :], bank(("glT",))[0:16, 0:TOK], ACT.Copy), ("glT",))
            for t, PX in enumerate((P0, P1)):
                act.wait_ge(sem("p_max"), t + 1)
                for h in range(8):
                    ins = act.activation(PX[:, h], PX[:, h], ACT.Exp, bias=pst[:, 0, t, h:h + 1],
                                         accum_out=pst[:, 1, t, h:h + 1])
                ins.then_inc(sem("p_exp"), 1)
                if t == 0:
                    pump("gk", 1)
            pump("gk")
            for t in range(NT):
                copy_out("gk", GQK[:, 1, t], t)
            for j in range(2):
                aux_wait(act, ("gz", j))
                for i in range(2):
                    ins = act.activation(T1[:, 2 * j + i], halves(("gz", j))[:, i], ACT.Abs,
                                         bias=gain("gbias", 2 * j + i))
                chain(ins)
                act.activation(T1[:, 2 * j:2 * j + 2], T1[:, 2 * j:2 * j + 2], ACT.Exp, scale=-1.0
                               ).then_inc(sem("gz_abs"), 1)
            act.wait_ge(sem("gz_abs"), 2)
            act.activation(T1, T1, ACT.Ln, bias=epsc[:, 2:3]).then_inc(sem("gz_ln"), 1)
            pump("gv0", 1)
            act.wait_ge(sem("g_cum"), 1)
            act.activation(T1, T3, ACT.Exp, scale=1.0 / 16)
            act.activation(T4, T3, ACT.Exp, scale=-1.0 / 16).then_inc(sem("g_exp"), 1)
            act.wait_ge(sem("g_rest"), 1)
            act.activation(T2, T2, ACT.Exp, scale=1.0 / 16).then_inc(sem("g_exp"), 1)
            pump("gv0")
            for t in range(NT):
                copy_out("gv0", GV[:, t, 0:512], t)
            for i in range(6):
                aux_wait(act, ("pt", i))
                aux_free(act.activation(flat(PT[:, 4 * i:4 * i + 4]), bank(("pt", i))[:, :], ACT.Copy), ("pt", i))
            pump("gv1")
            for t in range(NT):
                copy_out("gv1", GV[:, t, 512:1024], t)
            for t in range(NT):
                aux_wait(act, ("kdt", t))
                aux_free(act.activation(flat(KDT[:, t]), bank(("kdt", t))[:, :], ACT.Copy), ("kdt", t))
            for t in range(NT):
                aux_wait(act, ("ga", t))
                aux_free(act.activation(flat(GA[:, t]), bank(("ga", t))[:, :], ACT.Copy), ("ga", t))
            for n in range(2):
                pump(f"go{n}")
                for t in range(NT):
                    acc_wait(act, f"go{n}", t)
                    act.activation(SGO[:, t, 512 * n:512 * n + 512], acc_of(f"go{n}", t), ACT.Sigmoid
                                   ).then_inc(sem("go_sig"), 1)
            for t in range(NT):
                for i in range(2):
                    aux_wait(act, ("o", t, i))
                    aux_free(act.activation(OG[:, t, 512 * i:512 * i + 512], bank(("o", t, i))[:, :], ACT.Copy),
                             ("o", t, i))
                    aux_done(act, ("o", t, i))
                    for h in (2 * i, 2 * i + 1):
                        ins = act.activation(junk[:, 256 * h:256 * h + 256], OG[:, t, 256 * h:256 * h + 256], ACT.Square,
                                             accum_out=gst[:, t, h:h + 1])
                chain(ins)
            rstd(flat(gst[:, :]), 256).then_inc(sem("g_rstd"), 1)
            act.wait_ge(sem("t_free"), 1)
            for w, c in enumerate(("gm", "gg")):
                for n in range(2):
                    pump(f"{c}{n}")
                    for t in range(NT):
                        copy_out(f"{c}{n}", SG[:, w, t, 512 * n:512 * n + 512], t, ACT.Sigmoid)
                    if (w, n) == (0, 0):
                        split_hi("ym", range(4))
                    if (w, n) == (1, 0):
                        split_hi("yg", range(8), lambda k: gain("gout", k % 2))
            for n in range(2):
                pump(f"bg{n}")
            split_hi("mix", range(8))
            pump("wo1")
            norm_stats(1, lambda t: acc_done(act, "wo1", t))
            split_hi("n2", range(8), lambda k: gain("norm2", k))
            for n in range(9):
                if n < 8:
                    pump(f"up{n}")
                    for t in range(NT):
                        acc_wait(act, f"up{n}", t)
                        act.activation(RL[:, n % 2, t], acc_of(f"up{n}", t), ACT.Relu).then_inc(sem("relu"), 1)
                if n >= 1:
                    split_hi("u", range(4 * n - 4, 4 * n))
            pump("dn0")
            pump("dn1")
            if STAGES >= 2:
                def post_norm(c, i, YB):
                    for n in range(2):
                        pump(f"{c}{n}")
                        for t in range(NT):
                            copy_out(f"{c}{n}", YB[:, t, 512 * n:512 * n + 512], t)
                    for t in range(NT):
                        for n in range(2):
                            acc_done(act, f"{c}{n}", t)
                        chain(act.activation(junk[:, :], YB[:, t], ACT.Square, accum_out=ystat[:, i, t:t + 1]))
                    rstd(ystat[:, i], D).then_inc(sem("y_rstd"), 1)

                def dn_done(t):
                    for n in range(2):
                        acc_done(act, f"dn{n}", t)

                norm_stats(2, dn_done)
                split_hi("en", range(8), lambda k: gain("epre", k))
                pump("eg")
                pump("ea0")
                for t in range(NT):
                    copy_out("ea0", AV[:, t, 0:512], t)
                aux_wait(act, ("gat", 1))
                chain(act.activation(flat(RX), bank(("gat", 1))[0:4, :], ACT.Abs))
                chain(act.activation(flat(RX), flat(RX), ACT.Exp, scale=-1.0))
                act.activation(flat(RX), flat(RX), ACT.Ln, bias=epsc[0:4, 2:3]).then_inc(sem("eg_ln"), 1)
                pump("eb0")
                for t in range(NT):
                    copy_out("eb0", ETMP[:, t], t, ACT.Sigmoid)
                pump("ea1")
                for t in range(NT):
                    copy_out("ea1", AV[:, t, 512:1024], t)

                def by_channel(j):
                    aux_wait(act, ("uT", j))
                    aux_free(act.activation(EU[:, 2 * j:2 * j + 2, 15:15 + TOK], halves(("uT", j)), ACT.Copy), ("uT", j))

                by_channel(0)
                by_channel(1)
                pump("eb1")
                for t in range(NT):
                    act.wait_ge(sem("u_gated"), t + 1)
                    copy_out("eb1", ETMP[:, t], t, ACT.Sigmoid)
                aux_done(act, ("mcol",))
                act.activation(flat(mcol[:, 1]), flat(mcol[:, 1]), ACT.Exp, scale=-1.0).then_inc(sem("clamp"), 1)
                for h in range(4):
                    aux_done(act, ("mb", h))
                    act.activation(flat(DW[:, h]), flat(DW[:, h]), ACT.Exp, scale=-1.0).then_inc(sem("dw_exp"), 1)
                pump("eq")
                for t in range(NT):
                    copy_out("eq", EQK[:, 0, t], t)
                by_channel(2)
                by_channel(3)
                pump("ek")
                for t in range(NT):
                    copy_out("ek", EQK[:, 1, t], t)
                for w in range(2):
                    if w == 1:
                        pump("ev0")
                        for t in range(NT):
                            copy_out("ev0", EV[:, t, 0:2, 0:256], t)
                    for j in range(2):
                        aux_wait(act, ("eqT", w, j))
                        aux_free(act.activation(EQT[:, w, 2 * j:2 * j + 2], halves(("eqT", w, j)), ACT.Copy,
                                                scale=(1.0, 128.0 ** -0.5)[w]), ("eqT", w, j))
                pump("ev1")
                for t in range(NT):
                    copy_out("ev1", EV[:, t, 2:4, 0:256], t)

                def numerators(h):
                    for t in range(NT):
                        act.wait_ge(sem("den"), 4 * h + t + 1)
                        aux_free(act.activation(HM[:, t, 256 * h:256 * h + 256], bank(("num", h, 0, t))[:, 0:256],
                                                ACT.Copy, scale=den[:, h, 0, t:t + 1]), ("num", h, 0, t))

                def out_gate(n):
                    pump(f"eo{n}")
                    for t in range(NT):
                        copy_out(f"eo{n}", SOB[:, t, 512 * n:512 * n + 512], t, ACT.Sigmoid)
                    pump(f"ew{n}")
                    for t in range(NT):
                        acc_wait(act, f"ew{n}", t)
                        act.wait_ge(sem("u_gated"), 4) if n == 0 else act.wait_ge(sem("etmp_used"), t + 1)
                        act.activation(ETMP[:, t], acc_of(f"ew{n}", t), ACT.Sigmoid).then_inc(sem("ew_sig"), 1)

                numerators(0)
                numerators(1)
                pump("eo0", 0)
                numerators(2)
                numerators(3)
                out_gate(0)
                out_gate(1)
                for t in range(NT):
                    aux_done(act, ("num", 3, 1, t))
                for h in range(4):
                    for t in range(NT):
                        aux_done(act, ("num", h, 1, t))
                        ins = act.activation(junk[:, 256 * (2 * (h % 2) + t):256 * (2 * (h % 2) + t) + 256],
                                             HM[:, t, 256 * h:256 * h + 256], ACT.Square, accum_out=est[:, t, h:h + 1])
                    chain(ins)
                rstd(flat(est[:, :]), 256).then_inc(sem("h_rstd"), 1)
                for n in range(2):
                    pump(f"ez{n}")
                    for t in range(NT):
                        acc_wait(act, f"ez{n}", t)
                        act.activation(SZA[:, t, 512 * n:512 * n + 512], acc_of(f"ez{n}", t), ACT.Sigmoid
                                       ).then_inc(sem("ez_sig"), 1)
                split_hi("eh", range(8), lambda k: gain("hn", k))
                for t in range(NT):
                    for i in range(2):
                        aux_wait(act, ("cvT", t, i))
                        aux_free(act.activation(AV[:, t, 512 * i:512 * i + 512], bank(("cvT", t, i))[:, :], ACT.Copy),
                                 ("cvT", t, i))
                act.wait_ge(sem("bn_done"), 1)
                rstd(bag[:, :, 1], 1, eps=1).then_inc(sem("bn_rstd"), 1)
                for t in range(NT):
                    act.wait_ge(sem("gn_out"), t + 1)
                    act.activation(XN[:, t], AV[:, t], ACT.Sigmoid).then_inc(sem("gn_sig"), 1)
                split_hi("ea", range(8))
                post_norm("ey", 0, AV)
            if STAGES >= 3:
                norm_stats(3, lambda t: act.wait_ge(sem("h_out"), t + 1))
                split_hi("on", range(8), lambda k: gain("opre", k))
                act.wait_ge(sem("angles"), 1)
                act.activation(trig[:, :].rearrange("p a t f -> p (a t f)"),
                               turns[:, :].rearrange("p a t f -> p (a t f)"), ACT.Sin).then_inc(sem("sines"), 1)
                for w, (c, n) in enumerate((("oq", 384), ("okv", 256))):
                    pump(c)
                    for t in range(NT):
                        acc_wait(act, c, t)
                        ins = act.activation(junk[:, 512 * t:512 * t + n], acc_of(c, t)[:, 0:n], ACT.Square,
                                             accum_out=cst[:, w, t:t + 1])
                    chain(ins)
                    rstd(cst[:, w], n).then_inc(sem("c_rstd"), 1)
                pump("of")
                for t in range(NT):
                    copy_out("of", FX[:, t], t)
                split_hi("cq", range(3), lambda k: gain("gq", k))
                split_hi("ckv", range(2), lambda k: gain("gkv", k))

                def gate(c, dst):
                    pump(c)
                    for t in range(NT):
                        acc_wait(act, c, t)
                        act.activation(dst(t), acc_of(c, t), ACT.Sigmoid).then_inc(sem("oz_sig"), 1)

                def keys(n):
                    pump(f"oc{n}")
                    for t in range(NT):
                        acc_wait(act, f"oc{n}", t)
                        act.activation(KN[:, t, 2 * n:2 * n + 2],
                                       acc_of(f"oc{n}", t).rearrange("p (h w d) -> p h w d", h=2, w=2)[:, :, 0],
                                       ACT.Copy).then_inc(sem("kn_copied"), 1)

                gate("oz0", lambda t: SZC[:, t, 0:512])
                for g in range(4):
                    aux_wait(act, ("dft", g))
                    aux_free(act.activation(ZT[:, 512 * g:512 * g + 512], bank(("dft", g))[:, :], ACT.Copy), ("dft", g))
                keys(0)
                keys(1)
                split_hi("fr", range(4))
                keys(2)
                keys(3)
                gate("oz1", lambda t: SZC[:, t, 512:1024])
                for n in range(3):
                    pump(f"ou{n}")
                    for t in range(NT):
                        copy_out(f"ou{n}", QF[:, t, 512 * n:512 * n + 512], t)
                gate("ozd", lambda t: YD[:, t])
                for j in range(4):
                    aux_wait(act, ("qnT", j))
                    aux_free(act.activation(QNT[:, 2 * j:2 * j + 2], halves(("qnT", j)), ACT.Copy, scale=192.0 ** -0.5),
                             ("qnT", j))
                for j in range(2):
                    aux_wait(act, ("qrT", j))
                    aux_free(act.activation(QRT[:, 2 * j:2 * j + 2], halves(("qrT", j)), ACT.Copy, scale=192.0 ** -0.5),
                             ("qrT", j))
                pump("ofd")

                def exponentials(h):
                    aux_wait(act, ("os", h))
                    act.wait_ge(sem("o_max"), h + 1)
                    for t in range(NT):
                        ins = act.activation(OP[h % 2][:, t], halves(("os", h))[:, t], ACT.Exp, bias=omx[:, h, t:t + 1],
                                             accum_out=osum[:, h, t:t + 1])
                    aux_free(ins, ("os", h))

                def turned(h):
                    aux_wait(act, ("opt", h))
                    aux_free(act.activation(flat(OPT[h % 3]), bank(("opt", h))[:, :], ACT.Copy), ("opt", h))

                for h in range(8):
                    exponentials(h)
                    if h >= 1:
                        turned(h - 1)
                turned(7)
                split_hi("yd", range(4))
                split_hi("yc", range(8))
                post_norm("oy", 1, YO)

        @block.vector
        def _(dve):
            chain = Chain(dve, "dve_chain")
            at = [0]

            def pump(c, ahead=SPLIT - 1):
                last = min(CH[CI[c]]["units"][-1] + ahead, len(UN) - 1)
                while at[0] <= last:
                    u = at[0]
                    dve.wait_ge(sem("hi_done"), u + 1)
                    dve.tensor_tensor(w_view(wlo[u % SPLIT], u), w_view(raw[u % RAW], u),
                                      w_view(whi[u % SPLIT], u).bitcast(F32), ALU.subtract).then_inc(sem("lo_done"), 1)
                    at[0] += 1

            def split_lo(name, ks, g=None):
                for j in range(ks[0] // 2, (ks[-1] + 2) // 2):
                    key = ("tr", name, j)
                    aux_wait(dve, key)
                    dve.wait_ge(sem("hi_split"), SPLITS[key] + 1)
                    for i in range(min(2, ks[-1] + 1 - 2 * j)):
                        hi, lo, _ = act_tile(name, 2 * j + i)
                        if g is None:
                            ins = dve.tensor_tensor(lo, halves(key)[:, i], hi.bitcast(F32), ALU.subtract)
                        else:
                            ins = dve.scalar_tensor_tensor(out=lo, in0=halves(key)[:, i], scalar=g(2 * j + i),
                                                           in1=hi.bitcast(F32), op0=ALU.mult, op1=ALU.subtract)
                    aux_free(ins, key)

            def normed(i):
                dve.wait_ge(sem("rstd"), i + 1)
                for t in range(NT):
                    dve.tensor_scalar(XN[:, t], H[:, t], stat[:, 2 * i + t:2 * i + t + 1], None, ALU.mult
                                      ).then_inc(sem("xn"), 1)

            def add_to_h(c, n, t):
                acc_wait(dve, c, t)
                acc_free(dve.tensor_tensor(H[:, t, 512 * n:512 * n + 512], acc_of(c, t),
                                           H[:, t, 512 * n:512 * n + 512], ALU.add), c)

            dve.memset(epsc[:, 0:1], 1e-6)
            dve.memset(epsc[:, 1:2], 1e-5)
            dve.memset(epsc[:, 2:3], 1.0).then_inc(sem("consts"), 1)
            chain(dve.memset(rmask[:, :], 1.0))
            chain(dve.memset(rmask[:, :].rearrange("p (c e) -> p c e", e=64)[:, :, 0:1], 0.0))
            aux_wait(dve, ("vec",))
            aux_free(dve.tensor_copy(vec[:, :], bank(("vec",))[:, 0:P]), ("vec",))
            for i in range(8):
                aux_wait(dve, ("bias", i))
                if i >= 2:
                    dve.wait_ge(sem("skew_out"), 16 * (i - 1))
                if i == 0:
                    dve.wait_ge(sem("rstd"), 1)
                aux_free(dve.tensor_copy(bias_w[i % 2], bank(("bias", i))[:, :]), ("bias", i))
                if i == 1:
                    normed(0)
            pump("mq", -1)
            split_lo("n1", range(8), lambda k: gain("norm1", k))
            for w, c in enumerate(("mq", "mk")):
                pump(c)
                for t in range(NT):
                    dve.wait_ge(sem("q_square"), 2 * w + t + 1)
                    dve.tensor_reduce(qst[:, w, t], QKN[:, w, t].rearrange("p (h d) -> p h d", h=8), AX.X, ALU.add
                                      ).then_inc(sem("q_sum"), 1)
                dve.wait_ge(sem("q_rstd"), w + 1)
                for t in range(NT):
                    acc_free(dve.tensor_tensor(QKN[:, w, t].rearrange("p (h d) -> p h d", h=8),
                                               acc_of(c, t).rearrange("p (h d) -> p h d", h=8),
                                               qst[:, w, t].unsqueeze(2).to_broadcast([P, 8, 64]), ALU.mult), c)
            pump("mv")
            for w in range(2):
                for j in range(2):
                    key = ("qkT", w, j)
                    aux_wait(dve, key)
                    aux_free(dve.tensor_scalar(QKT[:, w, 2 * j:2 * j + 2], halves(key), gain(("mq", "mk")[w], 0),
                                               (0.125, 1.0)[w], ALU.mult, ALU.mult), key)
            pump("gq")
            dve.wait_ge(sem("bias_in"), 16 * 16)
            for p in range(2):
                key = ("qk0", p)
                aux_wait(dve, key)
                aux_free(dve.tensor_tensor(P0[:, 4 * p:4 * p + 4], bank(key)[:, :].rearrange("p (h s) -> p h s", h=4),
                                           B0[:, 4 * p:4 * p + 4], ALU.add), key)
            aux_done(dve, ("qk0", 1))
            aux_done(dve, ("qk0", 0))
            dve.tensor_reduce(pst[:, 0, 0], P0, AX.X, ALU.max, negate=True).then_inc(sem("p_max"), 1)
            for i in range(2):
                for p in range(2):
                    key = ("qk1", p, i)
                    hs = slice(4 * p + 2 * i, 4 * p + 2 * i + 2)
                    aux_wait(dve, key)
                    aux_free(dve.tensor_tensor(P1[:, hs], halves(key), B1[:, hs], ALU.add), key)
            for i in range(2):
                for p in range(2):
                    aux_done(dve, ("qk1", p, i))
            dve.tensor_reduce(pst[:, 0, 1], P1, AX.X, ALU.max, negate=True).then_inc(sem("p_max"), 1)
            pump("gk")
            for j in range(2):
                dve.wait_ge(sem("gz_abs"), j + 1)
                for i in range(2):
                    ins = dve.tensor_scalar(T2[:, 2 * j + i], halves(("gz", j))[:, i], gain("gbias", 2 * j + i), 0.0,
                                            ALU.add, ALU.min)
                aux_free(ins, ("gz", j))
            for j in range(2):
                aux_done(dve, ("gz", j))
            dve.wait_ge(sem("gz_ln"), 1)
            chain(dve.tensor_tensor(T2, T2, T1, ALU.subtract))
            dve.tensor_tensor_scan(flat(T3), rmask[:, :], flat(T2), 0.0, ALU.mult, ALU.add).then_inc(sem("g_cum"), 1)
            dve.wait_ge(sem("g_cum"), 1)
            b3 = flat(T3).rearrange("p (c e) -> p c e", e=64)
            dve.tensor_tensor(flat(T2).rearrange("p (c e) -> p c e", e=64), b3[:, :, 63:64].to_broadcast([P, 16, 64]),
                              b3, ALU.subtract).then_inc(sem("g_rest"), 1)
            pump("gv0")
            dve.wait_ge(sem("p_exp"), 2)
            dve.reciprocal(flat(pst[:, 2]), flat(pst[:, 1])).then_inc(sem("p_recip"), 1)
            dve.wait_ge(sem("g_exp"), 1)
            chain(dve.tensor_copy(edl[:, :, :], T1.rearrange("p h (j e) -> p h j e", e=64)[:, :, :, 63]))
            for j in range(2):
                hs = slice(2 * j, 2 * j + 2)
                aux_wait(dve, ("gqT", j))
                aux_free(dve.scalar_tensor_tensor(out=QD[:, hs], in0=halves(("gqT", j)), scalar=128.0 ** -0.5,
                                                  in1=T1[:, hs], op0=ALU.mult, op1=ALU.mult), ("gqT", j))
            dve.wait_ge(sem("g_exp"), 2)
            for j in range(2):
                hs = slice(2 * j, 2 * j + 2)
                aux_wait(dve, ("gkT", j))
                dve.tensor_tensor(KI[:, hs], halves(("gkT", j)), T4[:, hs], ALU.mult)
                aux_free(dve.tensor_tensor(KD[:, hs], halves(("gkT", j)), T2[:, hs], ALU.mult), ("gkT", j))
            aux_done(dve, ("gkT", 1))
            dve.memset(epsc[:, 3:4], 0.0).then_inc(sem("t_free"), 1)
            pump("gv1")
            dve.wait_ge(sem("p_recip"), 1)
            for t in range(NT):
                aux_wait(dve, ("pv", t))
                r = pst[:, 2, t].rearrange("p (a h) -> p h a", a=2).unsqueeze(3).to_broadcast([P, 4, 2, 64])
                aux_free(dve.tensor_tensor(YM[:, t].rearrange("p (h a d) -> p h a d", a=2, d=64),
                                           bank(("pv", t))[:, :].rearrange("p (h a d) -> p h a d", a=2, d=64),
                                           r, ALU.mult), ("pv", t))
            pump("go0")
            for t in range(NT):
                dve.wait_ge(sem("go_sig"), t + 1)
                acc_free(dve.tensor_tensor(SGO[:, t, 0:512], SGO[:, t, 0:512], acc_of("go0", t), ALU.mult), "go0")
            for j in range(3):
                for i in range(2):
                    key = ("kv", j, i)
                    aux_wait(dve, key)
                    if j == 0:
                        ins = dve.tensor_copy(ST[0][:, 2 * i:2 * i + 2], halves(key))
                    else:
                        aux_done(dve, ("kv", j - 1, i))
                        for h in (2 * i, 2 * i + 1):
                            ins = dve.scalar_tensor_tensor(out=ST[j][:, h], in0=ST[j - 1][:, h], scalar=edl[:, h, j:j + 1],
                                                           in1=halves(key)[:, h - 2 * i], op0=ALU.mult, op1=ALU.add)
                    aux_free(ins, key)
            pump("go1")
            for t in range(NT):
                dve.wait_ge(sem("go_sig"), 2 + t + 1)
                acc_free(dve.tensor_tensor(SGO[:, t, 512:1024], SGO[:, t, 512:1024], acc_of("go1", t), ALU.mult), "go1")
            for t in range(NT):
                acc_done(dve, "go1", t)
            dve.wait_ge(sem("g_rstd"), 1)
            for t in range(NT):
                for h in range(4):
                    hs = slice(256 * h, 256 * h + 256)
                    ins = dve.scalar_tensor_tensor(out=OG[:, t, hs], in0=OG[:, t, hs], scalar=gst[:, t, h:h + 1],
                                                   in1=SGO[:, t, hs], op0=ALU.mult, op1=ALU.mult)
            ins.then_inc(sem("yg_ready"), 1)
            pump("gm0")
            split_lo("ym", range(4))
            pump("gm1")
            pump("gg0")
            split_lo("yg", range(8), lambda k: gain("gout", k % 2))
            pump("gg1")
            for n in range(2):
                cs = slice(512 * n, 512 * n + 512)
                pump(f"bm{n}")
                for t in range(NT):
                    acc_done(dve, f"gm{n}", t)
                    acc_wait(dve, f"bm{n}", t)
                    acc_free(dve.tensor_tensor(MX[:, t, cs], acc_of(f"bm{n}", t), SG[:, 0, t, cs], ALU.mult), f"bm{n}")
                pump(f"bg{n}")
                for t in range(NT):
                    acc_done(dve, f"gg{n}", t)
                    acc_wait(dve, f"bg{n}", t)
                    acc_free(dve.tensor_tensor(MTMP, acc_of(f"bg{n}", t), SG[:, 1, t, cs], ALU.mult), f"bg{n}")
                    acc_done(dve, f"bg{n}", t)
                    acc_done(dve, f"bm{n}", t)
                    chain2 = dve.tensor_tensor(MX[:, t, cs], MX[:, t, cs], MTMP, ALU.add)
                    chain2.then_inc(sem("mixed"), 1)
                    dve.wait_ge(sem("mixed"), 2 * n + t + 1)
            split_lo("mix", range(8))
            for n in range(2):
                pump(f"wo{n}")
                for t in range(NT):
                    add_to_h(f"wo{n}", n, t)
            normed(1)
            split_lo("n2", range(8), lambda k: gain("norm2", k))
            for n in range(9):
                if n < 8:
                    pump(f"up{n}")
                    for t in range(NT):
                        dve.wait_ge(sem("relu"), 2 * n + t + 1)
                        acc_free(dve.scalar_tensor_tensor(out=RL[:, n % 2, t], in0=acc_of(f"up{n}", t), scalar=0.0,
                                                          in1=RL[:, n % 2, t], op0=ALU.max, op1=ALU.mult), f"up{n}")
                if n >= 1:
                    split_lo("u", range(4 * n - 4, 4 * n))
            for n in range(2):
                pump(f"dn{n}")
                for t in range(NT):
                    add_to_h(f"dn{n}", n, t)
            if STAGES >= 2:
                normed(2)
                chain(dve.memset(EU[:, :, :], 0.0))
                dve.memset(rone[:, 0], 1.0)
                dve.memset(rone[:, 1], 0.0)
                chain(dve.memset(EV[:, :, :, 256:257], 1.0))
                dve.memset(epsc[:, 3:4], 0.0).then_inc(sem("even_consts"), 1)
                split_lo("en", range(8), lambda k: gain("epre", k))
                pump("eg")
                dve.wait_ge(sem("gbias_in"), 16)
                for t in range(NT):
                    acc_wait(dve, "eg", t)
                    acc_free(dve.tensor_tensor(gates[:, t].rearrange("p k d h -> p d k h"),
                                               acc_of("eg", t).rearrange("p (d k h) -> p d k h", d=2, k=2),
                                               gbias[:, :].rearrange("p (d k h) -> p d k h", d=2, k=2), ALU.add), "eg")
                pump("ea0")
                dve.wait_ge(sem("eg_ln"), 1)
                ins = dve.tensor_scalar(flat(RF), bank(("gat", 1))[0:4, :], 0.0, None, ALU.min)
                aux_free(ins, ("gat", 1))
                aux_done(dve, ("gat", 1))
                chain(dve.tensor_tensor(flat(RF), flat(RF), flat(RX), ALU.subtract))
                dve.tensor_tensor_scan(RX[:, 0], rone[:, 0], RF[:, 0], 0.0, ALU.mult, ALU.add)
                chain(dve.tensor_tensor_scan(RX[:, 1, ::-1], rone[:, 0], RF[:, 1, ::-1], 0.0, ALU.mult, ALU.add))
                aux_wait(dve, ("gat", 0))
                aux_free(dve.tensor_tensor(flat(RG), bank(("gat", 0))[0:4, :], flat(RX), ALU.subtract), ("gat", 0))
                aux_done(dve, ("gat", 0))
                dve.tensor_tensor_scan(RM[:, 0], RG[:, 0], rone[:, 1], 0.0, ALU.max, ALU.add)
                chain(dve.tensor_tensor_scan(RM[:, 1, ::-1], RG[:, 1, ::-1], rone[:, 1], 0.0, ALU.max, ALU.add))
                dve.tensor_tensor(flat(RF), flat(RX), flat(RM), ALU.add).then_inc(sem("m_rows"), 1)
                aux_wait(dve, ("wcv",))
                aux_free(dve.tensor_copy(flat(wcv[:, :]), bank(("wcv",))[:, 0:256]), ("wcv",))
                aux_done(dve, ("wcv",))

                taps = [(g, k, c) for g in range(2) for k in range(31) for c in range(4)]
                tap_at = [0]
                conv_done = sem("conv")

                def conv(n):
                    for _ in range(4 * n):
                        i = tap_at[0]
                        if i == len(taps):
                            return
                        g, k, c = taps[i]
                        if i == 0 or i == 124:
                            aux_done(dve, ("uT", 2 * g))
                            aux_done(dve, ("uT", 2 * g + 1))
                        c += 4 * g
                        if k == 0:
                            ins = dve.tensor_scalar(CV[:, c], EU[:, c, 0:TOK], wcv[:, c, 0:1], gain("convb", c),
                                                    ALU.mult, ALU.add)
                        else:
                            dve.wait_ge(conv_done, i - 3)
                            ins = dve.scalar_tensor_tensor(out=CV[:, c], in0=EU[:, c, k:k + TOK],
                                                           scalar=wcv[:, c, k:k + 1], in1=CV[:, c],
                                                           op0=ALU.mult, op1=ALU.add)
                        ins.then_inc(conv_done, 1)
                        tap_at[0] += 1

                def gate_u(n):
                    for t in range(NT):
                        cs = slice(512 * n, 512 * n + 512)
                        acc_done(dve, f"ea{n}", t)
                        acc_done(dve, f"eb{n}", t)
                        dve.tensor_tensor(AV[:, t, cs], AV[:, t, cs], ETMP[:, t], ALU.mult).then_inc(sem("u_gated"), 1)

                pump("eb0")
                gate_u(0)
                pump("ea1")
                conv(2)
                pump("eb1")
                gate_u(1)
                aux_wait(dve, ("mcol",))
                aux_free(dve.tensor_copy(mcol[:, :].rearrange("p g d t h -> p (g d t h)"), bank(("mcol",))[:, 0:32]),
                         ("mcol",))
                aux_done(dve, ("mcol",))
                for h in range(4):
                    aux_wait(dve, ("mb", h))
                    for d, st, o, a, n in ((0, 0, 0, 0, 256), (0, 1, 256, 128, 128), (1, 0, 0, 0, 128),
                                           (1, 1, 128, 0, 256)):
                        ins = dve.tensor_scalar(DW[:, h, d, o:o + n], halves(("mb", h))[:, d, a:a + n],
                                                mcol[:, 0, d, st, h:h + 1], 0.0, ALU.subtract, ALU.max)
                    aux_free(ins, ("mb", h))
                conv(5)
                pump("eq")
                conv(7)
                pump("ek")
                conv(7)
                pump("ev0")
                conv(6)
                pump("ev1", 2)
                for h in range(4):
                    key = ("kq", h)
                    aux_wait(dve, key)
                    dve.wait_ge(sem("dw_masked"), 2 * h + 2)
                    for d, st, o, a, n in ((0, 0, 0, 0, 256), (0, 1, 256, 128, 128), (1, 0, 0, 0, 128),
                                           (1, 1, 128, 0, 256)):
                        ins = dve.tensor_tensor(DW[:, h, d, o:o + n], DW[:, h, d, o:o + n],
                                                halves(key)[:, st, a:a + n], ALU.mult)
                    aux_free(ins, key)
                pump("ev1")

                def denominators(h):
                    for d in range(2):
                        for t in range(NT):
                            key = ("num", h, d, t)
                            one = den[:, h, d, t:t + 1]
                            aux_wait(dve, key)
                            x = bank(key)[:, 256:257]
                            chain(dve.tensor_tensor(one, x, mcol[:, 1, d, t, h:h + 1], ALU.max))
                            chain(dve.scalar_tensor_tensor(out=one, in0=x, scalar=-1.0, in1=one, op0=ALU.mult, op1=ALU.max))
                            dve.reciprocal(one, one).then_inc(sem("den"), 1)
                    for t in range(NT):
                        dve.wait_ge(sem("den"), 4 * h + 3 + t)
                        aux_done(dve, ("num", h, 0, t))
                        hs = HM[:, t, 256 * h:256 * h + 256]
                        aux_free(dve.scalar_tensor_tensor(out=hs, in0=bank(("num", h, 1, t))[:, 0:256],
                                                          scalar=den[:, h, 1, t:t + 1], in1=hs,
                                                          op0=ALU.mult, op1=ALU.add), ("num", h, 1, t))

                dve.wait_ge(sem("clamp"), 1)
                denominators(0)
                denominators(1)
                conv(4)
                pump("eo0", 0)
                denominators(2)
                denominators(3)
                conv(4)

                def out_gate(n):
                    pump(f"eo{n}")
                    conv(8)
                    pump(f"ew{n}")
                    for t in range(NT):
                        cs = slice(512 * n, 512 * n + 512)
                        acc_done(dve, f"eo{n}", t)
                        dve.wait_ge(sem("ew_sig"), 2 * n + t + 1)
                        dve.tensor_tensor(SOB[:, t, cs], SOB[:, t, cs], ETMP[:, t], ALU.mult).then_inc(sem("etmp_used"), 1)
                        dve.wait_ge(sem("etmp_used"), 2 * n + t + 1)
                        acc_free(dve.tensor_tensor(SOB[:, t, cs], SOB[:, t, cs], acc_of(f"ew{n}", t), ALU.mult), f"ew{n}")
                    conv(8)

                out_gate(0)
                out_gate(1)
                conv(62)
                dve.wait_ge(sem("h_rstd"), 1)
                for t in range(NT):
                    acc_done(dve, "ew0", t)
                    acc_done(dve, "ew1", t)
                    for h in range(4):
                        hs = slice(256 * h, 256 * h + 256)
                        ins = dve.scalar_tensor_tensor(out=HM[:, t, hs], in0=HM[:, t, hs], scalar=est[:, t, h:h + 1],
                                                       in1=SOB[:, t, hs], op0=ALU.mult, op1=ALU.mult)
                ins.then_inc(sem("yh_ready"), 1)
                for n in range(2):
                    pump(f"ez{n}")
                    for t in range(NT):
                        cs = slice(512 * n, 512 * n + 512)
                        dve.wait_ge(sem("ez_sig"), 2 * n + t + 1)
                        acc_free(dve.tensor_tensor(SZA[:, t, cs], SZA[:, t, cs], acc_of(f"ez{n}", t), ALU.mult), f"ez{n}")
                split_lo("eh", range(8), lambda k: gain("hn", k))
                for t in range(NT):
                    for i in range(2):
                        aux_done(dve, ("cvT", t, i))
                        for g in range(4 * i, 4 * i + 4):
                            ins = dve.bn_stats(bst[:, 8 * t + g], AV[:, t, P * g:P * g + P])
                chain(ins)
                for g in range(16):
                    ins = dve.bn_aggr(bag[:, g], bst[:, g])
                ins.then_inc(sem("bn_done"), 1)
                dve.wait_ge(sem("bn_rstd"), 1)
                for t in range(NT):
                    for g in range(8):
                        v = AV[:, t, P * g:P * g + P]
                        ins = dve.tensor_scalar(v, v, bag[:, 8 * t + g, 0:1], bag[:, 8 * t + g, 1:2],
                                                ALU.subtract, ALU.mult)
                    chain(ins)
                    dve.wait_ge(sem("gn_in"), 32)
                    chain(dve.tensor_tensor(AV[:, t], AV[:, t], gng[:, :], ALU.mult))
                    dve.tensor_tensor(AV[:, t], AV[:, t], gnb[:, :], ALU.add).then_inc(sem("gn_out"), 1)
                for t in range(NT):
                    acc_done(dve, "ez0", t)
                    acc_done(dve, "ez1", t)
                    dve.wait_ge(sem("gn_sig"), t + 1)
                    chain(dve.tensor_tensor(AV[:, t], AV[:, t], XN[:, t], ALU.mult))
                    dve.tensor_tensor(AV[:, t], AV[:, t], SZA[:, t], ALU.mult).then_inc(sem("ya_ready"), 1)
                split_lo("ea", range(8))

                def add_normed(i, g, YB):
                    dve.wait_ge(sem("y_rstd"), i + 1)
                    dve.wait_ge(sem("post_in"), 16 * (i + 1))
                    for t in range(NT):
                        chain(dve.scalar_tensor_tensor(out=YB[:, t], in0=YB[:, t], scalar=ystat[:, i, t:t + 1], in1=g,
                                                       op0=ALU.mult, op1=ALU.mult))
                        dve.tensor_tensor(H[:, t], H[:, t], YB[:, t], ALU.add).then_inc(sem("h_out"), 1)

                pump("ey0")
                pump("ey1")
                add_normed(0, post_g, AV)
            if STAGES >= 3:
                normed(3)
                split_lo("on", range(8), lambda k: gain("opre", k))
                C1, C2, C3 = TWO_PI
                magic = 1.5 * 2.0 ** 23
                dve.wait_ge(sem("pos_in"), 32)
                chain(dve.tensor_copy(pos[:, :], pos_i[:, :]))
                for t in range(NT):
                    ins = dve.tensor_scalar(ang[:, t], invf[:, :], pos[:, t:t + 1], None, ALU.mult)
                chain(ins)
                for w in range(2):
                    k, a = flat(turns[:, w]), flat(ang[:, :])
                    chain(dve.tensor_scalar(k, a, 1.0 / (2 * math.pi), 0.25 * w, ALU.mult, ALU.add))
                    chain(dve.tensor_scalar(k, k, magic, magic, ALU.add, ALU.subtract))
                    u = flat(trig[:, w])
                    chain(dve.scalar_tensor_tensor(out=u, in0=k, scalar=-C1, in1=a, op0=ALU.mult, op1=ALU.add))
                    chain(dve.scalar_tensor_tensor(out=u, in0=k, scalar=-C2, in1=u, op0=ALU.mult, op1=ALU.add))
                    chain(dve.scalar_tensor_tensor(out=u, in0=k, scalar=-C3, in1=u, op0=ALU.mult, op1=ALU.add))
                    chain(dve.tensor_scalar(k, u, 0.5 * math.pi * w, 3.1415925, ALU.add, ALU.min))
                    ins = dve.tensor_scalar(k, k, -3.1415925, None, ALU.max)
                    if w == 0:
                        chain(ins)
                ins.then_inc(sem("angles"), 1)
                for w, (c, n, o) in enumerate((("oq", 384, 0), ("okv", 256, 384))):
                    pump(c)
                    dve.wait_ge(sem("c_rstd"), w + 1)
                    for t in range(NT):
                        if w == 1:
                            dve.tensor_copy(KR0[:, t], acc_of(c, t)[:, 256:320])
                        acc_free(dve.tensor_scalar(XN[:, t, o:o + n], acc_of(c, t)[:, 0:n], cst[:, w, t:t + 1], None,
                                                   ALU.mult), c)

                def rotate(dst, src, t, n):
                    x1, x2 = src[:, :, 0:32], src[:, :, 32:64]
                    sin = trig[:, 0, t].unsqueeze(1).to_broadcast([P, n, 32])
                    cos = trig[:, 1, t].unsqueeze(1).to_broadcast([P, n, 32])
                    a, b, c, d = [rt[:, i, 0:32 * n].rearrange("p (h f) -> p h f", h=n) for i in range(4)]
                    dve.tensor_tensor(a, x1, cos, ALU.mult)
                    dve.tensor_tensor(b, x2, sin, ALU.mult)
                    dve.tensor_tensor(c, x1, sin, ALU.mult)
                    chain(dve.tensor_tensor(d, x2, cos, ALU.mult))
                    dve.tensor_tensor(dst[:, :, 0:32], a, b, ALU.subtract)
                    chain(dve.tensor_tensor(dst[:, :, 32:64], c, d, ALU.add))

                dve.wait_ge(sem("sines"), 1)
                for t in range(NT):
                    acc_done(dve, "okv", t)
                    rotate(KR[:, t, 0:1], KR0[:, t].unsqueeze(1), t, 1)
                    ins = dve.tensor_copy(KR[:, t, 1], KR[:, t, 0])
                ins.then_inc(sem("kr_ready"), 1)
                pump("of")
                split_lo("cq", range(3), lambda k: gain("gq", k))
                split_lo("ckv", range(2), lambda k: gain("gkv", k))

                def gate(c, n, dst):
                    pump(c)
                    for t in range(NT):
                        dve.wait_ge(sem("oz_sig"), 2 * n + t + 1)
                        acc_free(dve.tensor_tensor(dst(t), dst(t), acc_of(c, t), ALU.mult), c)

                def values(n):
                    pump(f"oc{n}")
                    for t in range(NT):
                        dve.wait_ge(sem("kn_copied"), 2 * n + t + 1)
                        acc_free(dve.tensor_copy(OV[:, t, 2 * n:2 * n + 2],
                                                 acc_of(f"oc{n}", t).rearrange("p (h w d) -> p h w d", h=2, w=2)[:, :, 1]),
                                 f"oc{n}")

                def key_tiles(j):
                    aux_wait(dve, ("knT", j))
                    aux_free(dve.tensor_copy(KNT[:, 2 * j:2 * j + 2], halves(("knT", j))), ("knT", j))

                gate("oz0", 0, lambda t: SZC[:, t, 0:512])
                aux_wait(dve, ("krT",))
                aux_free(dve.tensor_copy(KRT[:, :], bank(("krT",))[:, 0:TOK]), ("krT",))
                values(0)
                values(1)
                split_lo("fr", range(4))
                values(2)
                values(3)
                key_tiles(0)
                key_tiles(1)
                gate("oz1", 1, lambda t: SZC[:, t, 512:1024])
                key_tiles(2)
                key_tiles(3)
                for n in range(3):
                    pump(f"ou{n}")
                for t in range(NT):
                    for n in range(3):
                        acc_done(dve, f"ou{n}", t)
                    q = QF[:, t].rearrange("p (h f) -> p h f", h=8)[:, :, 128:192]
                    rotate(QR[:, t].rearrange("p (h f) -> p h f", h=8), q, t, 8)
                dve.memset(epsc[:, 3:4], 0.0).then_inc(sem("qr_ready"), 1)
                gate("ozd", 2, lambda t: YD[:, t])
                pump("ofd", 4)
                for t in range(NT):
                    acc_done(dve, "ozd", t)
                    acc_wait(dve, "ofd", t)
                    acc_free(dve.tensor_tensor(YD[:, t], YD[:, t], acc_of("ofd", t), ALU.mult), "ofd")
                for t in range(NT):
                    acc_done(dve, "oz0", t)
                    acc_done(dve, "oz1", t)

                def heads_out(p):
                    key = ("opv", p)
                    aux_wait(dve, key)
                    for h in (2 * p, 2 * p + 1):
                        for t in range(NT):
                            b = bank(key)[:, :].rearrange("p (h t d) -> p h t d", h=2, t=2)[:, h % 2, t]
                            ins = dve.scalar_tensor_tensor(out=YC[:, t, P * h:P * h + P], in0=b,
                                                           scalar=orec[:, h, t:t + 1], in1=SZC[:, t, P * h:P * h + P],
                                                           op0=ALU.mult, op1=ALU.mult)
                    aux_free(ins, key)

                for h in range(8):
                    aux_wait(dve, ("os", h))
                    dve.tensor_reduce(omx[:, h], halves(("os", h)), AX.X, ALU.max, negate=True).then_inc(sem("o_max"), 1)
                    if h >= 1:
                        aux_done(dve, ("os", h - 1))
                        chain(dve.reciprocal(orec[:, h - 1], osum[:, h - 1]))
                    if h >= 3 and h % 2:
                        heads_out((h - 3) // 2)
                aux_done(dve, ("os", 7))
                chain(dve.reciprocal(orec[:, 7], osum[:, 7]))
                heads_out(3)
                split_lo("yd", range(4))
                split_lo("yc", range(8))
                pump("oy0")
                pump("oy1")
                add_normed(1, post2[:, :], YO)

        @block.tensor
        def _(pe):
            done = [0]

            def product(c):
                i, ch = CI[c], CH[CI[c]]
                assert i == done[0]
                done[0] += 1
                if i >= 2:
                    pe.wait_ge(sem(f"acc_free{i % 2}"), 2 * (i // 2))
                seen = None
                for u in ch["units"]:
                    _, k0, nk, _, nn = UN[u]
                    pe.wait_ge(sem("lo_done"), u + 1)
                    hi = w_view(whi[u % SPLIT], u).rearrange("p (k n) -> p k n", k=nk)
                    lo = w_view(wlo[u % SPLIT], u).rearrange("p (k n) -> p k n", k=nk)
                    for t in range(NT):
                        for k in range(nk):
                            ah, al, key = act_tile(ch["acts"], k0 + k)
                            if t == 0 and key != seen:
                                aux_done(pe, key)
                                seen = key
                            ts = slice(t * P, t * P + P)
                            first, last = k0 + k == 0, k0 + k == ch["kts"] - 1
                            pe.matmul(acc_of(c, t), ah[:, ts], hi[:, k], start=first, stop=False)
                            pe.matmul(acc_of(c, t), ah[:, ts], lo[:, k], start=False, stop=False)
                            ins = pe.matmul(acc_of(c, t), al[:, ts], hi[:, k], start=False, stop=last)
                        if t == 0 and u == ch["units"][-1]:
                            ins.then_inc(sem("tile0_done"), 1)
                        if t == 1:
                            ins.then_inc(sem("units_used"), 1)

            order = [0]

            def take(key):
                assert AUX[order[0]] == key, (AUX[order[0]], key)
                i = order[0]
                order[0] += 1
                if i >= 4:
                    pe.wait_ge(sem(f"aux_free{i % 4}"), i // 4)
                return aux[i % 4]

            def give(ins, key):
                ins.then_inc(sem(f"aux_ready{PLACE[key] % 4}"), 1)

            def turn(name, ks, src):
                for j in range(ks[0] // 2, (ks[-1] + 2) // 2):
                    key = ("tr", name, j)
                    b = take(key)
                    for i in range(min(2, ks[-1] + 1 - 2 * j)):
                        for t in range(NT):
                            ins = pe.transpose(b[:, TOK * i + P * t:TOK * i + P * t + P], src(2 * j + i, t), ident[:, :])
                    give(ins, key)

            def cols(buf):
                return lambda k, t: buf[:, t, P * k:P * k + P]

            pe.wait_ge(sem("ident"), 1)
            pe.wait_ge(sem("vec_in"), 16 * 14)
            b = take(("vec",))
            give(pe.transpose(b[:, 0:P], vec_in[:, :], ident[:, :]), ("vec",))
            pe.wait_ge(sem("t5_in"), 32)
            for i in range(8):
                h = 2 * (i % 4) + i // 4
                b = take(("bias", i))
                give(pe.matmul(b[:, :], t5x[:, h:h + 1].to_broadcast([33, P]), onehot, start=True, stop=True), ("bias", i))
                if i == 3:
                    pass
            pe.wait_ge(sem("xn"), 2)
            turn("n1", range(8), cols(XN))
            product("mq")
            product("mk")
            product("mv")
            for w, c in enumerate(("mq", "mk")):
                for t in range(NT):
                    acc_done(pe, c, t)
                for j in range(2):
                    b = take(("qkT", w, j))
                    for i in range(2):
                        for t in range(NT):
                            k = 2 * j + i
                            ins = pe.transpose(b[:, TOK * i + P * t:TOK * i + P * t + P],
                                               QKN[:, w, t, P * k:P * k + P], ident[:, :])
                    give(ins, ("qkT", w, j))
            product("glow")
            product("gq")
            for t in range(NT):
                acc_done(pe, "glow", t)
            b = take(("glT",))
            for t in range(NT):
                ins = pe.transpose(b[0:16, P * t:P * t + P], gl[:, t], ident[:, :])
            give(ins, ("glT",))
            for w in range(2):
                for j in range(2):
                    aux_done(pe, ("qkT", w, j))

            def logits(out_ap, p, hp, t, ns):
                rows = slice(64 * p, 64 * p + 64)
                return pe.matmul(out_ap, QKT[rows, 0, hp, P * t:P * t + P], QKT[rows, 1, hp, 0:ns],
                                 start=True, stop=True)

            for p in range(2):
                b = take(("qk0", p))
                for hp in range(4):
                    ins = logits(b[:, P * hp:P * hp + P], p, hp, 0, P)
                give(ins, ("qk0", p))
            for i in range(2):
                for p in range(2):
                    b = take(("qk1", p, i))
                    for r in range(2):
                        ins = logits(b[:, TOK * r:TOK * r + TOK], p, 2 * i + r, 1, TOK)
                    give(ins, ("qk1", p, i))
            product("gk")
            aux_done(pe, ("glT",))
            pe.wait_ge(sem("gup_in"), 16)
            for j in range(2):
                b = take(("gz", j))
                for i in range(2):
                    h = 2 * j + i
                    ins = pe.matmul(b[:, TOK * i:TOK * i + TOK], gup[:, P * h:P * h + P], glT[:, :], start=True, stop=True)
                give(ins, ("gz", j))
            product("gv0")
            for i in range(6):
                b = take(("pt", i))
                pe.wait_ge(sem("p_exp"), 1 if i < 2 else 2)
                for r in range(4):
                    src = P0[:, 4 * i + r] if i < 2 else P1[:, 2 * (i - 2) + r // 2, P * (r % 2):P * (r % 2) + P]
                    ins = pe.transpose(b[:, P * r:P * r + P], src, ident[:, :])
                give(ins, ("pt", i))
            for w, c in enumerate(("gq", "gk")):
                for t in range(NT):
                    acc_done(pe, c, t)
                for j in range(2):
                    b = take((c + "T", j))
                    for i in range(2):
                        for t in range(NT):
                            k = 2 * j + i
                            ins = pe.transpose(b[:, TOK * i + P * t:TOK * i + P * t + P],
                                               GQK[:, w, t, P * k:P * k + P], ident[:, :])
                    give(ins, (c + "T", j))
            product("gv1")
            for i in range(6):
                aux_done(pe, ("pt", i))
            for t in range(NT):
                acc_done(pe, "mv", t)
                b = take(("pv", t))
                for q in range(8):
                    h = 2 * (q % 4) + q // 4
                    for s in range(t + 1):
                        blk = PT[:, q] if t == 0 else PT[:, 8 + 2 * q + s]
                        ins = pe.matmul(b[:, 64 * h:64 * h + 64], blk, MV[:, s, 64 * h:64 * h + 64],
                                        start=s == 0, stop=s == t)
                give(ins, ("pv", t))
            for key in (("gqT", 0), ("gqT", 1), ("gkT", 0), ("gkT", 1)):
                aux_done(pe, key)
            for t in range(NT):
                b = take(("kdt", t))
                for h in range(4):
                    ins = pe.transpose(b[:, P * h:P * h + P], KD[:, h, P * t:P * t + P], ident[:, :])
                give(ins, ("kdt", t))
            for t in range(NT):
                b = take(("ga", t))
                for h in range(4):
                    ins = pe.matmul(b[:, P * h:P * h + P], KI[:, h, P * t:P * t + P], QD[:, h, P * t:P * t + P],
                                    start=True, stop=True)
                give(ins, ("ga", t))
            product("go0")
            for n in range(2):
                for t in range(NT):
                    acc_done(pe, f"gv{n}", t)
            for t in range(NT):
                aux_done(pe, ("kdt", t))
            for j in range(3):
                rows = slice(64 * (j % 2), 64 * (j % 2) + 64)
                for i in range(2):
                    b = take(("kv", j, i))
                    for h in (2 * i, 2 * i + 1):
                        ins = pe.matmul(b[:, TOK * (h % 2):TOK * (h % 2) + TOK], KDT[rows, j // 2, h],
                                        GV[rows, j // 2, 256 * h:256 * h + 256], start=True, stop=True)
                    give(ins, ("kv", j, i))
            product("go1")
            for j in range(3):
                for i in range(2):
                    aux_done(pe, ("kv", j, i))
            for t in range(NT):
                pe.wait_ge(sem("ga_masked"), t + 1)
                for i in range(2):
                    b = take(("o", t, i))
                    for h in (2 * i, 2 * i + 1):
                        cs = slice(TOK * (h % 2), TOK * (h % 2) + TOK)
                        ins = pe.matmul(b[:, cs], GA[:, t, h], GV[:, t, 256 * h:256 * h + 256], start=True, stop=False,
                                        skip_group_check=True)
                        for j in (2 * t, 2 * t + 1):
                            if j == 0:
                                continue
                            r0 = 64 * (j % 2)
                            ins = pe.matmul(b[r0:r0 + 64, cs], QD[:, h, 64 * j:64 * j + 64], ST[j - 1][:, h],
                                            start=False, stop=True, skip_group_check=True)
                    give(ins, ("o", t, i))
            product("gm0")
            for t in range(NT):
                aux_done(pe, ("pv", t))
            turn("ym", range(4), cols(YM))
            product("gm1")
            product("gg0")
            pe.wait_ge(sem("yg_ready"), 1)
            turn("yg", range(8), cols(OG))
            product("gg1")
            for n in range(2):
                product(f"bm{n}")
                product(f"bg{n}")
            pe.wait_ge(sem("mixed"), 4)
            turn("mix", range(8), cols(MX))
            product("wo0")
            product("wo1")
            pe.wait_ge(sem("xn"), 4)
            turn("n2", range(8), cols(XN))
            for n in range(9):
                if n < 8:
                    product(f"up{n}")
                if n >= 1:
                    for t in range(NT):
                        acc_done(pe, f"up{n - 1}", t)
                    turn("u", range(4 * n - 4, 4 * n),
                         lambda k, t: RL[:, (k // 4) % 2, t, P * (k % 4):P * (k % 4) + P])
            product("dn0")
            product("dn1")
            if STAGES >= 2:
                pe.wait_ge(sem("xn"), 6)
                turn("en", range(8), cols(XN))
                product("eg")
                product("ea0")
                for t in range(NT):
                    acc_done(pe, "eg", t)
                for k in range(2):
                    b = take(("gat", k))
                    for d in range(2):
                        for t in range(NT):
                            ins = pe.transpose(b[0:4, TOK * d + P * t:TOK * d + P * t + P], gates[:, t, k, d], ident[:, :])
                    give(ins, ("gat", k))
                product("eb0")
                pe.wait_ge(sem("wcv_in"), 16)
                b = take(("wcv",))
                for c in range(8):
                    ins = pe.transpose(b[:, 32 * c:32 * c + 31], wcv_in[:, P * c:P * c + P], ident[0:31, 0:31])
                give(ins, ("wcv",))
                product("ea1")

                def by_channel(j):
                    b = take(("uT", j))
                    for i in range(2):
                        for t in range(NT):
                            c = 2 * j + i
                            ins = pe.transpose(b[:, TOK * i + P * t:TOK * i + P * t + P], AV[:, t, P * c:P * c + P],
                                               ident[:, :])
                    give(ins, ("uT", j))

                pe.wait_ge(sem("u_gated"), 2)
                pe.wait_ge(sem("even_consts"), 1)
                by_channel(0)
                by_channel(1)
                product("eb1")
                pe.wait_ge(sem("m_rows"), 1)
                b = take(("mcol",))
                for g, R in enumerate((RG, RF)):
                    for d in range(2):
                        for t in range(NT):
                            o = 4 * (4 * g + 2 * d + t)
                            ins = pe.transpose(b[:, o:o + 4], R[:, d, P * t:P * t + P], ident[0:4, 0:4])
                give(ins, ("mcol",))
                for h in range(4):
                    b = take(("mb", h))
                    give(pe.matmul(b[:, :], ident[0:4, h:h + 1].to_broadcast([4, P]), flat(RM), start=True, stop=True),
                         ("mb", h))
                product("eq")
                pe.wait_ge(sem("u_gated"), 4)
                by_channel(2)
                by_channel(3)
                product("ek")
                for w, c in enumerate(("eq", "ek")):
                    for t in range(NT):
                        acc_done(pe, c, t)
                    for j in range(2):
                        b = take(("eqT", w, j))
                        for i in range(2):
                            for t in range(NT):
                                k = 2 * j + i
                                ins = pe.transpose(b[:, TOK * i + P * t:TOK * i + P * t + P],
                                                   EQK[:, w, t, P * k:P * k + P], ident[:, :])
                        give(ins, ("eqT", w, j))
                    if w == 0:
                        product("ev0")
                for w in range(2):
                    for j in range(2):
                        aux_done(pe, ("eqT", w, j))
                for h in range(4):
                    b = take(("kq", h))
                    for st in range(NT):
                        ins = pe.matmul(b[:, TOK * st:TOK * st + TOK], EQT[:, 1, h, P * st:P * st + P], EQT[:, 0, h],
                                        start=True, stop=True)
                    give(ins, ("kq", h))
                product("ev1")

                def numerators(h):
                    for n in range(2):
                        for t in range(NT):
                            acc_done(pe, f"ev{n}", t)
                    aux_done(pe, ("kq", h))
                    for d in range(2):
                        for t in range(NT):
                            b = take(("num", h, d, t))
                            src = {(0, 0): [(0, 0)], (0, 1): [(1, 0), (2, 1)], (1, 0): [(0, 0), (1, 1)],
                                   (1, 1): [(2, 1)]}[d, t]
                            for i, (blk, st) in enumerate(src):
                                ins = pe.matmul(b[:, 0:257], DW[:, h, d, P * blk:P * blk + P], EV[:, st, h, 0:257],
                                                start=i == 0, stop=i == len(src) - 1)
                            give(ins, ("num", h, d, t))

                numerators(0)
                numerators(1)
                product("eo0")
                numerators(2)
                numerators(3)
                product("ew0")
                product("eo1")
                product("ew1")
                product("ez0")
                product("ez1")
                pe.wait_ge(sem("yh_ready"), 1)
                turn("eh", range(8), cols(HM))
                pe.wait_ge(sem("conv"), 248)
                for t in range(NT):
                    for i in range(2):
                        b = take(("cvT", t, i))
                        for c in range(4):
                            ins = pe.transpose(b[:, P * c:P * c + P], CV[:, 4 * i + c, P * t:P * t + P], ident[:, :])
                        give(ins, ("cvT", t, i))
                pe.wait_ge(sem("ya_ready"), 2)
                turn("ea", range(8), cols(AV))
                product("ey0")
                product("ey1")
            if STAGES >= 3:
                def turn_pairs(key, src):
                    b = take(key)
                    for i in range(2):
                        for t in range(NT):
                            ins = pe.transpose(b[:, TOK * i + P * t:TOK * i + P * t + P], src(i, t), ident[:, :])
                    give(ins, key)

                pe.wait_ge(sem("xn"), 8)
                turn("on", range(8), cols(XN))
                product("oq")
                product("okv")
                product("of")
                for c in ("oq", "okv"):
                    for t in range(NT):
                        acc_done(pe, c, t)
                turn("cq", range(3), cols(XN))
                turn("ckv", range(2), lambda k, t: XN[:, t, 384 + P * k:384 + P * k + P])
                product("oz0")
                pe.wait_ge(sem("kr_ready"), 1)
                b = take(("krT",))
                for t in range(NT):
                    ins = pe.transpose(b[:, P * t:P * t + P], KR[:, t].rearrange("p a f -> p (a f)"), ident[:, :])
                give(ins, ("krT",))
                pe.wait_ge(sem("dft_in"), 32)
                for t in range(NT):
                    acc_done(pe, "of", t)
                for g in range(4):
                    b = take(("dft", g))
                    for t in range(NT):
                        ins = pe.matmul(b[:, :], FX[:, t, P * g:P * g + P], dft_s[:, t], start=t == 0, stop=t == 1)
                    give(ins, ("dft", g))
                product("oc0")
                product("oc1")
                for g in range(4):
                    aux_done(pe, ("dft", g))
                for j in range(2):
                    key = ("tr", "fr", j)
                    b = take(key)
                    for i in range(2):
                        for w in range(2):
                            o = 512 * (2 * j + i) + TOK * w
                            ins = pe.matmul(b[:, TOK * i:TOK * i + TOK], dft_c[:, w], ZT[:, o:o + TOK],
                                            start=w == 0, stop=w == 1)
                    give(ins, key)
                product("oc2")
                product("oc3")
                for j in range(4):
                    if j == 2:
                        product("oz1")
                    for t in range(NT):
                        acc_done(pe, f"oc{j}", t)
                    turn_pairs(("knT", j), lambda i, t: KN[:, t, 2 * j + i])
                for n in range(3):
                    product(f"ou{n}")
                product("ozd")
                for n in range(3):
                    for t in range(NT):
                        acc_done(pe, f"ou{n}", t)
                for j in range(4):
                    turn_pairs(("qnT", j), lambda i, t: QF[:, t, 192 * (2 * j + i):192 * (2 * j + i) + P])
                pe.wait_ge(sem("qr_ready"), 1)
                for j in range(2):
                    turn_pairs(("qrT", j), lambda i, t: QR[:, t, P * (2 * j + i):P * (2 * j + i) + P])
                product("ofd")
                for key in [("knT", j) for j in range(4)] + [("qnT", j) for j in range(4)] + \
                        [("qrT", j) for j in range(2)] + [("krT",)]:
                    aux_done(pe, key)

                def turn_head(h):
                    b = take(("opt", h))
                    aux_done(pe, ("os", h))
                    for s in range(NT):
                        for t in range(NT):
                            ins = pe.transpose(b[:, TOK * s + P * t:TOK * s + P * t + P], OP[h % 2][:, t, P * s:P * s + P],
                                               ident[:, :])
                    give(ins, ("opt", h))

                def weigh(p):
                    b = take(("opv", p))
                    for h in (2 * p, 2 * p + 1):
                        aux_done(pe, ("opt", h))
                        for t in range(NT):
                            o = 256 * (h % 2) + P * t
                            for s in range(NT):
                                ins = pe.matmul(b[:, o:o + P], OPT[h % 3][:, s, P * t:P * t + P], OV[:, s, h],
                                                start=s == 0, stop=s == 1)
                    give(ins, ("opv", p))

                for h in range(8):
                    b = take(("os", h))
                    rows = slice(64 * (h % 2), 64 * (h % 2) + 64)
                    for t in range(NT):
                        o = TOK * t
                        pe.matmul(b[:, o:o + TOK], QNT[:, h, P * t:P * t + P], KNT[:, h], start=True, stop=False)
                        ins = pe.matmul(b[:, o:o + TOK], QRT[rows, h // 2, P * t:P * t + P], KRT[rows, :],
                                        start=False, stop=True)
                    give(ins, ("os", h))
                    if h >= 1:
                        turn_head(h - 1)
                    if h >= 3 and h % 2:
                        weigh((h - 3) // 2)
                turn_head(7)
                weigh(3)
                for t in range(NT):
                    acc_done(pe, "ofd", t)
                turn("yd", range(4), cols(YD))
                turn("yc", range(8), cols(YC))
                product("oy0")
                product("oy1")


SHAPES_OUT = (1, TOK, D)


def distance_buckets():
    import numpy as np
    hot = np.zeros((33, 512), np.float32)
    for j in range(512):
        d = 255 - j
        if d < 0:
            hot[32, j] = 1.0
            continue
        b = d
        if d >= 16:
            large = np.float32(np.log(np.float32(d) / np.float32(16.0))) / np.float32(math.log(128 / 16))
            b = min(31, 16 + int(np.float32(large * np.float32(16.0))))
        hot[b, j] = 1.0
    return hot


def constants():
    import numpy as np
    a = 2 * np.pi * (np.outer(np.arange(TOK), np.arange(TOK)) % TOK) / TOK
    b = 2 * np.pi * (np.outer(np.arange(P), np.arange(P)) % P) / P
    return {"onehot": distance_buckets(),
            "inv_freq": (10000.0 ** (-np.arange(0, 64, 2) / 64.0)).astype(np.float32),
            "dft_s": (np.concatenate([np.cos(a), -np.sin(a)], axis=1) / np.sqrt(TOK)).astype(np.float32),
            "dft_c": (np.stack([np.cos(b), np.sin(b)]) / np.sqrt(P)).astype(np.float32)}


def kernel(**inputs):
    import numpy as np
    import concourse.bacc as bacc
    from concourse.bass_utils import run_bass_kernel_spmd

    nc = bacc.Bacc("TRN2", target_bir_lowering=False, num_devices=1)
    arrays = {name: np.ascontiguousarray(a) for name, a in inputs.items()}
    arrays.update(constants())
    A = {name: nc.dram_tensor("in_" + name, a.shape, mybir.dt.from_np(a.dtype), kind="ExternalInput").ap()
         for name, a in arrays.items()}
    A["skew"] = nc.dram_tensor("skew", (8, P, 512), F32, kind="Internal").ap()
    out = nc.dram_tensor("out_h", SHAPES_OUT, F32, kind="ExternalOutput").ap()
    program(nc, A, out)
    r = run_bass_kernel_spmd(nc, [{"in_" + name: a for name, a in arrays.items()}], core_ids=[0])
    return r.results[0]["out_h"]
```

```python
import math
from contextlib import ExitStack

import concourse.bass as bass
from concourse import mybir

F32 = mybir.dt.float32
F32R = mybir.dt.float32r
I32 = mybir.dt.int32
ALU = mybir.AluOpType
ACT = mybir.ActivationFunctionType
AX = mybir.AxisListType
P = 128
TOK = 256
NT = TOK // P
D = 1024
FF = 4096
NEG = -1e30
UNIT = 1024
RAW, SPLIT = 4, 5
POOL_CHUNKS = ("ek", "ev0", "ev1", "eo0", "ew0", "eo1", "ew1", "ez0", "ez1")
POOL_UNITS = (1, 2, 3)
STAGES = 3

TWO_PI = (6.28125, 0.0019350051879882812, 2.0 * math.pi - 6.28125 - 0.0019350051879882812)

VEC_ROWS = {}


VEC_LOADS = [("norm1", "norm1_g"), ("gbias", "gla_gate_bias"), ("gout", "gla_out_norm_g"), ("norm2", "norm2_g"),
             ("epre", "even_g_pre_2"), ("convb", "even_conv_b_2"), ("hn", "even_hn_g_2"), ("opre", "odd_g_pre_2"),
             ("gq", "odd_g_q_2"), ("gkv", "odd_g_kv_2")]


def vec_plan(named):
    at = 0
    for name, n in named:
        VEC_ROWS[name] = (at, n)
        at += n
    return at


VECS = vec_plan([("norm1", 8), ("gbias", 4), ("gout", 2), ("norm2", 8), ("mq", 1), ("mk", 1),
                 ("epre", 8), ("convb", 8), ("hn", 8), ("opre", 8), ("gq", 3), ("gkv", 2)])


def program(nc, A, out):
    ctx = ExitStack()
    with ctx:
        def sb(name, shape, dt=F32, c=ctx):
            return c.enter_context(nc.sbuf_tensor(name, shape, dt))

        sems = {}

        def sem(name):
            if name not in sems:
                sems[name] = ctx.enter_context(nc.semaphore(name))
            return sems[name]

        w_in, e_in, o_in = A["w_in"][0], A["even_w_in_2"][0], A["odd_w_in_2"][0]
        CH, UN, CI = [], [], {}

        def chunk(name, w, n0, nn, kts, acts, part=None):
            if name not in CI:
                CI[name] = len(CH)
                CH.append(dict(name=name, nn=nn, kts=kts, acts=acts, units=[], parts=[]))
            ks = part or range(kts)
            per = max(1, UNIT // nn)
            units = []
            for k in range(ks[0], ks[-1] + 1, per):
                units.append(len(UN))
                UN.append((w, k, min(per, ks[-1] + 1 - k), n0, nn))
            CH[CI[name]]["units"] += units
            CH[CI[name]]["parts"].append(units)

        for name, n0 in [("mq", 0), ("mk", 512), ("mv", 1024)]:
            chunk(name, w_in, n0, 512, 8, "n1")
        chunk("glow", w_in, 3584, 16, 8, "n1")
        for name, n0 in [("gq", 1536), ("gk", 2048), ("gv0", 2560), ("gv1", 3072),
                         ("go0", 3600), ("go1", 4112), ("gm0", 4624), ("gm1", 5136),
                         ("gg0", 5648), ("gg1", 6160)]:
            chunk(name, w_in, n0, 512, 8, "n1")
        for n in range(2):
            chunk(f"bm{n}", A["w_branch_moba"][0], 512 * n, 512, 4, "ym")
            chunk(f"bg{n}", A["w_branch_gla"][0], 512 * n, 512, 8, "yg")
        for part in (range(0, 4), range(4, 8)):
            for n in range(2):
                chunk(f"wo{n}", A["w_out"][0], 512 * n, 512, 8, "mix", part)
        for n in range(8):
            chunk(f"up{n}", A["w_up"][0], 512 * n, 512, 8, "n2")
        for n in range(2):
            chunk(f"dn{n}", A["w_down"][0], 512 * n, 512, 32, "u")
        if STAGES >= 2:
            for name, n0 in [("ea0", 0), ("eg", 7168), ("eb0", 1024), ("ea1", 512), ("eb1", 1536), ("eq", 3072), ("ek", 3584),
                             ("ev0", 4096), ("ev1", 4608), ("eo0", 5120), ("ew0", 6144), ("eo1", 5632),
                             ("ew1", 6656), ("ez0", 2048), ("ez1", 2560)]:
                chunk(name, e_in, n0, 16 if name == "eg" else 512, 8, "en")
            for part in (range(8, 16), range(0, 4), range(4, 8)):
                for n in range(2):
                    chunk(f"ey{n}", A["even_w_out_2"][0], 512 * n, 512, 16, "ey", part)
        if STAGES >= 3:
            ukv, uq = A["odd_w_ukv_2"][0], A["odd_w_uq_2"][0]
            chunk("oq", o_in, 0, 384, 8, "on")
            chunk("okv", o_in, 384, 320, 8, "on")
            chunk("of", o_in, 704, 512, 8, "on")
            chunk("oz0", o_in, 1216, 512, 8, "on")
            for n in range(4):
                chunk(f"oc{n}", ukv, 512 * n, 512, 2, "ckv")
            chunk("oz1", o_in, 1728, 512, 8, "on")
            for n in range(3):
                chunk(f"ou{n}", uq, 512 * n, 512, 3, "cq")
            chunk("ozd", o_in, 2240, 512, 8, "on")
            chunk("ofd", A["odd_w_fd_2"][0], 0, 512, 4, "fr")
            for n in range(2):
                chunk(f"oy{n}", A["odd_w_out_2"][0], 512 * n, 512, 12, "oy")

        BY_POOL = [CH[CI[c]]["units"][i] for c in (POOL_CHUNKS if STAGES >= 2 else ()) for i in POOL_UNITS]

        def split_keys(name, kts):
            return [("tr", name, j) for j in range((kts + 1) // 2)]

        AUX = [("vec",)] + split_keys("n1", 8) + [("bias",)]
        AUX += [("qkT", w, j) for w in range(2) for j in range(2)]
        AUX += [("glT",), ("qk0", 0), ("qk0", 1)] + [("qk1", p, i) for i in range(2) for p in range(2)]
        AUX += [("gz", 0), ("gz", 1)]
        AUX += [("pt", i) for i in range(6)]
        AUX += [("gqT", 0), ("gqT", 1), ("gkT", 0), ("gkT", 1)]
        AUX += [("pv", 0), ("pv", 1), ("kdt", 0), ("kdt", 1), ("ga", 0), ("ga", 1)]
        AUX += [("kv", j, i) for j in range(3) for i in range(2)]
        AUX += [("o", t, i) for t in range(2) for i in range(2)]
        AUX += split_keys("ym", 4) + split_keys("yg", 8) + split_keys("mix", 8) + split_keys("n2", 8)
        AUX += split_keys("u", 32)
        if STAGES >= 2:
            AUX += split_keys("en", 8) + [("gat", 0), ("gat", 1), ("wcv",), ("uT", 0), ("uT", 1), ("mcol",)]
            AUX += [("mb", h) for h in range(4)] + [("uT", 2), ("uT", 3)]
            AUX += [("eqT", w, j) for w in range(2) for j in range(2)] + [("kq", h) for h in range(4)]
            AUX += [("num", h, d, t) for h in range(4) for d in range(2) for t in range(2)]
            AUX += [("cvT", 0, t) for t in range(2)] + split_keys("eh", 8) + split_keys("ea", 8)[0:2]
            AUX += [("cvT", 1, t) for t in range(2)] + split_keys("ea", 8)[2:4]
        if STAGES >= 3:
            AUX += split_keys("on", 8) + split_keys("cq", 3) + split_keys("ckv", 2) + [("krT",)]
            AUX += [("dft", g) for g in range(4)] + split_keys("fr", 4) + [("knT", j) for j in range(4)]
            AUX += [("qnT", j) for j in range(4)] + [("qrT", j) for j in range(2)]
            for h in range(8):
                AUX += [("os", h)] + [("opt", h - 1)] * (h >= 1) + [("opv", (h - 3) // 2)] * (h >= 3 and h % 2)
            AUX += [("opt", 7), ("opv", 3)] + split_keys("yd", 4) + split_keys("yc", 8)
        PLACE = {key: i for i, key in enumerate(AUX)}
        SPLITS = {key: i for i, key in enumerate(k for k in AUX if k[0] == "tr")}

        raw = [sb(f"raw{i}", [P, UNIT]) for i in range(RAW)]
        whi = [sb(f"whi{i}", [P, UNIT], F32R) for i in range(SPLIT)]
        wlo = [sb(f"wlo{i}", [P, UNIT], F32R) for i in range(SPLIT)]
        H = sb("H", [P, NT, D])
        XN = sb("XN", [P, NT, D])
        a_hi, a_lo = sb("a_hi", [P, 8, TOK], F32R), sb("a_lo", [P, 8, TOK], F32R)
        b_hi, b_lo = sb("b_hi", [P, 12, TOK], F32R), sb("b_lo", [P, 12, TOK], F32R)
        ident = sb("ident", [P, P])
        vec_in, vec = sb("vec_in", [P, P]), sb("vec", [P, P])
        stat = sb("stat", [P, 8])
        epsc = sb("epsc", [P, 4])
        ystat = sb("ystat", [P, 2, NT, 2])
        yrms = sb("yrms", [P, 2, NT])
        junk = sb("junk", [P, D])
        acc = [ctx.enter_context(nc.psum_tensor(f"acc{i}", [P, 512], F32)) for i in range(4)]
        aux = [ctx.enter_context(nc.psum_tensor(f"aux{i}", [P, 512], F32)) for i in range(4)]

        def gain(name, k):
            r = VEC_ROWS[name][0] + k
            return vec[:, r:r + 1]

        c1 = ExitStack()
        t5x = sb("t5x", [33, 8], c=c1)
        B0, B1 = sb("B0", [P, 8, P], c=c1), sb("B1", [P, 8, TOK], c=c1)
        QKN = sb("QKN", [P, 2, NT, 512], c=c1)
        QKT = sb("QKT", [P, 2, 4, TOK], c=c1)
        PR = sb("PR", [P, 8 * 384], c=c1)
        PT = sb("PT", [P, 24, P], c=c1)
        MV = sb("MV", [P, NT, 512], c=c1)
        GQK = sb("GQK", [P, 2, NT, 512], c=c1)
        T = sb("T", [P, 4, 4, TOK], c=c1)
        rmask = sb("rmask", [P, 4 * TOK], c=c1)
        gl = sb("gl", [P, NT, 16], c=c1)
        glT = sb("glT", [16, TOK], c=c1)
        gup = sb("gup", [16, 512], c=c1)
        edl = sb("edl", [P, 4, 4], c=c1)
        qst = sb("qst", [P, 2, NT, 8], c=c1)
        pst = sb("pst", [P, 3, NT, 8], c=c1)
        gst = sb("gst", [P, NT, 4], c=c1)
        c1.close()

        def flat(ap):
            while len(ap.shape) > 2:
                ap = ap.rearrange("p a b -> p (a b)") if len(ap.shape) == 3 else \
                    ap.rearrange("p a b c -> p (a b c)") if len(ap.shape) == 4 else \
                    ap.rearrange("p a b c d -> p (a b c d)")
            return ap

        P0 = PR[:, 0:1024].rearrange("p (h s) -> p h s", h=8)
        P1 = PR[:, 1024:3072].rearrange("p (h s) -> p h s", h=8)
        T1, T2, T3, T4 = T[:, 0], T[:, 1], T[:, 2], T[:, 3]
        bias_rows = junk[0:8, 0:512]
        onehot = flat(GQK[0:33, 0, 0:1])
        ST = [flat(B0[:, :, :]).rearrange("p (h v) -> p h v", h=4),
              flat(B1[:, 0:4]).rearrange("p (h v) -> p h v", h=4),
              flat(B1[:, 4:8]).rearrange("p (h v) -> p h v", h=4)]
        QD = flat(QKN[:, 0]).rearrange("p (h c) -> p h c", h=4)
        KI = flat(QKN[:, 1]).rearrange("p (h c) -> p h c", h=4)
        KD = QKT[:, 0]
        KDT = flat(QKT[:, 1]).rearrange("p (t h d) -> p t h d", t=2, h=4)
        OG = PR[:, 0:2048].rearrange("p (t n) -> p t n", t=2)
        GA = PR[:, 2048:3072].rearrange("p (t h c) -> p t h c", t=2, h=4)
        SGO = flat(PT[:, 0:16]).rearrange("p (t n) -> p t n", t=2)
        YM = GQK[:, 0]
        SG = flat(T[:, :, :, :]).rearrange("p (w t n) -> p w t n", w=2, t=2)
        MX, MTMP = OG, QKN[:, 1, 0]
        GV = XN

        c2 = ExitStack()
        u_hi, u_lo = sb("u_hi", [P, 20, TOK], F32R, c=c2), sb("u_lo", [P, 20, TOK], F32R, c=c2)
        RL = sb("RL", [P, 2, NT, 512], c=c2)
        c2.close()

        c3 = ExitStack()
        if STAGES >= 2:
            AV = sb("AV", [P, NT, D], c=c3)
            EU = sb("EU", [P, 8, TOK + 30], c=c3)
            CV = sb("CV", [P, 8, TOK], c=c3)
            wcv = sb("wcv", [P, 8, 32], c=c3)
            gates = sb("gates", [P, NT, 2, 2, 4], c=c3)
            gbias = sb("gbias", [P, 16], c=c3)
            rone = sb("rone", [4, 2, TOK], c=c3)
            mcol = sb("mcol", [P, 2, 2, NT, 4], c=c3)
            den = sb("den", [P, 4, 2, NT], c=c3)
            EQK = sb("EQK", [P, 2, NT, 512], c=c3)
            EQT = sb("EQT", [P, 2, 4, TOK], c=c3)
            EV = sb("EV", [P, NT, 4, 258], c=c3)
            DW = sb("DW", [P, 4, 2, 384], c=c3)
            SOB = sb("SOB", [P, NT, D], c=c3)
            ETMP = sb("ETMP", [P, NT, 512], c=c3)
            gng, gnb = sb("gng", [P, D], c=c3), sb("gnb", [P, D], c=c3)
            est = sb("est", [P, NT, 4], c=c3)
            bst, bag = sb("bst", [P, 16, 6], c=c3), sb("bag", [P, 16, 2], c=c3)
            HM = flat(EQK[:, :, :, :]).rearrange("p (t n) -> p t n", t=NT)
            SZA = flat(EQT[:, :, :, :]).rearrange("p (t n) -> p t n", t=NT)
            post_g = flat(EV[:, 0])[:, 0:D]
            YTMP = AV
            wcv_in = flat(CV[0:31, 0:4])
            BLOCKS = ((0, 0, 0, 0, 256), (0, 1, 256, 128, 128), (1, 0, 0, 0, 128), (1, 1, 128, 0, 256))
            RF, RX = XN[0:4, 0, 0:512].rearrange("p (d t) -> p d t", d=2), XN[0:4, 0, 512:1024].rearrange("p (d t) -> p d t", d=2)
            RG, RM = XN[0:4, 1, 0:512].rearrange("p (d t) -> p d t", d=2), XN[0:4, 1, 512:1024].rearrange("p (d t) -> p d t", d=2)
        c3.close()

        c4 = ExitStack()
        if STAGES >= 3:
            QF = sb("QF", [P, NT, 1536], c=c4)
            KN = sb("KN", [P, NT, 8, P], c=c4)
            OV = sb("OV", [P, NT, 8, P], c=c4)
            KR0, KR = sb("KR0", [P, NT, 64], c=c4), sb("KR", [P, NT, 2, 64], c=c4)
            KRT = sb("KRT", [P, TOK], c=c4)
            QNT, KNT = sb("QNT", [P, 8, TOK], c=c4), sb("KNT", [P, 8, TOK], c=c4)
            QRT = sb("QRT", [P, 4, TOK], c=c4)
            SZC = sb("SZC", [P, NT, D], c=c4)
            YD = sb("YD", [P, NT, 512], c=c4)
            FX = sb("FX", [P, NT, 512], c=c4)
            dft_s = sb("dft_s", [P, NT, 512], c=c4)
            dft_c = sb("dft_c", [P, 2, P], c=c4)
            ZT = sb("ZT", [P, 5 * 512], c=c4)
            post2 = sb("post2", [P, D], c=c4)
            pos_i = sb("pos_i", [P, NT], I32, c=c4)
            pos = sb("pos", [P, NT], c=c4)
            invf = sb("invf", [P, 32], c=c4)
            ang = sb("ang", [P, NT, 32], c=c4)
            turns = sb("turns", [P, 2, NT, 32], c=c4)
            trig = sb("trig", [P, 2, NT, 32], c=c4)

            cst = sb("cst", [P, 2, NT], c=c4)
            omx, osum, orec = [sb(n, [P, 8, NT], c=c4) for n in ("omx", "osum", "orec")]
            OP = [ZT[:, 512 * i:512 * i + 512].rearrange("p (t s) -> p t s", t=NT) for i in range(2)]
            OPT = [ZT[:, 1024 + 512 * i:1536 + 512 * i].rearrange("p (s t) -> p s t", s=NT) for i in range(3)]
            YC = QF[:, :, 0:D]
            rt = ZT[:, 0:1024].rearrange("p (a b) -> p a b", a=4)
            QR = XN[:, :, 0:512]
            YTMP2 = KN[:, :].rearrange("p t h d -> p t (h d)")
        c4.close()

        def bank(key):
            return aux[PLACE[key] % 4]

        def aux_wait(e, key):
            i = PLACE[key]
            e.wait_ge(sem(f"aux_ready{i % 4}"), i // 4 + 1)

        def aux_free(ins, key):
            ins.then_inc(sem(f"aux_free{PLACE[key] % 4}"), 1)

        def aux_done(e, key):
            i = PLACE[key]
            e.wait_ge(sem(f"aux_free{i % 4}"), i // 4 + 1)

        def acc_wait(e, c, t):
            if t == 0:
                e.wait_ge(sem("tile0_done"), CI[c] + 1)
            else:
                e.wait_ge(sem("units_used"), CH[CI[c]]["units"][-1] + 1)

        def acc_of(c, t):
            return acc[2 * (CI[c] % 2) + t][:, 0:CH[CI[c]]["nn"]]

        def acc_free(ins, c):
            ins.then_inc(sem(f"acc_free{CI[c] % 2}"), 1)

        def acc_done(e, c, t):
            e.wait_ge(sem(f"acc_free{CI[c] % 2}"), 2 * (CI[c] // 2) + t + 1)

        class Chain:
            def __init__(self, e, name):
                self.e, self.s, self.n = e, sem(name), 0

            def __call__(self, ins):
                self.n += 1
                ins.then_inc(self.s, 1)
                self.e.wait_ge(self.s, self.n)

        def lo_wait(e, u):
            if u in BY_POOL:
                e.wait_ge(sem("lo_done_pool"), BY_POOL.index(u) + 1)
            else:
                e.wait_ge(sem("lo_done"), u + 1 - sum(v < u for v in BY_POOL))

        def lo_part(e, u):
            e.wait_ge(sem("hi_done"), u + 1)
            return e.tensor_tensor(w_view(wlo[u % SPLIT], u), w_view(raw[u % RAW], u),
                                   w_view(whi[u % SPLIT], u).bitcast(F32), ALU.subtract)

        def w_view(buf, u):
            _, _, nk, _, nn = UN[u]
            return buf[:, 0:nk * nn]

        WHERE = {"n1": (a_hi, a_lo, 0), "mix": (a_hi, a_lo, 0), "n2": (a_hi, a_lo, 0), "en": (a_hi, a_lo, 0),
                 "on": (a_hi, a_lo, 0), "eh": (a_hi, a_lo, 0), "ym": (b_hi, b_lo, 0), "yg": (b_hi, b_lo, 4),
                 "ea": (b_hi, b_lo, 0), "cq": (b_hi, b_lo, 0), "ckv": (b_hi, b_lo, 3), "fr": (b_hi, b_lo, 5),
                 "yd": (b_hi, b_lo, 8), "yc": (b_hi, b_lo, 0)}

        def act_tile(name, k):
            if name == "ey":
                name, k = ("ea", k) if k < 8 else ("eh", k - 8)
            if name == "oy":
                name, k = ("yc", k) if k < 8 else ("yd", k - 8)
            key = ("tr", name, k // 2)
            if name == "u":
                return (b_hi[:, k], b_lo[:, k], key) if k < 12 else (u_hi[:, k - 12], u_lo[:, k - 12], key)
            if name == "eh" and k < 4:
                return b_hi[:, 8 + k], b_lo[:, 8 + k], key
            hi, lo, o = WHERE[name]
            return hi[:, o + k], lo[:, o + k], key

        def halves(key):
            return bank(key)[:, :].rearrange("p (k t) -> p k t", k=2)

        def gain_and_bias(e, chain, i, t):
            cs = slice(512 * i, 512 * i + 512)
            chain(e.tensor_tensor(AV[:, t, cs], AV[:, t, cs], gng[:, cs], ALU.mult))
            e.tensor_tensor(AV[:, t, cs], AV[:, t, cs], gnb[:, cs], ALU.add).then_inc(sem("gn_out"), 1)

        block = ctx.enter_context(nc.Block())

        @block.sync
        def _(sp):
            for n in range(2):
                cs = slice(512 * n, 512 * n + 512)
                sp.dma_start(H[:, :, cs], A["x"][0].rearrange("(t p) d -> p t d", p=P)[:, :, cs]
                             ).then_inc(sem(f"x_in{n}"), 16)
            for u, (w, k, nk, n0, nn) in enumerate(UN):
                if u >= RAW:
                    lo_wait(sp, u - RAW)
                dst = raw[u % RAW][:, 0:nk * nn].rearrange("p (k n) -> p k n", k=nk)
                src = w[k * P:(k + nk) * P, n0:n0 + nn].rearrange("(k p) n -> p k n", p=P)
                sp.dma_start(dst, src).then_inc(sem(f"raw_in{u % RAW}"), 16)
            for n in range(2):
                for t in range(NT):
                    sp.wait_ge(sem("h_out"), 2 * NT * (STAGES - 2) + NT * n + t + 1)
                    sp.dma_start(out[0, t * P:(t + 1) * P, 512 * n:512 * n + 512], H[:, t, 512 * n:512 * n + 512]
                                 ).then_inc(sem("stored"), 16)
            sp.wait_ge(sem("stored"), 16 * 2 * NT)

        @block.gpsimd
        def _(pool):
            chain = Chain(pool, "pool_chain")
            pool.memset(vec_in[:, :], 0.0).then_inc(sem("vec_zero"), 1)
            chain(pool.memset(ident[:, :], 0.0))
            pool.affine_select(out=ident[:, :], in_=ident[:, :], compare_op=ALU.not_equal, fill=1.0, base=0,
                               pattern=[[-1, P]], channel_multiplier=1).then_inc(sem("ident"), 1)
            pool.wait_ge(sem("vec_zero"), 1)
            chain(pool.memset(t5x[:, :], NEG))
            pool.dma_start(t5x[0:32, :], A["t5_bias"]).then_inc(sem("t5_in"), 16)
            pool.dma_start(onehot, A["onehot"]).then_inc(sem("t5_in"), 16)
            pool.dma_start(gup[:, :], A["gla_gate_up"][0]).then_inc(sem("gup_in"), 16)
            for name, key in VEC_LOADS[1::2]:
                r, n = VEC_ROWS[name]
                pool.dma_start(vec_in[r:r + n, :], A[key][0].rearrange("(r c) -> r c", c=P)).then_inc(sem("vec_in_pool"), 16)
            aux_done(pool, ("bias",))
            pool.dma_start(A["skew"], bias_rows.unsqueeze(1).to_broadcast([8, P, 512])).then_inc(sem("skew_out"), 16)
            pool.wait_ge(sem("skew_out"), 16)
            for t, B in enumerate((B0, B1)):
                for a in range(2):
                    src = bass.AP(tensor=A["skew"].tensor, offset=A["skew"].offset + 512 * P * a + 255 - P * t,
                                  ap=[[511, P], [1024 * P, 4], [1, P * (t + 1)]])
                    pool.dma_start(B[:, 4 * a:4 * a + 4], src).then_inc(sem("bias_in"), 16)
            for t in range(NT):
                aux_done(pool, ("ga", t))
                chain(pool.affine_select(out=GA[:, t], in_=GA[:, t], compare_op=ALU.is_ge, fill=0.0, base=0,
                                         pattern=[[0, 4], [1, P]], channel_multiplier=-1))
                pool.memset(GA[0:64, t, :, 64:128], 0.0).then_inc(sem("ga_masked"), 1)
            if STAGES >= 2:
                pool.wait_ge(sem("units_used"), CH[CI["dn1"]]["units"][-1] + 1)
                pool.dma_start(gbias[:, :], A["even_b_gate_2"][0].partition_broadcast(P)).then_inc(sem("gbias_in"), 16)
                pool.dma_start(wcv_in, A["even_conv_w_2"][0]).then_inc(sem("wcv_in"), 16)
                pool.dma_start(gng[:, :], A["even_gn_g_2"][0].partition_broadcast(P)).then_inc(sem("gn_in"), 16)
                pool.dma_start(gnb[:, :], A["even_gn_b_2"][0].partition_broadcast(P)).then_inc(sem("gn_in"), 16)
                for n in range(2):
                    cs = slice(512 * n, 512 * n + 512)
                    for t in range(NT):
                        acc_done(pool, f"ea{n}", t)
                        acc_done(pool, f"eb{n}", t)
                        pool.tensor_tensor(AV[:, t, cs], AV[:, t, cs], ETMP[:, t], ALU.mult).then_inc(sem("u_gated"), 1)
                for h in range(4):
                    pool.wait_ge(sem("dw_exp"), h + 1)
                    for d in range(2):
                        v = DW[:, h, d].rearrange("p (b c) -> p b c", b=3)[:, 0:3:2]
                        pool.affine_select(out=v, in_=v, compare_op=ALU.is_ge, fill=0.0, base=0,
                                           pattern=[[0, 2], [1 - 2 * d, P]], channel_multiplier=2 * d - 1
                                           ).then_inc(sem("dw_masked"), 1)
                def lo_parts(c):
                    for u in CH[CI[c]]["units"]:
                        if u in BY_POOL:
                            lo_part(pool, u).then_inc(sem("lo_done_pool"), 1)

                for c in ("ek", "ev0", "ev1", "eo0", "ew0", "eo1"):
                    lo_parts(c)
                for n in range(2):
                    cs = slice(512 * n, 512 * n + 512)
                    for t in range(NT):
                        acc_done(pool, f"eo{n}", t)
                        acc_done(pool, f"ew{n}", t)
                        pool.tensor_tensor(SOB[:, t, cs], SOB[:, t, cs], ETMP[:, t], ALU.mult
                                           ).then_inc(sem("etmp_used"), 1)
                    for c in (("ew1", "ez0"), ("ez1",))[n]:
                        lo_parts(c)
                pool.wait_ge(sem("gn_in"), 32)
                for t in range(NT):
                    pool.wait_ge(sem("gn_unit"), t + 1)
                    gain_and_bias(pool, chain, 0, t)
                aux_wait(pool, ("num", 3, 1, 1))
                pool.dma_start(post_g, A["even_g_post_2"][0].partition_broadcast(P)).then_inc(sem("post_in"), 16)
            if STAGES >= 3:
                pool.wait_ge(sem("h_out"), 2 * NT)
                pool.dma_start(pos_i[:, :], A["positions_2"][0].rearrange("(t p) -> p t", p=P),
                               allow_slow_non_contiguous=True).then_inc(sem("pos_in"), 16)
                pool.dma_start(invf[:, :], A["inv_freq"].partition_broadcast(P)).then_inc(sem("pos_in"), 16)
                pool.dma_start(dft_s[:, :], A["dft_s"].rearrange("(t p) n -> p t n", p=P)).then_inc(sem("dft_in"), 16)
                pool.dma_start(dft_c[:, :], A["dft_c"].rearrange("a p n -> p a n")).then_inc(sem("dft_in"), 16)
                pool.dma_start(post2[:, :], A["odd_g_post_2"][0].partition_broadcast(P)).then_inc(sem("post_in"), 16)

        @block.scalar
        def _(act):
            chain = Chain(act, "act_chain")
            at = [0]
            loaded = [None]

            def use(tables):
                if loaded[0] != tables:
                    act.preload_act_table_set(tables)
                    loaded[0] = tables

            def pump(c, ahead=SPLIT - 1):
                last = min(CH[CI[c]]["units"][-1] + ahead, len(UN) - 1)
                while at[0] <= last:
                    u = at[0]
                    act.wait_ge(sem(f"raw_in{u % RAW}"), 16 * (u // RAW + 1))
                    if u >= SPLIT:
                        act.wait_ge(sem("units_used"), u - SPLIT + 1)
                    act.activation(w_view(whi[u % SPLIT], u), w_view(raw[u % RAW], u), ACT.Copy
                                   ).then_inc(sem("hi_done"), 1)
                    at[0] += 1

            def split_hi(name, ks, g=None):
                for j in range(ks[0] // 2, (ks[-1] + 2) // 2):
                    key = ("tr", name, j)
                    aux_wait(act, key)
                    for i in range(min(2, ks[-1] + 1 - 2 * j)):
                        hi = act_tile(name, 2 * j + i)[0]
                        if g is None:
                            ins = act.activation(hi, halves(key)[:, i], ACT.Copy)
                        else:
                            ins = act.activation(hi, halves(key)[:, i], ACT.Copy, scale=g(2 * j + i))
                    ins.then_inc(sem("hi_split"), 1)

            def rstd(ap, n, eps=0):
                use("natural_log_exp_and_others")
                chain(act.activation(ap, ap, ACT.Ln, scale=1.0 / n, bias=epsc[0:ap.shape[0], eps:eps + 1]))
                return act.activation(ap, ap, ACT.Exp, scale=-0.5)

            def norm_stats(i, before):
                for t in range(NT):
                    before(t)
                    chain(act.activation(junk[:, :], H[:, t], ACT.Square, accum_out=stat[:, 2 * i + t:2 * i + t + 1]))
                rstd(stat[:, 2 * i:2 * i + 2], D).then_inc(sem("rstd"), 1)
                act.wait_ge(sem("rstd"), i + 1)

            def rms(i, t):
                return stat[:, 2 * i + t:2 * i + t + 1]

            TABLES = {ACT.Sigmoid: "sigmoid_and_others", ACT.Silu: "silu_and_others"}

            def copy_out(c, dst, t, func=ACT.Copy, scale=1.0):
                if func in TABLES:
                    use(TABLES[func])
                acc_wait(act, c, t)
                acc_free(act.activation(dst, acc_of(c, t), func, scale=scale), c)

            act.wait_ge(sem("vec_zero"), 1)
            for name, key in VEC_LOADS[0::2]:
                r, n = VEC_ROWS[name]
                act.dma_start(vec_in[r:r + n, :], A[key][0].rearrange("(r c) -> r c", c=P)).then_inc(sem("vec_in"), 16)
            for name, key in (("mq", "moba_q_norm_g"), ("mk", "moba_k_norm_g")):
                r = VEC_ROWS[name][0]
                for i in range(2):
                    act.dma_start(vec_in[r:r + 1, 64 * i:64 * i + 64], A[key]).then_inc(sem("vec_in"), 16)

            act.wait_ge(sem("consts"), 1)
            for n in range(2):
                act.wait_ge(sem(f"x_in{n}"), 16)
            aux_done(act, ("vec",))
            split_hi("n1", range(4), lambda k: gain("norm1", k))
            pump("mq", -3)
            split_hi("n1", range(4, 8), lambda k: gain("norm1", k))
            pump("mq", 0)
            norm_stats(0, lambda t: None)
            for w, c in enumerate(("mq", "mk")):
                pump(c)
                for t in range(NT):
                    acc_wait(act, c, t)
                    act.activation(QKN[:, w, t], acc_of(c, t), ACT.Square, scale=rms(0, t)).then_inc(sem("q_square"), 1)
                act.wait_ge(sem("q_sum"), 2 * w + 2)
                rstd(flat(qst[:, w]), 64).then_inc(sem("q_rstd"), 1)
            pump("mv")
            for t in range(NT):
                copy_out("mv", MV[:, t], t, scale=rms(0, t))
            pump("glow")
            for t in range(NT):
                copy_out("glow", gl[:, t], t, scale=rms(0, t))
            pump("gq")
            for t in range(NT):
                copy_out("gq", GQK[:, 0, t], t, scale=rms(0, t))
            aux_wait(act, ("glT",))
            aux_free(act.activation(glT[:, :], bank(("glT",))[0:16, 0:TOK], ACT.Copy), ("glT",))
            for t, PX in enumerate((P0, P1)):
                act.wait_ge(sem("p_max"), t + 1)
                for h in range(8):
                    ins = act.activation(PX[:, h], PX[:, h], ACT.Exp, bias=pst[:, 0, t, h:h + 1],
                                         accum_out=pst[:, 1, t, h:h + 1])
                ins.then_inc(sem("p_exp"), 1)
                if t == 0:
                    pump("gk", 1)
            pump("gk")
            for t in range(NT):
                copy_out("gk", GQK[:, 1, t], t, scale=rms(0, t))
            for j in range(2):
                aux_wait(act, ("gz", j))
                for i in range(2):
                    ins = act.activation(T1[:, 2 * j + i], halves(("gz", j))[:, i], ACT.Abs,
                                         bias=gain("gbias", 2 * j + i))
                chain(ins)
                act.activation(T1[:, 2 * j:2 * j + 2], T1[:, 2 * j:2 * j + 2], ACT.Exp, scale=-1.0
                               ).then_inc(sem("gz_abs"), 1)
            act.wait_ge(sem("gz_abs"), 2)
            act.activation(T1, T1, ACT.Ln, bias=epsc[:, 2:3]).then_inc(sem("gz_ln"), 1)
            pump("gv0", 1)
            act.wait_ge(sem("g_cum"), 1)
            act.activation(T1, T3, ACT.Exp, scale=1.0 / 16)
            act.activation(T4, T3, ACT.Exp, scale=-1.0 / 16).then_inc(sem("g_exp"), 1)
            act.wait_ge(sem("g_rest"), 1)
            act.activation(T2, T2, ACT.Exp, scale=1.0 / 16).then_inc(sem("g_exp"), 1)
            pump("gv0")
            for t in range(NT):
                copy_out("gv0", GV[:, t, 0:512], t, scale=rms(0, t))
            for i in range(6):
                aux_wait(act, ("pt", i))
                aux_free(act.activation(flat(PT[:, 4 * i:4 * i + 4]), bank(("pt", i))[:, :], ACT.Copy), ("pt", i))
            pump("gv1")
            for t in range(NT):
                copy_out("gv1", GV[:, t, 512:1024], t, scale=rms(0, t))
            for t in range(NT):
                aux_wait(act, ("kdt", t))
                aux_free(act.activation(flat(KDT[:, t]), bank(("kdt", t))[:, :], ACT.Copy), ("kdt", t))
            for t in range(NT):
                aux_wait(act, ("ga", t))
                aux_free(act.activation(flat(GA[:, t]), bank(("ga", t))[:, :], ACT.Copy), ("ga", t))
            for n in range(2):
                pump(f"go{n}")
                for t in range(NT):
                    copy_out(f"go{n}", SGO[:, t, 512 * n:512 * n + 512], t, ACT.Silu, rms(0, t))
            for t in range(NT):
                for i in range(2):
                    aux_wait(act, ("o", t, i))
                    aux_free(act.activation(OG[:, t, 512 * i:512 * i + 512], bank(("o", t, i))[:, :], ACT.Copy),
                             ("o", t, i))
                    aux_done(act, ("o", t, i))
                    for h in (2 * i, 2 * i + 1):
                        ins = act.activation(junk[:, 256 * h:256 * h + 256], OG[:, t, 256 * h:256 * h + 256], ACT.Square,
                                             accum_out=gst[:, t, h:h + 1])
                chain(ins)
            rstd(flat(gst[:, :]), 256).then_inc(sem("g_rstd"), 1)
            act.wait_ge(sem("t_free"), 1)
            for w, c in enumerate(("gm", "gg")):
                for n in range(2):
                    pump(f"{c}{n}")
                    for t in range(NT):
                        copy_out(f"{c}{n}", SG[:, w, t, 512 * n:512 * n + 512], t, ACT.Sigmoid, rms(0, t))
                    if (w, n) == (0, 0):
                        split_hi("ym", range(4))
                    if (w, n) == (1, 0):
                        split_hi("yg", range(8), lambda k: gain("gout", k % 2))
            pump("bm1")
            split_hi("mix", range(4))
            pump("bg1")
            split_hi("mix", range(4, 8))
            pump("wo1", 3)
            split_hi("n2", range(4), lambda k: gain("norm2", k))
            pump("wo1")
            use("natural_log_exp_and_others")
            split_hi("n2", range(4, 8), lambda k: gain("norm2", k))
            pump("wo1", 5)

            def wo_done(t):
                for n in range(2):
                    acc_done(act, f"wo{n}", t)

            norm_stats(1, wo_done)
            for n in range(9):
                if n < 8:
                    pump(f"up{n}")
                    for t in range(NT):
                        copy_out(f"up{n}", RL[:, n % 2, t], t, ACT.Relu, rms(1, t))
                if n >= 1:
                    split_hi("u", range(4 * n - 4, 4 * n))
            pump("dn0")
            pump("dn1", 3)
            if STAGES >= 2:
                def post_norm(c, i):
                    for n in range(2):
                        pump(f"{c}{n}")
                        if n == 1:
                            use("natural_log_exp_and_others")
                        for t in range(NT):
                            acc_wait(act, f"{c}{n}", t)
                            act.activation(junk[:, 512 * t:512 * t + 512], acc_of(f"{c}{n}", t), ACT.Square,
                                           accum_out=ystat[:, i, t, n:n + 1]).then_inc(sem("y_squared"), 1)
                        act.wait_ge(sem("y_squared"), 4 * i + 2 * n + 2)
                    for t in range(NT):
                        ins = act.activation(yrms[:, i, t:t + 1], ystat[:, i, t, 0:1], ACT.Identity,
                                             bias=ystat[:, i, t, 1:2])
                    chain(ins)
                    rstd(yrms[:, i], D).then_inc(sem("y_rstd"), 1)

                def dn_done(t):
                    for n in range(2):
                        acc_done(act, f"dn{n}", t)

                use("natural_log_exp_and_others")
                split_hi("en", range(4), lambda k: gain("epre", k))
                pump("dn1")
                split_hi("en", range(4, 8), lambda k: gain("epre", k))
                pump("dn1", 5)
                norm_stats(2, dn_done)
                pump("ea0")
                for t in range(NT):
                    copy_out("ea0", AV[:, t, 0:512], t, scale=rms(2, t))
                pump("eb0")
                use("natural_log_exp_and_others")
                aux_wait(act, ("gat", 1))
                chain(act.activation(flat(RX), bank(("gat", 1))[0:4, :], ACT.Abs))
                chain(act.activation(flat(RX), flat(RX), ACT.Exp, scale=-1.0))
                act.activation(flat(RX), flat(RX), ACT.Ln, bias=epsc[0:4, 2:3]).then_inc(sem("eg_ln"), 1)
                for t in range(NT):
                    copy_out("eb0", ETMP[:, t], t, ACT.Sigmoid, rms(2, t))
                pump("ea1")
                for t in range(NT):
                    copy_out("ea1", AV[:, t, 512:1024], t, scale=rms(2, t))

                def by_channel(j):
                    aux_wait(act, ("uT", j))
                    aux_free(act.activation(EU[:, 2 * j:2 * j + 2, 15:15 + TOK], halves(("uT", j)), ACT.Copy), ("uT", j))

                by_channel(0)
                by_channel(1)
                pump("eb1")
                for t in range(NT):
                    act.wait_ge(sem("u_gated"), t + 1)
                    copy_out("eb1", ETMP[:, t], t, ACT.Sigmoid, rms(2, t))
                aux_done(act, ("mcol",))
                use("natural_log_exp_and_others")
                act.activation(flat(mcol[:, 1]), flat(mcol[:, 1]), ACT.Exp, scale=-1.0).then_inc(sem("clamp"), 1)
                for h in range(4):
                    aux_wait(act, ("mb", h))
                    for d, st, o, a, n in BLOCKS:
                        ins = act.activation(DW[:, h, d, o:o + n], halves(("mb", h))[:, d, a:a + n], ACT.Relu,
                                             bias=mcol[:, 0, d, st, h:h + 1])
                    aux_free(ins, ("mb", h))
                    aux_done(act, ("mb", h))
                    act.activation(flat(DW[:, h]), flat(DW[:, h]), ACT.Exp, scale=-1.0).then_inc(sem("dw_exp"), 1)
                pump("eq")
                for t in range(NT):
                    copy_out("eq", EQK[:, 0, t], t, scale=rms(2, t))
                by_channel(2)
                by_channel(3)
                pump("ek")
                for t in range(NT):
                    copy_out("ek", EQK[:, 1, t], t, scale=rms(2, t))
                for w in range(2):
                    if w == 1:
                        pump("ev0")
                        for t in range(NT):
                            copy_out("ev0", EV[:, t, 0:2, 0:256], t, scale=rms(2, t))
                    for j in range(2):
                        aux_wait(act, ("eqT", w, j))
                        aux_free(act.activation(EQT[:, w, 2 * j:2 * j + 2], halves(("eqT", w, j)), ACT.Copy,
                                                scale=(1.0, 128.0 ** -0.5)[w]), ("eqT", w, j))
                pump("ev1")
                for t in range(NT):
                    copy_out("ev1", EV[:, t, 2:4, 0:256], t, scale=rms(2, t))

                def numerators(h):
                    for t in range(NT):
                        act.wait_ge(sem("den"), h + 1)
                        aux_free(act.activation(HM[:, t, 256 * h:256 * h + 256], bank(("num", h, 0, t))[:, 0:256],
                                                ACT.Copy, scale=den[:, h, 0, t:t + 1]), ("num", h, 0, t))

                def out_gate(n):
                    pump(f"eo{n}")
                    for t in range(NT):
                        copy_out(f"eo{n}", SOB[:, t, 512 * n:512 * n + 512], t, ACT.Sigmoid, rms(2, t))
                    pump(f"ew{n}")
                    for t in range(NT):
                        if n == 0:
                            act.wait_ge(sem("u_gated"), 4)
                        else:
                            act.wait_ge(sem("etmp_used"), t + 1)
                        copy_out(f"ew{n}", ETMP[:, t], t, ACT.Silu, rms(2, t))

                numerators(0)
                numerators(1)
                pump("eo0", 3)
                numerators(2)
                numerators(3)

                def by_token(i):
                    for t in range(NT):
                        aux_wait(act, ("cvT", i, t))
                        aux_free(act.activation(AV[:, t, 512 * i:512 * i + 512], bank(("cvT", i, t))[:, :], ACT.Copy),
                                 ("cvT", i, t))

                def group_rstd(i):
                    act.wait_ge(sem("bn_done"), i + 1)
                    rstd(bag[:, 8 * i:8 * i + 8, 1], 1, eps=1).then_inc(sem("bn_rstd"), 1)

                def conv_silu(i):
                    use("silu_and_others")
                    for t in range(NT):
                        act.wait_ge(sem("gn_out"), 2 * i + t + 1)
                        act.activation(XN[:, t, 512 * i:512 * i + 512], AV[:, t, 512 * i:512 * i + 512], ACT.Silu
                                       ).then_inc(sem("gn_silu"), 1)

                out_gate(0)
                by_token(0)
                out_gate(1)
                for t in range(NT):
                    aux_done(act, ("num", 3, 1, t))
                for h in range(4):
                    for t in range(NT):
                        aux_done(act, ("num", h, 1, t))
                        ins = act.activation(junk[:, 256 * (2 * (h % 2) + t):256 * (2 * (h % 2) + t) + 256],
                                             HM[:, t, 256 * h:256 * h + 256], ACT.Square, accum_out=est[:, t, h:h + 1])
                    chain(ins)
                rstd(flat(est[:, :]), 256).then_inc(sem("h_rstd"), 1)
                group_rstd(0)
                for n in range(2):
                    pump(f"ez{n}")
                    for t in range(NT):
                        copy_out(f"ez{n}", SZA[:, t, 512 * n:512 * n + 512], t, ACT.Silu, rms(2, t))
                    if n == 0:
                        split_hi("eh", range(4), lambda k: gain("hn", k))
                split_hi("eh", range(4, 8), lambda k: gain("hn", k))
                conv_silu(0)
                pump("ez1", 8)
                split_hi("ea", range(4))
                pump("ez1", 11)
                by_token(1)
                group_rstd(1)
                pump("ez1", 12)
                conv_silu(1)
                pump("ez1", 14)
                split_hi("ea", range(4, 8))
                post_norm("ey", 0)
            if STAGES >= 3:
                split_hi("on", range(4), lambda k: gain("opre", k))
                split_hi("on", range(4, 8), lambda k: gain("opre", k))
                norm_stats(3, lambda t: act.wait_ge(sem("h_out"), 2 * NT))
                for w, (c, n) in enumerate((("oq", 384), ("okv", 256))):
                    pump(c)
                    for t in range(NT):
                        acc_wait(act, c, t)
                        act.activation(junk[:, 512 * t:512 * t + n], acc_of(c, t)[:, 0:n], ACT.Square, scale=rms(3, t),
                                       accum_out=cst[:, w, t:t + 1])
                        if w == 1:
                            act.activation(KR0[:, t], acc_of(c, t)[:, 256:320], ACT.Copy, scale=rms(3, t))
                        ins = act.activation(XN[:, t, 384 * w:384 * w + n], acc_of(c, t)[:, 0:n], ACT.Copy,
                                             scale=rms(3, t))
                        acc_free(ins, c)
                        acc_done(act, c, t)
                    rstd(cst[:, w], n).then_inc(sem("c_rstd"), 1)
                    act.wait_ge(sem("c_rstd"), w + 1)
                    if w == 0:
                        act.wait_ge(sem("angles"), 1)
                        use("trig_and_small")
                        act.activation(trig[:, :].rearrange("p a t f -> p (a t f)"),
                                       turns[:, :].rearrange("p a t f -> p (a t f)"), ACT.Sin
                                       ).then_inc(sem("sines"), 1)
                pump("of")
                for t in range(NT):
                    copy_out("of", FX[:, t], t, scale=rms(3, t))
                split_hi("cq", range(3), lambda k: gain("gq", k))
                split_hi("ckv", range(2), lambda k: gain("gkv", k))

                def gate(c, dst):
                    pump(c)
                    for t in range(NT):
                        copy_out(c, dst(t), t, ACT.Silu, rms(3, t))

                def keys(n):
                    pump(f"oc{n}")
                    for t in range(NT):
                        acc_wait(act, f"oc{n}", t)
                        act.activation(KN[:, t, 2 * n:2 * n + 2],
                                       acc_of(f"oc{n}", t).rearrange("p (h w d) -> p h w d", h=2, w=2)[:, :, 0],
                                       ACT.Copy, scale=cst[:, 1, t:t + 1]).then_inc(sem("kn_copied"), 1)

                gate("oz0", lambda t: SZC[:, t, 0:512])
                for g in range(4):
                    aux_wait(act, ("dft", g))
                    aux_free(act.activation(ZT[:, 512 * g:512 * g + 512], bank(("dft", g))[:, :], ACT.Copy), ("dft", g))
                keys(0)
                keys(1)
                split_hi("fr", range(4))
                keys(2)
                keys(3)
                gate("oz1", lambda t: SZC[:, t, 512:1024])
                for n in range(3):
                    pump(f"ou{n}")
                    for t in range(NT):
                        copy_out(f"ou{n}", QF[:, t, 512 * n:512 * n + 512], t, scale=cst[:, 0, t:t + 1])
                gate("ozd", lambda t: YD[:, t])
                for j in range(4):
                    aux_wait(act, ("qnT", j))
                    aux_free(act.activation(QNT[:, 2 * j:2 * j + 2], halves(("qnT", j)), ACT.Copy, scale=192.0 ** -0.5),
                             ("qnT", j))
                for j in range(2):
                    aux_wait(act, ("qrT", j))
                    aux_free(act.activation(QRT[:, 2 * j:2 * j + 2], halves(("qrT", j)), ACT.Copy, scale=192.0 ** -0.5),
                             ("qrT", j))
                pump("ofd")
                use("natural_log_exp_and_others")

                def exponentials(h):
                    aux_wait(act, ("os", h))
                    act.wait_ge(sem("o_max"), h + 1)
                    for t in range(NT):
                        ins = act.activation(OP[h % 2][:, t], halves(("os", h))[:, t], ACT.Exp, bias=omx[:, h, t:t + 1],
                                             accum_out=osum[:, h, t:t + 1])
                    aux_free(ins, ("os", h))

                def turned(h):
                    aux_wait(act, ("opt", h))
                    aux_free(act.activation(flat(OPT[h % 3]), bank(("opt", h))[:, :], ACT.Copy), ("opt", h))

                for h in range(8):
                    exponentials(h)
                    if h >= 1:
                        turned(h - 1)
                turned(7)
                split_hi("yd", range(4))
                split_hi("yc", range(8))
                post_norm("oy", 1)

        @block.vector
        def _(dve):
            chain = Chain(dve, "dve_chain")
            at = [0]

            def pump(c, ahead=SPLIT - 1, between=None):
                last = min(CH[CI[c]]["units"][-1] + ahead, len(UN) - 1)
                while at[0] <= last:
                    u = at[0]
                    at[0] += 1
                    if u not in BY_POOL:
                        lo_part(dve, u).then_inc(sem("lo_done"), 1)
                        if between:
                            between()

            def split_lo(name, ks, g=None):
                for j in range(ks[0] // 2, (ks[-1] + 2) // 2):
                    key = ("tr", name, j)
                    aux_wait(dve, key)
                    dve.wait_ge(sem("hi_split"), SPLITS[key] + 1)
                    for i in range(min(2, ks[-1] + 1 - 2 * j)):
                        hi, lo, _ = act_tile(name, 2 * j + i)
                        if g is None:
                            ins = dve.tensor_tensor(lo, halves(key)[:, i], hi.bitcast(F32), ALU.subtract)
                        else:
                            ins = dve.scalar_tensor_tensor(out=lo, in0=halves(key)[:, i], scalar=g(2 * j + i),
                                                           in1=hi.bitcast(F32), op0=ALU.mult, op1=ALU.subtract)
                    aux_free(ins, key)

            def rms(i, t):
                return stat[:, 2 * i + t:2 * i + t + 1]

            def add_to_h(c, n, t):
                acc_wait(dve, c, t)
                acc_free(dve.tensor_tensor(H[:, t, 512 * n:512 * n + 512], acc_of(c, t),
                                           H[:, t, 512 * n:512 * n + 512], ALU.add), c)

            dve.memset(epsc[:, 0:1], 1e-6)
            dve.memset(epsc[:, 1:2], 1e-5)
            dve.memset(epsc[:, 2:3], 1.0).then_inc(sem("consts"), 1)
            chain(dve.memset(rmask[:, :], 1.0))
            chain(dve.memset(rmask[:, :].rearrange("p (c e) -> p c e", e=64)[:, :, 0:1], 0.0))
            aux_wait(dve, ("vec",))
            aux_free(dve.tensor_copy(vec[:, :], bank(("vec",))[:, 0:P]), ("vec",))
            split_lo("n1", range(4), lambda k: gain("norm1", k))
            pump("mq", -3)
            split_lo("n1", range(4, 8), lambda k: gain("norm1", k))
            pump("mq", 0)
            aux_wait(dve, ("bias",))
            dve.wait_ge(sem("rstd"), 1)
            aux_free(dve.tensor_copy(bias_rows, bank(("bias",))[0:8, :]), ("bias",))
            for w, c in enumerate(("mq", "mk")):
                pump(c)
                for t in range(NT):
                    dve.wait_ge(sem("q_square"), 2 * w + t + 1)
                    dve.tensor_reduce(qst[:, w, t], QKN[:, w, t].rearrange("p (h d) -> p h d", h=8), AX.X, ALU.add
                                      ).then_inc(sem("q_sum"), 1)
                dve.wait_ge(sem("q_rstd"), w + 1)
                for t in range(NT):
                    acc_free(dve.scalar_tensor_tensor(out=QKN[:, w, t].rearrange("p (h d) -> p h d", h=8),
                                                      in0=acc_of(c, t).rearrange("p (h d) -> p h d", h=8),
                                                      scalar=rms(0, t),
                                                      in1=qst[:, w, t].unsqueeze(2).to_broadcast([P, 8, 64]),
                                                      op0=ALU.mult, op1=ALU.mult), c)
            pump("mv")
            for w in range(2):
                for j in range(2):
                    key = ("qkT", w, j)
                    aux_wait(dve, key)
                    aux_free(dve.tensor_scalar(QKT[:, w, 2 * j:2 * j + 2], halves(key), gain(("mq", "mk")[w], 0),
                                               (0.125, 1.0)[w], ALU.mult, ALU.mult), key)
            pump("gq")
            dve.wait_ge(sem("bias_in"), 64)
            for p in range(2):
                key = ("qk0", p)
                aux_wait(dve, key)
                aux_free(dve.tensor_tensor(P0[:, 4 * p:4 * p + 4], bank(key)[:, :].rearrange("p (h s) -> p h s", h=4),
                                           B0[:, 4 * p:4 * p + 4], ALU.add), key)
            aux_done(dve, ("qk0", 1))
            aux_done(dve, ("qk0", 0))
            dve.tensor_reduce(pst[:, 0, 0], P0, AX.X, ALU.max, negate=True).then_inc(sem("p_max"), 1)
            for i in range(2):
                for p in range(2):
                    key = ("qk1", p, i)
                    hs = slice(4 * p + 2 * i, 4 * p + 2 * i + 2)
                    aux_wait(dve, key)
                    aux_free(dve.tensor_tensor(P1[:, hs], halves(key), B1[:, hs], ALU.add), key)
            for i in range(2):
                for p in range(2):
                    aux_done(dve, ("qk1", p, i))
            dve.tensor_reduce(pst[:, 0, 1], P1, AX.X, ALU.max, negate=True).then_inc(sem("p_max"), 1)
            pump("gk")
            for j in range(2):
                dve.wait_ge(sem("gz_abs"), j + 1)
                for i in range(2):
                    ins = dve.tensor_scalar(T2[:, 2 * j + i], halves(("gz", j))[:, i], gain("gbias", 2 * j + i), 0.0,
                                            ALU.add, ALU.min)
                aux_free(ins, ("gz", j))
            for j in range(2):
                aux_done(dve, ("gz", j))
            dve.wait_ge(sem("gz_ln"), 1)
            chain(dve.tensor_tensor(T2, T2, T1, ALU.subtract))
            dve.tensor_tensor_scan(flat(T3), rmask[:, :], flat(T2), 0.0, ALU.mult, ALU.add).then_inc(sem("g_cum"), 1)
            dve.wait_ge(sem("g_cum"), 1)
            b3 = flat(T3).rearrange("p (c e) -> p c e", e=64)
            dve.tensor_tensor(flat(T2).rearrange("p (c e) -> p c e", e=64), b3[:, :, 63:64].to_broadcast([P, 16, 64]),
                              b3, ALU.subtract).then_inc(sem("g_rest"), 1)
            pump("gv0")
            dve.wait_ge(sem("p_exp"), 2)
            dve.reciprocal(flat(pst[:, 2]), flat(pst[:, 1])).then_inc(sem("p_recip"), 1)
            dve.wait_ge(sem("g_exp"), 1)
            chain(dve.tensor_copy(edl[:, :, :], T1.rearrange("p h (j e) -> p h j e", e=64)[:, :, :, 63]))
            for j in range(2):
                hs = slice(2 * j, 2 * j + 2)
                aux_wait(dve, ("gqT", j))
                aux_free(dve.scalar_tensor_tensor(out=QD[:, hs], in0=halves(("gqT", j)), scalar=128.0 ** -0.5,
                                                  in1=T1[:, hs], op0=ALU.mult, op1=ALU.mult), ("gqT", j))
            dve.wait_ge(sem("g_exp"), 2)
            for j in range(2):
                hs = slice(2 * j, 2 * j + 2)
                aux_wait(dve, ("gkT", j))
                dve.tensor_tensor(KI[:, hs], halves(("gkT", j)), T4[:, hs], ALU.mult)
                aux_free(dve.tensor_tensor(KD[:, hs], halves(("gkT", j)), T2[:, hs], ALU.mult), ("gkT", j))
            aux_done(dve, ("gkT", 1))
            dve.memset(epsc[:, 3:4], 0.0).then_inc(sem("t_free"), 1)
            pump("gv1")
            dve.wait_ge(sem("p_recip"), 1)
            for t in range(NT):
                aux_wait(dve, ("pv", t))
                r = pst[:, 2, t].rearrange("p (a h) -> p h a", a=2).unsqueeze(3).to_broadcast([P, 4, 2, 64])
                aux_free(dve.tensor_tensor(YM[:, t].rearrange("p (h a d) -> p h a d", a=2, d=64),
                                           bank(("pv", t))[:, :].rearrange("p (h a d) -> p h a d", a=2, d=64),
                                           r, ALU.mult), ("pv", t))
            pump("go0")
            for j in range(3):
                for i in range(2):
                    key = ("kv", j, i)
                    aux_wait(dve, key)
                    if j == 0:
                        ins = dve.tensor_copy(ST[0][:, 2 * i:2 * i + 2], halves(key))
                    else:
                        aux_done(dve, ("kv", j - 1, i))
                        for h in (2 * i, 2 * i + 1):
                            ins = dve.scalar_tensor_tensor(out=ST[j][:, h], in0=ST[j - 1][:, h], scalar=edl[:, h, j:j + 1],
                                                           in1=halves(key)[:, h - 2 * i], op0=ALU.mult, op1=ALU.add)
                    aux_free(ins, key)
            pump("go1")
            for n in range(2):
                for t in range(NT):
                    acc_done(dve, f"go{n}", t)
            dve.wait_ge(sem("g_rstd"), 1)
            for t in range(NT):
                for h in range(4):
                    hs = slice(256 * h, 256 * h + 256)
                    ins = dve.scalar_tensor_tensor(out=OG[:, t, hs], in0=OG[:, t, hs], scalar=gst[:, t, h:h + 1],
                                                   in1=SGO[:, t, hs], op0=ALU.mult, op1=ALU.mult)
            ins.then_inc(sem("yg_ready"), 1)
            pump("gm0")
            split_lo("ym", range(4))
            pump("gm1")
            pump("gg0")
            split_lo("yg", range(8), lambda k: gain("gout", k % 2))
            pump("gg1")
            for n in range(2):
                cs = slice(512 * n, 512 * n + 512)
                pump(f"bm{n}")
                for t in range(NT):
                    acc_done(dve, f"gm{n}", t)
                    acc_wait(dve, f"bm{n}", t)
                    acc_free(dve.tensor_tensor(MX[:, t, cs], acc_of(f"bm{n}", t), SG[:, 0, t, cs], ALU.mult), f"bm{n}")
                if n == 1:
                    split_lo("mix", range(4))
                pump(f"bg{n}")
                for t in range(NT):
                    acc_done(dve, f"gg{n}", t)
                    acc_wait(dve, f"bg{n}", t)
                    acc_free(dve.tensor_tensor(MTMP, acc_of(f"bg{n}", t), SG[:, 1, t, cs], ALU.mult), f"bg{n}")
                    acc_done(dve, f"bg{n}", t)
                    acc_done(dve, f"bm{n}", t)
                    ins = dve.tensor_tensor(MX[:, t, cs], MX[:, t, cs], MTMP, ALU.add)
                    ins.then_inc(sem("mixed"), 1)
                    dve.wait_ge(sem("mixed"), 2 * n + t + 1)
            split_lo("mix", range(4, 8))
            for n in range(2):
                pump(f"wo{n}", 3)
                if n == 1:
                    split_lo("n2", range(4), lambda k: gain("norm2", k))
                for t in range(NT):
                    add_to_h(f"wo{n}", n, t)
            pump("wo1")
            split_lo("n2", range(4, 8), lambda k: gain("norm2", k))
            for n in range(9):
                if n < 8:
                    pump(f"up{n}")
                    for t in range(NT):
                        acc_done(dve, f"up{n}", t)
                        dve.tensor_tensor(RL[:, n % 2, t], RL[:, n % 2, t], RL[:, n % 2, t], ALU.mult
                                          ).then_inc(sem("squared"), 1)
                if n >= 1:
                    split_lo("u", range(4 * n - 4, 4 * n))
            for n in range(2):
                pump(f"dn{n}", 3)
                if STAGES >= 2 and n == 1:
                    split_lo("en", range(4), lambda k: gain("epre", k))
                for t in range(NT):
                    add_to_h(f"dn{n}", n, t)
            pump("dn1")
            if STAGES >= 2:
                split_lo("en", range(4, 8), lambda k: gain("epre", k))
                pump("dn1", 5)
                chain(dve.memset(EU[:, :, :], 0.0))
                dve.memset(rone[:, 0], 1.0)
                dve.memset(rone[:, 1], 0.0)
                chain(dve.memset(EV[:, :, :, 256:257], 1.0))
                dve.memset(epsc[:, 3:4], 0.0).then_inc(sem("even_consts"), 1)
                pump("eg")
                dve.wait_ge(sem("gbias_in"), 16)
                dve.wait_ge(sem("rstd"), 3)
                for t in range(NT):
                    acc_wait(dve, "eg", t)
                    for d in range(2):
                        ins = dve.scalar_tensor_tensor(out=gates[:, t, :, d],
                                                       in0=acc_of("eg", t)[:, 8 * d:8 * d + 8].rearrange("p (k h) -> p k h", k=2),
                                                       scalar=rms(2, t),
                                                       in1=gbias[:, 8 * d:8 * d + 8].rearrange("p (k h) -> p k h", k=2),
                                                       op0=ALU.mult, op1=ALU.add)
                    acc_free(ins, "eg")
                pump("eb0")
                dve.wait_ge(sem("eg_ln"), 1)
                ins = dve.tensor_scalar(flat(RF), bank(("gat", 1))[0:4, :], 0.0, None, ALU.min)
                aux_free(ins, ("gat", 1))
                aux_done(dve, ("gat", 1))
                chain(dve.tensor_tensor(flat(RF), flat(RF), flat(RX), ALU.subtract))
                dve.tensor_tensor_scan(RX[:, 0], rone[:, 0], RF[:, 0], 0.0, ALU.mult, ALU.add)
                chain(dve.tensor_tensor_scan(RX[:, 1, ::-1], rone[:, 0], RF[:, 1, ::-1], 0.0, ALU.mult, ALU.add))
                aux_wait(dve, ("gat", 0))
                aux_free(dve.tensor_tensor(flat(RG), bank(("gat", 0))[0:4, :], flat(RX), ALU.subtract), ("gat", 0))
                aux_done(dve, ("gat", 0))
                dve.tensor_tensor_scan(RM[:, 0], RG[:, 0], rone[:, 1], 0.0, ALU.max, ALU.add)
                chain(dve.tensor_tensor_scan(RM[:, 1, ::-1], RG[:, 1, ::-1], rone[:, 1], 0.0, ALU.max, ALU.add))
                dve.tensor_tensor(flat(RF), flat(RX), flat(RM), ALU.add).then_inc(sem("m_rows"), 1)
                aux_wait(dve, ("wcv",))
                aux_free(dve.tensor_copy(flat(wcv[:, :]), bank(("wcv",))[:, 0:256]), ("wcv",))
                aux_done(dve, ("wcv",))

                taps = [(g, k, c) for g in range(2) for k in range(31) for c in range(4)]
                tap_at = [0]
                conv_done = sem("conv")

                def conv(n=22):
                    for i in range(tap_at[0], min(tap_at[0] + n, len(taps))):
                        tap_at[0] += 1
                        g, k, c = taps[i]
                        if i == 0 or i == 124:
                            aux_done(dve, ("uT", 2 * g))
                            aux_done(dve, ("uT", 2 * g + 1))
                        c += 4 * g
                        if k == 0:
                            ins = dve.tensor_scalar(CV[:, c], EU[:, c, 0:TOK], wcv[:, c, 0:1], gain("convb", c),
                                                    ALU.mult, ALU.add)
                        else:
                            dve.wait_ge(conv_done, i - 3)
                            ins = dve.scalar_tensor_tensor(out=CV[:, c], in0=EU[:, c, k:k + TOK],
                                                           scalar=wcv[:, c, k:k + 1], in1=CV[:, c],
                                                           op0=ALU.mult, op1=ALU.add)
                        ins.then_inc(conv_done, 1)

                pump("ea1")
                conv(8)
                pump("eb1")
                aux_wait(dve, ("mcol",))
                dve.tensor_scalar(flat(mcol[:, 0]), bank(("mcol",))[:, 0:16], -1.0, None, ALU.mult)
                aux_free(dve.tensor_copy(flat(mcol[:, 1]), bank(("mcol",))[:, 16:32]), ("mcol",))
                conv(20)
                pump("eq", between=lambda: conv(9))
                pump("ek", between=lambda: conv(25))
                pump("ev0", between=lambda: conv(25))
                for h in range(4):
                    key = ("kq", h)
                    aux_wait(dve, key)
                    dve.wait_ge(sem("dw_masked"), 2 * h + 2)
                    for d, st, o, a, n in BLOCKS:
                        ins = dve.tensor_tensor(DW[:, h, d, o:o + n], DW[:, h, d, o:o + n],
                                                halves(key)[:, st, a:a + n], ALU.mult)
                    aux_free(ins, key)
                pump("ev1", 2, between=lambda: conv(20))

                def denominators(h):
                    banks = [(d, t) for d in range(2) for t in range(NT)]
                    for d, t in banks:
                        aux_wait(dve, ("num", h, d, t))
                        ins = dve.tensor_tensor(den[:, h, d, t:t + 1], bank(("num", h, d, t))[:, 256:257],
                                                mcol[:, 1, d, t, h:h + 1], ALU.max)
                    chain(ins)
                    for d, t in banks:
                        one = den[:, h, d, t:t + 1]
                        ins = dve.scalar_tensor_tensor(out=one, in0=bank(("num", h, d, t))[:, 256:257], scalar=-1.0,
                                                       in1=one, op0=ALU.mult, op1=ALU.max)
                    chain(ins)
                    dve.reciprocal(den[:, h].rearrange("p d t -> p (d t)"), den[:, h].rearrange("p d t -> p (d t)")
                                   ).then_inc(sem("den"), 1)
                    for t in range(NT):
                        dve.wait_ge(sem("den"), h + 1)
                        aux_done(dve, ("num", h, 0, t))
                        hs = HM[:, t, 256 * h:256 * h + 256]
                        aux_free(dve.scalar_tensor_tensor(out=hs, in0=bank(("num", h, 1, t))[:, 0:256],
                                                          scalar=den[:, h, 1, t:t + 1], in1=hs,
                                                          op0=ALU.mult, op1=ALU.add), ("num", h, 1, t))

                dve.wait_ge(sem("clamp"), 1)
                denominators(0)
                denominators(1)
                pump("eo0", 0)
                conv(24)
                pump("eo0", 3)
                denominators(2)
                denominators(3)
                pump("eo0")
                conv(20)
                pump("ew0", between=conv)

                def group_stats(i):
                    for t in range(NT):
                        aux_done(dve, ("cvT", i, t))
                        for g in range(4):
                            ins = dve.bn_stats(bst[:, 8 * i + 4 * t + g], AV[:, t, P * (4 * i + g):P * (4 * i + g + 1)])
                    chain(ins)
                    for g in range(8):
                        ins = dve.bn_aggr(bag[:, 8 * i + g], bst[:, 8 * i + g])
                    ins.then_inc(sem("bn_done"), 1)

                def group_norm(i, t):
                    for g in range(4):
                        v, m = AV[:, t, P * (4 * i + g):P * (4 * i + g + 1)], bag[:, 8 * i + 4 * t + g]
                        ins = dve.tensor_scalar(v, v, m[:, 0:1], m[:, 1:2], ALU.subtract, ALU.mult)
                    if i == 0:
                        ins.then_inc(sem("gn_unit"), 1)
                    else:
                        chain(ins)
                        gain_and_bias(dve, chain, i, t)

                def conv_out(i):
                    cs = slice(512 * i, 512 * i + 512)
                    for t in range(NT):
                        acc_done(dve, f"ez{i}", t)
                        dve.wait_ge(sem("gn_silu"), 2 * i + t + 1)
                        dve.tensor_tensor(AV[:, t, cs], XN[:, t, cs], SZA[:, t, cs], ALU.mult
                                          ).then_inc(sem("ya_ready"), 1)

                pump("eo1", 2, between=conv)
                group_stats(0)
                pump("eo1", between=conv)
                pump("ew1", between=conv)
                dve.wait_ge(sem("h_rstd"), 1)
                dve.wait_ge(sem("etmp_used"), 4)
                for t in range(NT):
                    for h in range(4):
                        hs = slice(256 * h, 256 * h + 256)
                        ins = dve.scalar_tensor_tensor(out=HM[:, t, hs], in0=HM[:, t, hs], scalar=est[:, t, h:h + 1],
                                                       in1=SOB[:, t, hs], op0=ALU.mult, op1=ALU.mult)
                ins.then_inc(sem("yh_ready"), 1)
                pump("ez0")
                dve.wait_ge(sem("gn_in"), 32)
                dve.wait_ge(sem("bn_rstd"), 1)
                group_norm(0, 0)
                group_norm(0, 1)
                split_lo("eh", range(4), lambda k: gain("hn", k))
                pump("ez1", 2, between=lambda: conv(6))
                pump("ez1")
                split_lo("eh", range(4, 8), lambda k: gain("hn", k))
                pump("ez1", 5)
                conv_out(0)
                pump("ez1", 8, between=lambda: conv(5))
                split_lo("ea", range(4))
                conv(len(taps))
                pump("ez1", 11)
                group_stats(1)
                dve.wait_ge(sem("bn_rstd"), 2)
                group_norm(1, 0)
                pump("ez1", 12)
                group_norm(1, 1)
                conv_out(1)
                pump("ez1", 14)
                split_lo("ea", range(4, 8))

                def times_gain(c, n, i, g, tmp):
                    if n == 0:
                        dve.wait_ge(sem("post_in"), 16 * (i + 1))
                    for t in range(NT):
                        dve.wait_ge(sem("y_squared"), 4 * i + 2 * n + t + 1)
                        cs = slice(512 * n, 512 * n + 512)
                        acc_free(dve.tensor_tensor(tmp[:, t, cs], acc_of(f"{c}{n}", t), g[:, cs], ALU.mult), f"{c}{n}")

                def add_normed(c, i, tmp):
                    dve.wait_ge(sem("y_rstd"), i + 1)
                    for n in range(2):
                        cs = slice(512 * n, 512 * n + 512)
                        for t in range(NT):
                            acc_done(dve, f"{c}{n}", t)
                            dve.scalar_tensor_tensor(out=H[:, t, cs], in0=tmp[:, t, cs], scalar=yrms[:, i, t:t + 1],
                                                     in1=H[:, t, cs], op0=ALU.mult, op1=ALU.add
                                                     ).then_inc(sem("h_out"), 1)

                for n in range(2):
                    pump(f"ey{n}")
                    times_gain("ey", n, 0, post_g, YTMP)
                add_normed("ey", 0, YTMP)
            if STAGES >= 3:
                split_lo("on", range(4), lambda k: gain("opre", k))
                split_lo("on", range(4, 8), lambda k: gain("opre", k))
                pump("oq")
                C1, C2, C3 = TWO_PI
                magic = 1.5 * 2.0 ** 23
                dve.wait_ge(sem("pos_in"), 32)
                chain(dve.tensor_copy(pos[:, :], pos_i[:, :]))
                for t in range(NT):
                    ins = dve.tensor_scalar(ang[:, t], invf[:, :], pos[:, t:t + 1], None, ALU.mult)
                chain(ins)
                for w in range(2):
                    k, a = flat(turns[:, w]), flat(ang[:, :])
                    chain(dve.tensor_scalar(k, a, 1.0 / (2 * math.pi), 0.25 * w, ALU.mult, ALU.add))
                    chain(dve.tensor_scalar(k, k, magic, magic, ALU.add, ALU.subtract))
                    u = flat(trig[:, w])
                    chain(dve.scalar_tensor_tensor(out=u, in0=k, scalar=-C1, in1=a, op0=ALU.mult, op1=ALU.add))
                    chain(dve.scalar_tensor_tensor(out=u, in0=k, scalar=-C2, in1=u, op0=ALU.mult, op1=ALU.add))
                    chain(dve.scalar_tensor_tensor(out=u, in0=k, scalar=-C3, in1=u, op0=ALU.mult, op1=ALU.add))
                    chain(dve.tensor_scalar(k, u, 0.5 * math.pi * w, 3.1415925, ALU.add, ALU.min))
                    ins = dve.tensor_scalar(k, k, -3.1415925, None, ALU.max)
                    if w == 0:
                        chain(ins)
                ins.then_inc(sem("angles"), 1)
                pump("okv")

                def rotate(dst, src, t, n):
                    x1, x2 = src[:, :, 0:32], src[:, :, 32:64]
                    sin = trig[:, 0, t].unsqueeze(1).to_broadcast([P, n, 32])
                    cos = trig[:, 1, t].unsqueeze(1).to_broadcast([P, n, 32])
                    a, b, c, d = [rt[:, i, 0:32 * n].rearrange("p (h f) -> p h f", h=n) for i in range(4)]
                    dve.tensor_tensor(a, x1, cos, ALU.mult)
                    dve.tensor_tensor(b, x2, sin, ALU.mult)
                    dve.tensor_tensor(c, x1, sin, ALU.mult)
                    chain(dve.tensor_tensor(d, x2, cos, ALU.mult))
                    dve.tensor_tensor(dst[:, :, 0:32], a, b, ALU.subtract)
                    chain(dve.tensor_tensor(dst[:, :, 32:64], c, d, ALU.add))

                dve.wait_ge(sem("sines"), 1)
                for t in range(NT):
                    acc_done(dve, "okv", t)
                    rotate(KR[:, t, 0:1], KR0[:, t].unsqueeze(1), t, 1)
                    ins = dve.tensor_copy(KR[:, t, 1], KR[:, t, 0])
                ins.then_inc(sem("kr_ready"), 1)
                pump("of")
                split_lo("cq", range(3), lambda k: gain("gq", k))
                split_lo("ckv", range(2), lambda k: gain("gkv", k))

                def values(n):
                    pump(f"oc{n}")
                    for t in range(NT):
                        dve.wait_ge(sem("kn_copied"), 2 * n + t + 1)
                        acc_free(dve.tensor_scalar(OV[:, t, 2 * n:2 * n + 2],
                                                   acc_of(f"oc{n}", t).rearrange("p (h w d) -> p h w d", h=2, w=2)[:, :, 1],
                                                   cst[:, 1, t:t + 1], None, ALU.mult), f"oc{n}")

                def key_tiles(j):
                    aux_wait(dve, ("knT", j))
                    aux_free(dve.tensor_copy(KNT[:, 2 * j:2 * j + 2], halves(("knT", j))), ("knT", j))

                pump("oz0")
                aux_wait(dve, ("krT",))
                aux_free(dve.tensor_copy(KRT[:, :], bank(("krT",))[:, 0:TOK]), ("krT",))
                values(0)
                values(1)
                split_lo("fr", range(4))
                values(2)
                values(3)
                key_tiles(0)
                key_tiles(1)
                pump("oz1")
                key_tiles(2)
                key_tiles(3)
                for n in range(3):
                    pump(f"ou{n}")
                for t in range(NT):
                    for n in range(3):
                        acc_done(dve, f"ou{n}", t)
                    q = QF[:, t].rearrange("p (h f) -> p h f", h=8)[:, :, 128:192]
                    rotate(QR[:, t].rearrange("p (h f) -> p h f", h=8), q, t, 8)
                dve.memset(epsc[:, 3:4], 0.0).then_inc(sem("qr_ready"), 1)
                pump("ozd")
                pump("ofd", 4)
                for t in range(NT):
                    acc_done(dve, "ozd", t)
                    acc_wait(dve, "ofd", t)
                    acc_free(dve.tensor_tensor(YD[:, t], YD[:, t], acc_of("ofd", t), ALU.mult), "ofd")
                for t in range(NT):
                    acc_done(dve, "oz0", t)
                    acc_done(dve, "oz1", t)

                def heads_out(p):
                    key = ("opv", p)
                    aux_wait(dve, key)
                    for h in (2 * p, 2 * p + 1):
                        for t in range(NT):
                            b = bank(key)[:, :].rearrange("p (h t d) -> p h t d", h=2, t=2)[:, h % 2, t]
                            ins = dve.scalar_tensor_tensor(out=YC[:, t, P * h:P * h + P], in0=b,
                                                           scalar=orec[:, h, t:t + 1], in1=SZC[:, t, P * h:P * h + P],
                                                           op0=ALU.mult, op1=ALU.mult)
                    aux_free(ins, key)

                for h in range(8):
                    aux_wait(dve, ("os", h))
                    dve.tensor_reduce(omx[:, h], halves(("os", h)), AX.X, ALU.max, negate=True).then_inc(sem("o_max"), 1)
                    if h >= 1:
                        aux_done(dve, ("os", h - 1))
                        chain(dve.reciprocal(orec[:, h - 1], osum[:, h - 1]))
                    if h >= 3 and h % 2:
                        heads_out((h - 3) // 2)
                aux_done(dve, ("os", 7))
                chain(dve.reciprocal(orec[:, 7], osum[:, 7]))
                heads_out(3)
                split_lo("yd", range(4))
                split_lo("yc", range(8))
                for n in range(2):
                    pump(f"oy{n}")
                    times_gain("oy", n, 1, post2, YTMP2)
                add_normed("oy", 1, YTMP2)

        @block.tensor
        def _(pe):
            done = [0]

            def product(c, n0=0, n1=None):
                i, ch = CI[c], CH[CI[c]]
                if i >= 2 and n0 == 0:
                    pe.wait_ge(sem(f"acc_free{i % 2}"), 2 * (i // 2))
                seen = None
                for u in ch["units"][n0:n1]:
                    assert u == done[0]
                    done[0] += 1
                    _, k0, nk, _, nn = UN[u]
                    lo_wait(pe, u)
                    hi = w_view(whi[u % SPLIT], u).rearrange("p (k n) -> p k n", k=nk)
                    lo = w_view(wlo[u % SPLIT], u).rearrange("p (k n) -> p k n", k=nk)
                    for t in range(NT):
                        for k in range(nk):
                            ah, al, key = act_tile(ch["acts"], k0 + k)
                            if t == 0 and key != seen:
                                aux_done(pe, key)
                                seen = key
                            ts = slice(t * P, t * P + P)
                            first = u == ch["units"][0] and k == 0
                            last = u == ch["units"][-1] and k == nk - 1
                            pe.matmul(acc_of(c, t), ah[:, ts], hi[:, k], start=first, stop=False)
                            pe.matmul(acc_of(c, t), ah[:, ts], lo[:, k], start=False, stop=False)
                            ins = pe.matmul(acc_of(c, t), al[:, ts], hi[:, k], start=False, stop=last)
                        if t == 0 and u == ch["units"][-1]:
                            ins.then_inc(sem("tile0_done"), 1)
                        if t == 1:
                            ins.then_inc(sem("units_used"), 1)

            order = [0]

            def take(key):
                assert AUX[order[0]] == key, (AUX[order[0]], key)
                i = order[0]
                order[0] += 1
                if i >= 4:
                    pe.wait_ge(sem(f"aux_free{i % 4}"), i // 4)
                return aux[i % 4]

            def give(ins, key):
                ins.then_inc(sem(f"aux_ready{PLACE[key] % 4}"), 1)

            def turn(name, ks, src):
                for j in range(ks[0] // 2, (ks[-1] + 2) // 2):
                    key = ("tr", name, j)
                    b = take(key)
                    for i in range(min(2, ks[-1] + 1 - 2 * j)):
                        for t in range(NT):
                            ins = pe.transpose(b[:, TOK * i + P * t:TOK * i + P * t + P], src(2 * j + i, t), ident[:, :])
                    give(ins, key)

            def cols(buf):
                return lambda k, t: buf[:, t, P * k:P * k + P]

            pe.wait_ge(sem("ident"), 1)
            pe.wait_ge(sem("vec_in"), 16 * (len(VEC_LOADS[0::2]) + 4))
            pe.wait_ge(sem("vec_in_pool"), 16 * len(VEC_LOADS[1::2]))
            b = take(("vec",))
            give(pe.transpose(b[:, 0:P], vec_in[:, :], ident[:, :]), ("vec",))
            pe.wait_ge(sem("x_in0"), 16)
            turn("n1", range(4), cols(H))
            pe.wait_ge(sem("x_in1"), 16)
            turn("n1", range(4, 8), cols(H))
            pe.wait_ge(sem("t5_in"), 32)
            b = take(("bias",))
            give(pe.matmul(b[0:8, :], t5x[:, :], onehot, start=True, stop=True),
                 ("bias",))
            product("mq")
            product("mk")
            product("mv")
            for w, c in enumerate(("mq", "mk")):
                for t in range(NT):
                    acc_done(pe, c, t)
                for j in range(2):
                    b = take(("qkT", w, j))
                    for i in range(2):
                        for t in range(NT):
                            k = 2 * j + i
                            ins = pe.transpose(b[:, TOK * i + P * t:TOK * i + P * t + P],
                                               QKN[:, w, t, P * k:P * k + P], ident[:, :])
                    give(ins, ("qkT", w, j))
            product("glow")
            product("gq")
            for t in range(NT):
                acc_done(pe, "glow", t)
            b = take(("glT",))
            for t in range(NT):
                ins = pe.transpose(b[0:16, P * t:P * t + P], gl[:, t], ident[:, :])
            give(ins, ("glT",))
            for w in range(2):
                for j in range(2):
                    aux_done(pe, ("qkT", w, j))

            def logits(out_ap, p, hp, t, ns):
                rows = slice(64 * p, 64 * p + 64)
                return pe.matmul(out_ap, QKT[rows, 0, hp, P * t:P * t + P], QKT[rows, 1, hp, 0:ns],
                                 start=True, stop=True)

            for p in range(2):
                b = take(("qk0", p))
                for hp in range(4):
                    ins = logits(b[:, P * hp:P * hp + P], p, hp, 0, P)
                give(ins, ("qk0", p))
            for i in range(2):
                for p in range(2):
                    b = take(("qk1", p, i))
                    for r in range(2):
                        ins = logits(b[:, TOK * r:TOK * r + TOK], p, 2 * i + r, 1, TOK)
                    give(ins, ("qk1", p, i))
            product("gk")
            aux_done(pe, ("glT",))
            pe.wait_ge(sem("gup_in"), 16)
            for j in range(2):
                b = take(("gz", j))
                for i in range(2):
                    h = 2 * j + i
                    ins = pe.matmul(b[:, TOK * i:TOK * i + TOK], gup[:, P * h:P * h + P], glT[:, :], start=True, stop=True)
                give(ins, ("gz", j))
            product("gv0")
            for i in range(6):
                b = take(("pt", i))
                pe.wait_ge(sem("p_exp"), 1 if i < 2 else 2)
                for r in range(4):
                    src = P0[:, 4 * i + r] if i < 2 else P1[:, 2 * (i - 2) + r // 2, P * (r % 2):P * (r % 2) + P]
                    ins = pe.transpose(b[:, P * r:P * r + P], src, ident[:, :])
                give(ins, ("pt", i))
            for w, c in enumerate(("gq", "gk")):
                for t in range(NT):
                    acc_done(pe, c, t)
                for j in range(2):
                    b = take((c + "T", j))
                    for i in range(2):
                        for t in range(NT):
                            k = 2 * j + i
                            ins = pe.transpose(b[:, TOK * i + P * t:TOK * i + P * t + P],
                                               GQK[:, w, t, P * k:P * k + P], ident[:, :])
                    give(ins, (c + "T", j))
            product("gv1")
            for i in range(6):
                aux_done(pe, ("pt", i))
            for t in range(NT):
                acc_done(pe, "mv", t)
                b = take(("pv", t))
                for q in range(8):
                    h = 2 * (q % 4) + q // 4
                    for s in range(t + 1):
                        blk = PT[:, q] if t == 0 else PT[:, 8 + 2 * q + s]
                        ins = pe.matmul(b[:, 64 * h:64 * h + 64], blk, MV[:, s, 64 * h:64 * h + 64],
                                        start=s == 0, stop=s == t)
                give(ins, ("pv", t))
            for key in (("gqT", 0), ("gqT", 1), ("gkT", 0), ("gkT", 1)):
                aux_done(pe, key)
            for t in range(NT):
                b = take(("kdt", t))
                for h in range(4):
                    ins = pe.transpose(b[:, P * h:P * h + P], KD[:, h, P * t:P * t + P], ident[:, :])
                give(ins, ("kdt", t))
            for t in range(NT):
                b = take(("ga", t))
                for h in range(4):
                    ins = pe.matmul(b[:, P * h:P * h + P], KI[:, h, P * t:P * t + P], QD[:, h, P * t:P * t + P],
                                    start=True, stop=True)
                give(ins, ("ga", t))
            product("go0")
            for n in range(2):
                for t in range(NT):
                    acc_done(pe, f"gv{n}", t)
            for t in range(NT):
                aux_done(pe, ("kdt", t))
            for j in range(3):
                rows = slice(64 * (j % 2), 64 * (j % 2) + 64)
                for i in range(2):
                    b = take(("kv", j, i))
                    for h in (2 * i, 2 * i + 1):
                        ins = pe.matmul(b[:, TOK * (h % 2):TOK * (h % 2) + TOK], KDT[rows, j // 2, h],
                                        GV[rows, j // 2, 256 * h:256 * h + 256], start=True, stop=True)
                    give(ins, ("kv", j, i))
            product("go1")
            for j in range(3):
                for i in range(2):
                    aux_done(pe, ("kv", j, i))
            for t in range(NT):
                pe.wait_ge(sem("ga_masked"), t + 1)
                for i in range(2):
                    b = take(("o", t, i))
                    for h in (2 * i, 2 * i + 1):
                        cs = slice(TOK * (h % 2), TOK * (h % 2) + TOK)
                        ins = pe.matmul(b[:, cs], GA[:, t, h], GV[:, t, 256 * h:256 * h + 256], start=True, stop=False,
                                        skip_group_check=True)
                        for j in (2 * t, 2 * t + 1):
                            if j == 0:
                                continue
                            r0 = 64 * (j % 2)
                            ins = pe.matmul(b[r0:r0 + 64, cs], QD[:, h, 64 * j:64 * j + 64], ST[j - 1][:, h],
                                            start=False, stop=True, skip_group_check=True)
                    give(ins, ("o", t, i))
            product("gm0")
            for t in range(NT):
                aux_done(pe, ("pv", t))
            turn("ym", range(4), cols(YM))
            product("gm1")
            product("gg0")
            pe.wait_ge(sem("yg_ready"), 1)
            turn("yg", range(8), cols(OG))
            product("gg1")
            product("bm0")
            product("bg0")
            product("bm1")
            pe.wait_ge(sem("mixed"), 2)
            turn("mix", range(4), cols(MX))
            product("bg1")
            product("wo0", 0, 2)
            pe.wait_ge(sem("mixed"), 4)
            turn("mix", range(4, 8), cols(MX))
            product("wo1", 0, 2)
            product("wo0", 2, 4)
            product("wo1", 2, 3)

            def h_added(c, n):
                for t in range(NT):
                    acc_done(pe, f"{c}{n}", t)

            h_added("wo", 0)
            turn("n2", range(4), cols(H))
            product("wo1", 3, 4)
            product("up0", 0, 1)
            h_added("wo", 1)
            turn("n2", range(4, 8), cols(H))
            product("up0", 1, 4)
            for n in range(9):
                if 0 < n < 8:
                    product(f"up{n}")
                if n >= 1:
                    pe.wait_ge(sem("squared"), 2 * n)
                    turn("u", range(4 * n - 4, 4 * n),
                         lambda k, t: RL[:, (k // 4) % 2, t, P * (k % 4):P * (k % 4) + P])
            product("dn0")
            product("dn1", 0, 15)
            if STAGES >= 2:
                h_added("dn", 0)
                turn("en", range(4), cols(H))
            product("dn1", 15, 16)
            if STAGES >= 2:
                product("ea0", 0, 1)
                h_added("dn", 1)
                turn("en", range(4, 8), cols(H))
                product("ea0", 1, 4)
                product("eg")
                product("eb0")
                for t in range(NT):
                    acc_done(pe, "eg", t)
                for k in range(2):
                    b = take(("gat", k))
                    for d in range(2):
                        for t in range(NT):
                            ins = pe.transpose(b[0:4, TOK * d + P * t:TOK * d + P * t + P], gates[:, t, k, d], ident[:, :])
                    give(ins, ("gat", k))
                pe.wait_ge(sem("wcv_in"), 16)
                b = take(("wcv",))
                for c in range(8):
                    ins = pe.transpose(b[:, 32 * c:32 * c + 31], wcv_in[:, P * c:P * c + P], ident[0:31, 0:31])
                give(ins, ("wcv",))
                product("ea1")

                def by_channel(j):
                    b = take(("uT", j))
                    for i in range(2):
                        for t in range(NT):
                            c = 2 * j + i
                            ins = pe.transpose(b[:, TOK * i + P * t:TOK * i + P * t + P], AV[:, t, P * c:P * c + P],
                                               ident[:, :])
                    give(ins, ("uT", j))

                pe.wait_ge(sem("u_gated"), 2)
                pe.wait_ge(sem("even_consts"), 1)
                by_channel(0)
                by_channel(1)
                product("eb1")
                pe.wait_ge(sem("m_rows"), 1)
                b = take(("mcol",))
                for g, R in enumerate((RG, RF)):
                    for d in range(2):
                        for t in range(NT):
                            o = 4 * (4 * g + 2 * d + t)
                            ins = pe.transpose(b[:, o:o + 4], R[:, d, P * t:P * t + P], ident[0:4, 0:4])
                give(ins, ("mcol",))
                for h in range(4):
                    b = take(("mb", h))
                    give(pe.matmul(b[:, :], ident[0:4, h:h + 1].to_broadcast([4, P]), flat(RM), start=True, stop=True),
                         ("mb", h))
                product("eq")
                pe.wait_ge(sem("u_gated"), 4)
                by_channel(2)
                by_channel(3)
                product("ek")
                for w, c in enumerate(("eq", "ek")):
                    for t in range(NT):
                        acc_done(pe, c, t)
                    for j in range(2):
                        b = take(("eqT", w, j))
                        for i in range(2):
                            for t in range(NT):
                                k = 2 * j + i
                                ins = pe.transpose(b[:, TOK * i + P * t:TOK * i + P * t + P],
                                                   EQK[:, w, t, P * k:P * k + P], ident[:, :])
                        give(ins, ("eqT", w, j))
                    if w == 0:
                        product("ev0")
                for w in range(2):
                    for j in range(2):
                        aux_done(pe, ("eqT", w, j))
                for h in range(4):
                    b = take(("kq", h))
                    for st in range(NT):
                        ins = pe.matmul(b[:, TOK * st:TOK * st + TOK], EQT[:, 1, h, P * st:P * st + P], EQT[:, 0, h],
                                        start=True, stop=True)
                    give(ins, ("kq", h))
                product("ev1")

                def numerators(h):
                    for n in range(2):
                        for t in range(NT):
                            acc_done(pe, f"ev{n}", t)
                    aux_done(pe, ("kq", h))
                    for d in range(2):
                        for t in range(NT):
                            b = take(("num", h, d, t))
                            src = {(0, 0): [(0, 0)], (0, 1): [(1, 0), (2, 1)], (1, 0): [(0, 0), (1, 1)],
                                   (1, 1): [(2, 1)]}[d, t]
                            for i, (blk, st) in enumerate(src):
                                ins = pe.matmul(b[:, 0:257], DW[:, h, d, P * blk:P * blk + P], EV[:, st, h, 0:257],
                                                start=i == 0, stop=i == len(src) - 1)
                            give(ins, ("num", h, d, t))

                numerators(0)
                numerators(1)
                product("eo0")
                numerators(2)
                numerators(3)
                product("ew0")

                def by_token(i):
                    pe.wait_ge(sem("conv"), 124 * (i + 1))
                    for t in range(NT):
                        b = take(("cvT", i, t))
                        for c in range(4):
                            ins = pe.transpose(b[:, P * c:P * c + P], CV[:, 4 * i + c, P * t:P * t + P], ident[:, :])
                        give(ins, ("cvT", i, t))

                by_token(0)
                product("eo1")
                product("ew1")
                product("ez0")
                pe.wait_ge(sem("yh_ready"), 1)
                turn("eh", range(4), cols(HM))
                product("ez1")
                turn("eh", range(4, 8), cols(HM))
                product("ey0", 0, 4)
                pe.wait_ge(sem("ya_ready"), 2)
                turn("ea", range(4), cols(AV))
                product("ey1", 0, 4)
                by_token(1)
                product("ey0", 4, 6)
                product("ey1", 4, 6)
                pe.wait_ge(sem("ya_ready"), 4)
                turn("ea", range(4, 8), cols(AV))
                product("ey0", 6, 8)
                product("ey1", 6, 8)
            if STAGES >= 3:
                def turn_pairs(key, src):
                    b = take(key)
                    for i in range(2):
                        for t in range(NT):
                            ins = pe.transpose(b[:, TOK * i + P * t:TOK * i + P * t + P], src(i, t), ident[:, :])
                    give(ins, key)

                pe.wait_ge(sem("h_out"), 2)
                turn("on", range(4), cols(H))
                product("oq", 0, 1)
                pe.wait_ge(sem("h_out"), 4)
                turn("on", range(4, 8), cols(H))
                product("oq", 1, 4)
                product("okv")
                product("of")
                for c in ("oq", "okv"):
                    for t in range(NT):
                        acc_done(pe, c, t)
                turn("cq", range(3), cols(XN))
                turn("ckv", range(2), lambda k, t: XN[:, t, 384 + P * k:384 + P * k + P])
                product("oz0")
                pe.wait_ge(sem("kr_ready"), 1)
                b = take(("krT",))
                for t in range(NT):
                    ins = pe.transpose(b[:, P * t:P * t + P], KR[:, t].rearrange("p a f -> p (a f)"), ident[:, :])
                give(ins, ("krT",))
                pe.wait_ge(sem("dft_in"), 32)
                for t in range(NT):
                    acc_done(pe, "of", t)
                for g in range(4):
                    b = take(("dft", g))
                    for t in range(NT):
                        ins = pe.matmul(b[:, :], FX[:, t, P * g:P * g + P], dft_s[:, t], start=t == 0, stop=t == 1)
                    give(ins, ("dft", g))
                product("oc0")
                product("oc1")
                for g in range(4):
                    aux_done(pe, ("dft", g))
                for j in range(2):
                    key = ("tr", "fr", j)
                    b = take(key)
                    for i in range(2):
                        for w in range(2):
                            o = 512 * (2 * j + i) + TOK * w
                            ins = pe.matmul(b[:, TOK * i:TOK * i + TOK], dft_c[:, w], ZT[:, o:o + TOK],
                                            start=w == 0, stop=w == 1)
                    give(ins, key)
                product("oc2")
                product("oc3")
                for j in range(4):
                    if j == 2:
                        product("oz1")
                    for t in range(NT):
                        acc_done(pe, f"oc{j}", t)
                    turn_pairs(("knT", j), lambda i, t: KN[:, t, 2 * j + i])
                for n in range(3):
                    product(f"ou{n}")
                product("ozd")
                for n in range(3):
                    for t in range(NT):
                        acc_done(pe, f"ou{n}", t)
                for j in range(4):
                    turn_pairs(("qnT", j), lambda i, t: QF[:, t, 192 * (2 * j + i):192 * (2 * j + i) + P])
                pe.wait_ge(sem("qr_ready"), 1)
                for j in range(2):
                    turn_pairs(("qrT", j), lambda i, t: QR[:, t, P * (2 * j + i):P * (2 * j + i) + P])
                product("ofd")
                for key in [("knT", j) for j in range(4)] + [("qnT", j) for j in range(4)] + \
                        [("qrT", j) for j in range(2)] + [("krT",)]:
                    aux_done(pe, key)

                def turn_head(h):
                    b = take(("opt", h))
                    aux_done(pe, ("os", h))
                    for s in range(NT):
                        for t in range(NT):
                            ins = pe.transpose(b[:, TOK * s + P * t:TOK * s + P * t + P], OP[h % 2][:, t, P * s:P * s + P],
                                               ident[:, :])
                    give(ins, ("opt", h))

                def weigh(p):
                    b = take(("opv", p))
                    for h in (2 * p, 2 * p + 1):
                        aux_done(pe, ("opt", h))
                        for t in range(NT):
                            o = 256 * (h % 2) + P * t
                            for s in range(NT):
                                ins = pe.matmul(b[:, o:o + P], OPT[h % 3][:, s, P * t:P * t + P], OV[:, s, h],
                                                start=s == 0, stop=s == 1)
                    give(ins, ("opv", p))

                for h in range(8):
                    b = take(("os", h))
                    rows = slice(64 * (h % 2), 64 * (h % 2) + 64)
                    for t in range(NT):
                        o = TOK * t
                        pe.matmul(b[:, o:o + TOK], QNT[:, h, P * t:P * t + P], KNT[:, h], start=True, stop=False)
                        ins = pe.matmul(b[:, o:o + TOK], QRT[rows, h // 2, P * t:P * t + P], KRT[rows, :],
                                        start=False, stop=True)
                    give(ins, ("os", h))
                    if h >= 1:
                        turn_head(h - 1)
                    if h >= 3 and h % 2:
                        weigh((h - 3) // 2)
                turn_head(7)
                weigh(3)
                for t in range(NT):
                    acc_done(pe, "ofd", t)
                turn("yd", range(4), cols(YD))
                turn("yc", range(8), cols(YC))
                product("oy0")
                product("oy1")


SHAPES_OUT = (1, TOK, D)


def distance_buckets():
    import numpy as np
    hot = np.zeros((33, 512), np.float32)
    for j in range(512):
        d = 255 - j
        if d < 0:
            hot[32, j] = 1.0
            continue
        b = d
        if d >= 16:
            large = np.float32(np.log(np.float32(d) / np.float32(16.0))) / np.float32(math.log(128 / 16))
            b = min(31, 16 + int(np.float32(large * np.float32(16.0))))
        hot[b, j] = 1.0
    return hot


def constants():
    import numpy as np
    a = 2 * np.pi * (np.outer(np.arange(TOK), np.arange(TOK)) % TOK) / TOK
    b = 2 * np.pi * (np.outer(np.arange(P), np.arange(P)) % P) / P
    return {"onehot": distance_buckets(),
            "inv_freq": (10000.0 ** (-np.arange(0, 64, 2) / 64.0)).astype(np.float32),
            "dft_s": (np.concatenate([np.cos(a), -np.sin(a)], axis=1) / np.sqrt(TOK)).astype(np.float32),
            "dft_c": (np.stack([np.cos(b), np.sin(b)]) / np.sqrt(P)).astype(np.float32)}


def kernel(**inputs):
    import numpy as np
    import concourse.bacc as bacc
    from concourse.bass_utils import run_bass_kernel_spmd

    nc = bacc.Bacc("TRN2", target_bir_lowering=False, num_devices=1)
    arrays = {name: np.ascontiguousarray(a) for name, a in inputs.items()}
    arrays.update(constants())
    A = {name: nc.dram_tensor("in_" + name, a.shape, mybir.dt.from_np(a.dtype), kind="ExternalInput").ap()
         for name, a in arrays.items()}
    A["skew"] = nc.dram_tensor("skew", (8, P, 512), F32, kind="Internal").ap()
    out = nc.dram_tensor("out_h", SHAPES_OUT, F32, kind="ExternalOutput").ap()
    program(nc, A, out)
    r = run_bass_kernel_spmd(nc, [{"in_" + name: a for name, a in arrays.items()}], core_ids=[0])
    return r.results[0]["out_h"]
```
